# Optimizing a Trainium2 kernel written in Bass

```python
import math
import jax, jax.numpy as jnp
from jax import lax
import numpy as np

D_MODEL = 1024
BATCH = 1
SEQ = 256
DEPTH = 2

MIX_WIDTH = D_MODEL
HALF_W = MIX_WIDTH // 2
HEAD_DIM = 64
A_HEADS = HALF_W // (2 * HEAD_DIM)
A_QK_W = A_HEADS * 2 * HEAD_DIM
A_V_W = A_HEADS * 2 * HEAD_DIM
B_HEADS = HALF_W // HEAD_DIM
B_W = B_HEADS * HEAD_DIM
IDX_HEADS = 8
IDX_DIM = 32
DSA_TOPK = 256
C_HEADS = HALF_W // HEAD_DIM
C_W = C_HEADS * HEAD_DIM
MOBA_BLOCK = 256
MOBA_TOPK = 3
S5_GROUP_CH = 16
S5_GROUPS = HALF_W // S5_GROUP_CH
S5_STATE = 64
S5_W = S5_GROUPS * S5_GROUP_CH
ROPE_THETA = 500000.0
ROT_HEAD = HEAD_DIM // 4
ROT_IDX = IDX_DIM // 4
Q_BLOCK = 128
MOBA_QBLOCK = 64
N_GROUPS = 4
EXPERTS_PER_GROUP = 8
N_EXPERTS = N_GROUPS * EXPERTS_PER_GROUP
TOPK_FINE = 2
EXPERT_FF = 512
MOE_BLOCK = 128
NORM_EPS = 1e-6
N_EVEN = (DEPTH + 1) // 2
N_ODD = DEPTH // 2
EVEN_SPLIT = (A_QK_W, A_QK_W, A_V_W, B_W, B_W, B_W, IDX_HEADS * IDX_DIM, IDX_DIM, IDX_HEADS)
EVEN_IN = sum(EVEN_SPLIT)
ODD_SPLIT = (C_W, C_W, C_W, S5_W)
ODD_IN = sum(ODD_SPLIT)

kernel_name = "hybrid_diff_dsa_moba_s5_hmoe"

F32 = jnp.float32

def rms_norm(x, gain=None):
    xf = x.astype(F32)
    y = xf * lax.rsqrt(jnp.mean(xf * xf, axis=-1, keepdims=True) + NORM_EPS)
    if gain is not None:
        y = y * gain.astype(F32)
    return y.astype(x.dtype)

def rope_tables(n_pos, rot_dim):
    pos = jnp.arange(n_pos, dtype=F32)
    inv = ROPE_THETA ** (-(jnp.arange(0, rot_dim, 2, dtype=F32) / rot_dim))
    ang = pos[:, None] * inv[None, :]
    return jnp.cos(ang), jnp.sin(ang)

def apply_rope(x, cos, sin):
    half = cos.shape[-1]
    bshape = (1, cos.shape[0]) + (1,) * (x.ndim - 3) + (half,)
    cs = cos.reshape(bshape).astype(x.dtype)
    sn = sin.reshape(bshape).astype(x.dtype)
    x1 = x[..., :half]
    x2 = x[..., half:2 * half]
    return jnp.concatenate([x1 * cs - x2 * sn, x2 * cs + x1 * sn, x[..., 2 * half:]], axis=-1)

def _split(z, sizes):
    out, start = [], 0
    for s in sizes:
        out.append(z[..., start:start + s])
        start += s
    return out

def diff_attention(q, k, v, lam, lam_init, subln_g):
    bsz, seq, n_h, _, d = q.shape
    nqb = seq // Q_BLOCK
    scale = d ** -0.5
    q_blocks = q.reshape(bsz, nqb, Q_BLOCK, n_h, 2, d).swapaxes(0, 1)
    k_pos = jnp.arange(seq)

    def one_block(args):
        q_blk, blk = args
        q_pos = blk * Q_BLOCK + jnp.arange(Q_BLOCK)
        s = jnp.einsum('bqhcd,bkhcd->bhcqk', q_blk, k, preferred_element_type=F32) * scale
        s = jnp.where(k_pos[None, :] <= q_pos[:, None], s, -jnp.inf)
        p = jax.nn.softmax(s, axis=-1)
        attn = p[:, :, 0] - lam * p[:, :, 1]
        return jnp.einsum('bhqk,bkhe->bqhe', attn.astype(v.dtype), v)

    o = lax.map(one_block, (q_blocks, jnp.arange(nqb)))
    o = o.swapaxes(0, 1).reshape(bsz, seq, n_h, v.shape[-1])
    o = rms_norm(o, subln_g) * (1.0 - lam_init)
    return o.reshape(bsz, seq, n_h * v.shape[-1])

def dsa_attention(q, k, v, q_idx, k_idx, w_idx):
    bsz, seq, n_h, d = q.shape
    n_sel = min(DSA_TOPK, seq // 4)
    nqb = seq // Q_BLOCK
    scale = d ** -0.5
    k_pos = jnp.arange(seq)
    b_idx = jnp.arange(bsz)[:, None, None]

    def to_blocks(t):
        return t.reshape((bsz, nqb, Q_BLOCK) + t.shape[2:]).swapaxes(0, 1)

    def one_block(args):
        q_blk, qi_blk, wi_blk, blk = args
        q_pos = blk * Q_BLOCK + jnp.arange(Q_BLOCK)
        logits = jnp.einsum('bqhd,bsd->bqhs', qi_blk, k_idx, preferred_element_type=F32)
        score = jnp.einsum('bqh,bqhs->bqs', wi_blk.astype(F32), jax.nn.relu(logits))
        score = jnp.where((k_pos[None, :] <= q_pos[:, None])[None], score, -jnp.inf)
        _, sel = lax.top_k(score, n_sel)
        valid = sel <= q_pos[None, :, None]
        k_sel = k[b_idx, sel]
        v_sel = v[b_idx, sel]
        s = jnp.einsum('bqhd,bqnhd->bqhn', q_blk, k_sel, preferred_element_type=F32) * scale
        s = jnp.where(valid[:, :, None, :], s, -jnp.inf)
        p = jax.nn.softmax(s, axis=-1)
        return jnp.einsum('bqhn,bqnhd->bqhd', p.astype(v.dtype), v_sel)

    o = lax.map(one_block, (to_blocks(q), to_blocks(q_idx), to_blocks(w_idx), jnp.arange(nqb)))
    return o.swapaxes(0, 1).reshape(bsz, seq, n_h * d)

def moba_attention(q, k, v):
    bsz, seq, n_h, d = q.shape
    n_blk = -(-seq // MOBA_BLOCK)
    n_sel = max(1, min(MOBA_TOPK, n_blk - 1))
    pad = n_blk * MOBA_BLOCK - seq
    scale = d ** -0.5
    k_pad = jnp.pad(k, ((0, 0), (0, pad), (0, 0), (0, 0)))
    v_pad = jnp.pad(v, ((0, 0), (0, pad), (0, 0), (0, 0)))
    k_blocks = k_pad.reshape(bsz, n_blk, MOBA_BLOCK, n_h, d)
    k_mean = jnp.mean(k_blocks.astype(F32), axis=2)
    k_bt = k_blocks.transpose(0, 1, 3, 2, 4)
    v_bt = v_pad.reshape(bsz, n_blk, MOBA_BLOCK, n_h, d).transpose(0, 1, 3, 2, 4)
    nqb = seq // MOBA_QBLOCK
    q_blocks = q.reshape(bsz, nqb, MOBA_QBLOCK, n_h, d).swapaxes(0, 1)
    b_idx = jnp.arange(bsz)[:, None, None, None]
    h_idx = jnp.arange(n_h)[None, None, :, None]

    def one_block(args):
        q_blk, blk = args
        q_start = blk * MOBA_QBLOCK
        q_pos = q_start + jnp.arange(MOBA_QBLOCK)
        own = q_start // MOBA_BLOCK
        gate = jnp.einsum('bqhd,bnhd->bqhn', q_blk.astype(F32), k_mean)
        gate = jnp.where(jnp.arange(n_blk) < own, gate, -jnp.inf)
        _, sel = lax.top_k(gate, n_sel)
        valid = sel < own
        k_sel = k_bt[b_idx, sel, h_idx]
        v_sel = v_bt[b_idx, sel, h_idx]
        s_sel = jnp.einsum('bqhd,bqhnpd->bqhnp', q_blk, k_sel, preferred_element_type=F32) * scale
        s_sel = jnp.where(valid[..., None], s_sel, -jnp.inf)
        s_sel = s_sel.reshape(bsz, MOBA_QBLOCK, n_h, n_sel * MOBA_BLOCK)
        k_own = lax.dynamic_slice_in_dim(k_pad, own * MOBA_BLOCK, MOBA_BLOCK, axis=1)
        v_own = lax.dynamic_slice_in_dim(v_pad, own * MOBA_BLOCK, MOBA_BLOCK, axis=1)
        own_pos = own * MOBA_BLOCK + jnp.arange(MOBA_BLOCK)
        s_own = jnp.einsum('bqhd,bphd->bqhp', q_blk, k_own, preferred_element_type=F32) * scale
        s_own = jnp.where((own_pos[None, :] <= q_pos[:, None])[None, :, None, :], s_own, -jnp.inf)
        p = jax.nn.softmax(jnp.concatenate([s_sel, s_own], axis=-1), axis=-1).astype(v.dtype)
        p_sel = p[..., :n_sel * MOBA_BLOCK].reshape(bsz, MOBA_QBLOCK, n_h, n_sel, MOBA_BLOCK)
        p_own = p[..., n_sel * MOBA_BLOCK:]
        return (jnp.einsum('bqhnp,bqhnpd->bqhd', p_sel, v_sel)
                + jnp.einsum('bqhp,bphd->bqhd', p_own, v_own))

    o = lax.map(one_block, (q_blocks, jnp.arange(nqb)))
    return o.swapaxes(0, 1).reshape(bsz, seq, n_h * d)

def _ssm_combine(left, right):
    a1r, a1i, b1r, b1i = left
    a2r, a2i, b2r, b2i = right
    return (a1r * a2r - a1i * a2i,
            a1r * a2i + a1i * a2r,
            a2r * b1r - a2i * b1i + b2r,
            a2r * b1i + a2i * b1r + b2i)

def s5_scan(u, lam_re, lam_im, b_re, b_im, c_re, c_im, d_skip, log_dt):
    lam_re, lam_im = lam_re.astype(F32), lam_im.astype(F32)
    dt = jnp.exp(log_dt.astype(F32))[:, None]
    mag = jnp.exp(lam_re * dt)
    abar_re = mag * jnp.cos(lam_im * dt)
    abar_im = mag * jnp.sin(lam_im * dt)
    den = lam_re * lam_re + lam_im * lam_im
    coef_re = ((abar_re - 1.0) * lam_re + abar_im * lam_im) / den
    coef_im = (abar_im * lam_re - (abar_re - 1.0) * lam_im) / den
    b_re, b_im = b_re.astype(F32), b_im.astype(F32)
    bbar_re = coef_re[..., None] * b_re - coef_im[..., None] * b_im
    bbar_im = coef_re[..., None] * b_im + coef_im[..., None] * b_re
    uf = u.astype(F32)
    bu_re = jnp.einsum('gpc,bsgc->sbgp', bbar_re, uf)
    bu_im = jnp.einsum('gpc,bsgc->sbgp', bbar_im, uf)
    seq = u.shape[1]
    a_re = jnp.broadcast_to(abar_re[None, None], (seq, 1) + abar_re.shape)
    a_im = jnp.broadcast_to(abar_im[None, None], (seq, 1) + abar_im.shape)
    _, _, h_re, h_im = lax.associative_scan(_ssm_combine, (a_re, a_im, bu_re, bu_im), axis=0)
    y = (jnp.einsum('gcp,sbgp->bsgc', c_re.astype(F32), h_re)
         - jnp.einsum('gcp,sbgp->bsgc', c_im.astype(F32), h_im)
         + d_skip.astype(F32) * uf)
    return y.astype(u.dtype)

def even_mixer(h, w_in, w_out, a_qn, a_kn, a_lq1, a_lk1, a_lq2, a_lk2, a_subln,
               b_qn, b_kn, idx_kn, lam_init, rope_head, rope_idx):
    bsz, seq, _ = h.shape
    cos_h, sin_h = rope_head
    cos_i, sin_i = rope_idx
    z = h @ w_in
    aq, ak, av, bq, bk, bv, iq, ik, iw = _split(z, EVEN_SPLIT)
    aq = apply_rope(rms_norm(aq.reshape(bsz, seq, A_HEADS, 2, HEAD_DIM), a_qn), cos_h, sin_h)
    ak = apply_rope(rms_norm(ak.reshape(bsz, seq, A_HEADS, 2, HEAD_DIM), a_kn), cos_h, sin_h)
    av = av.reshape(bsz, seq, A_HEADS, 2 * HEAD_DIM)
    lam = (jnp.exp(jnp.sum(a_lq1.astype(F32) * a_lk1.astype(F32)))
           - jnp.exp(jnp.sum(a_lq2.astype(F32) * a_lk2.astype(F32))) + lam_init)
    o_a = diff_attention(aq, ak, av, lam, lam_init, a_subln)
    bq = apply_rope(rms_norm(bq.reshape(bsz, seq, B_HEADS, HEAD_DIM), b_qn), cos_h, sin_h)
    bk = apply_rope(rms_norm(bk.reshape(bsz, seq, B_HEADS, HEAD_DIM), b_kn), cos_h, sin_h)
    bv = bv.reshape(bsz, seq, B_HEADS, HEAD_DIM)
    iq = apply_rope(iq.reshape(bsz, seq, IDX_HEADS, IDX_DIM), cos_i, sin_i)
    ik = apply_rope(rms_norm(ik, idx_kn), cos_i, sin_i)
    o_b = dsa_attention(bq, bk, bv, iq, ik, iw)
    return jnp.concatenate([o_a, o_b], axis=-1) @ w_out

def odd_mixer(h, w_in, w_out, c_qn, c_kn, lam_re, lam_im, b_re, b_im, c_re, c_im,
              d_skip, log_dt, glu_w, glu_b, rope_head):
    bsz, seq, _ = h.shape
    cos_h, sin_h = rope_head
    z = h @ w_in
    cq, ck, cv, u = _split(z, ODD_SPLIT)
    cq = apply_rope(rms_norm(cq.reshape(bsz, seq, C_HEADS, HEAD_DIM), c_qn), cos_h, sin_h)
    ck = apply_rope(rms_norm(ck.reshape(bsz, seq, C_HEADS, HEAD_DIM), c_kn), cos_h, sin_h)
    cv = cv.reshape(bsz, seq, C_HEADS, HEAD_DIM)
    o_c = moba_attention(cq, ck, cv)
    y = s5_scan(u.reshape(bsz, seq, S5_GROUPS, S5_GROUP_CH), lam_re, lam_im, b_re, b_im,
                c_re, c_im, d_skip, log_dt).reshape(bsz, seq, S5_W)
    y = jax.nn.gelu(y)
    y = y * jax.nn.sigmoid(y @ glu_w + glu_b)
    return jnp.concatenate([o_c, y], axis=-1) @ w_out

def hier_moe(h, wg, bg, we, be, w1, w3, w2):
    bsz, seq, dm = h.shape
    n_tok = bsz * seq
    xf = h.reshape(n_tok, dm)
    coarse = (xf @ wg).astype(F32) + bg.astype(F32)
    grp = jnp.argmax(coarse, axis=-1)
    tok = jnp.arange(n_tok)
    p_grp = jax.nn.softmax(coarse, axis=-1)[tok, grp][:, None]
    fine = ((xf @ we).astype(F32) + be.astype(F32)).reshape(n_tok, N_GROUPS, EXPERTS_PER_GROUP)
    fine_g = fine[tok, grp]
    top_v, top_i = lax.top_k(fine_g, TOPK_FINE)
    weight = p_grp * jax.nn.softmax(top_v, axis=-1)
    expert = grp[:, None] * EXPERTS_PER_GROUP + top_i
    n_asg = n_tok * TOPK_FINE
    flat_e = expert.reshape(n_asg)
    flat_t = jnp.arange(n_asg) // TOPK_FINE
    flat_w = weight.reshape(n_asg)
    order = jnp.argsort(flat_e, stable=True)
    se = flat_e[order]
    counts = jnp.bincount(flat_e, length=N_EXPERTS)
    padded = ((counts + MOE_BLOCK - 1) // MOE_BLOCK) * MOE_BLOCK
    start = jnp.cumsum(counts) - counts
    pend = jnp.cumsum(padded)
    pstart = pend - padded
    dest = pstart[se] + (jnp.arange(n_asg) - start[se])
    n_pad = n_asg + N_EXPERTS * MOE_BLOCK
    n_blk = n_pad // MOE_BLOCK
    buf_tok = jnp.full((n_pad,), n_tok, dtype=jnp.int32).at[dest].set(flat_t[order].astype(jnp.int32))
    buf_w = jnp.zeros((n_pad,), F32).at[dest].set(flat_w[order])
    blk_e = jnp.clip(jnp.searchsorted(pend, jnp.arange(n_blk) * MOE_BLOCK, side='right'), 0, N_EXPERTS - 1)
    x_pad = jnp.concatenate([xf, jnp.zeros((1, dm), xf.dtype)], axis=0)
    xb = x_pad[buf_tok].reshape(n_blk, MOE_BLOCK, dm)

    def expert_block(args):
        xi, e = args
        hid = jax.nn.silu(xi @ w1[e]) * (xi @ w3[e])
        return hid @ w2[e]

    yb = lax.map(expert_block, (xb, blk_e)).reshape(n_pad, dm)
    yb = yb * buf_w[:, None].astype(yb.dtype)
    out = jnp.zeros((n_tok + 1, dm), yb.dtype).at[buf_tok].add(yb)[:n_tok]
    return out.reshape(bsz, seq, dm)

def setup_inputs(seed: int = 0) -> dict:
    key = jax.random.key(seed)
    ks = iter(jax.random.split(key, 64))

    def nrm(shape, scale):
        return jax.random.normal(next(ks), shape, F32) * scale

    def gain(shape):
        return 1.0 + nrm(shape, 0.1)

    d = D_MODEL
    inputs = {
        "x": nrm((BATCH, SEQ, d), 1.0),
        "c": nrm((BATCH, d), 1.0),
        "ada_w": nrm((DEPTH, d, 6 * d), 0.5 * d ** -0.5),
        "ada_b": nrm((DEPTH, 6 * d), 0.02),
        "moe_wg": nrm((DEPTH, d, N_GROUPS), d ** -0.5),
        "moe_bg": nrm((DEPTH, N_GROUPS), 0.01),
        "moe_we": nrm((DEPTH, d, N_EXPERTS), d ** -0.5),
        "moe_be": nrm((DEPTH, N_EXPERTS), 0.01),
        "moe_w1": nrm((DEPTH, N_EXPERTS, d, EXPERT_FF), d ** -0.5),
        "moe_w3": nrm((DEPTH, N_EXPERTS, d, EXPERT_FF), d ** -0.5),
        "moe_w2": nrm((DEPTH, N_EXPERTS, EXPERT_FF, d), EXPERT_FF ** -0.5),
        "ev_w_in": nrm((N_EVEN, d, EVEN_IN), d ** -0.5),
        "ev_w_out": nrm((N_EVEN, MIX_WIDTH, d), MIX_WIDTH ** -0.5),
        "a_qn": gain((N_EVEN, HEAD_DIM)),
        "a_kn": gain((N_EVEN, HEAD_DIM)),
        "a_lq1": nrm((N_EVEN, HEAD_DIM), 0.1),
        "a_lk1": nrm((N_EVEN, HEAD_DIM), 0.1),
        "a_lq2": nrm((N_EVEN, HEAD_DIM), 0.1),
        "a_lk2": nrm((N_EVEN, HEAD_DIM), 0.1),
        "a_subln": gain((N_EVEN, 2 * HEAD_DIM)),
        "b_qn": gain((N_EVEN, HEAD_DIM)),
        "b_kn": gain((N_EVEN, HEAD_DIM)),
        "b_idx_kn": gain((N_EVEN, IDX_DIM)),
        "od_w_in": nrm((N_ODD, d, ODD_IN), d ** -0.5),
        "od_w_out": nrm((N_ODD, MIX_WIDTH, d), MIX_WIDTH ** -0.5),
        "c_qn": gain((N_ODD, HEAD_DIM)),
        "c_kn": gain((N_ODD, HEAD_DIM)),
        "s5_lam_re": -0.5 + nrm((N_ODD, S5_GROUPS, S5_STATE), 0.01),
        "s5_lam_im": jnp.pi * jnp.arange(S5_STATE, dtype=F32) + nrm((N_ODD, S5_GROUPS, S5_STATE), 0.01),
        "s5_b_re": nrm((N_ODD, S5_GROUPS, S5_STATE, S5_GROUP_CH), (2 * S5_GROUP_CH) ** -0.5),
        "s5_b_im": nrm((N_ODD, S5_GROUPS, S5_STATE, S5_GROUP_CH), (2 * S5_GROUP_CH) ** -0.5),
        "s5_c_re": nrm((N_ODD, S5_GROUPS, S5_GROUP_CH, S5_STATE), 0.5),
        "s5_c_im": nrm((N_ODD, S5_GROUPS, S5_GROUP_CH, S5_STATE), 0.5),
        "s5_d": nrm((N_ODD, S5_GROUPS, S5_GROUP_CH), 0.5),
        "s5_log_dt": jax.random.uniform(next(ks), (N_ODD, S5_GROUPS), F32,
                                        minval=math.log(1e-3), maxval=math.log(1e-1)),
        "s5_glu_w": nrm((N_ODD, S5_W, S5_W), S5_W ** -0.5),
        "s5_glu_b": nrm((N_ODD, S5_W), 0.02),
    }
    return inputs

def reference(x, c, ada_w, ada_b, moe_wg, moe_bg, moe_we, moe_be, moe_w1, moe_w3, moe_w2,
              ev_w_in, ev_w_out, a_qn, a_kn, a_lq1, a_lk1, a_lq2, a_lk2, a_subln,
              b_qn, b_kn, b_idx_kn, od_w_in, od_w_out, c_qn, c_kn,
              s5_lam_re, s5_lam_im, s5_b_re, s5_b_im, s5_c_re, s5_c_im, s5_d, s5_log_dt,
              s5_glu_w, s5_glu_b):
    seq = x.shape[1]
    rope_head = rope_tables(seq, ROT_HEAD)
    rope_idx = rope_tables(seq, ROT_IDX)
    c_act = jax.nn.silu(c)
    for l in range(DEPTH):
        mod = c_act @ ada_w[l] + ada_b[l]
        sh1, sc1, g1, sh2, sc2, g2 = jnp.split(mod, 6, axis=-1)
        h = rms_norm(x) * (1.0 + sc1[:, None, :]) + sh1[:, None, :]
        i = l // 2
        if l % 2 == 0:
            lam_init = 0.8 - 0.6 * math.exp(-0.3 * l)
            y = even_mixer(h, ev_w_in[i], ev_w_out[i], a_qn[i], a_kn[i], a_lq1[i], a_lk1[i],
                           a_lq2[i], a_lk2[i], a_subln[i], b_qn[i], b_kn[i], b_idx_kn[i],
                           lam_init, rope_head, rope_idx)
        else:
            y = odd_mixer(h, od_w_in[i], od_w_out[i], c_qn[i], c_kn[i], s5_lam_re[i], s5_lam_im[i],
                          s5_b_re[i], s5_b_im[i], s5_c_re[i], s5_c_im[i], s5_d[i], s5_log_dt[i],
                          s5_glu_w[i], s5_glu_b[i], rope_head)
        x = x + g1[:, None, :] * y
        h = rms_norm(x) * (1.0 + sc2[:, None, :]) + sh2[:, None, :]
        x = x + g2[:, None, :] * hier_moe(h, moe_wg[l], moe_bg[l], moe_we[l], moe_be[l],
                                          moe_w1[l], moe_w3[l], moe_w2[l])
    return x


_drawn_inputs = setup_inputs


def setup_inputs(seed=0):
    import zlib

    import numpy as np

    out = dict(_drawn_inputs(seed))
    spreads = {}
    factors = {'moe_bg': 6.162,
     'moe_be': 6.868,
     'a_qn': 3.737,
     'a_kn': 4.42,
     'a_lq1': 5.565,
     'a_lk1': 6.245,
     'a_lq2': 5.719,
     'a_lk2': 8.0,
     'a_subln': 2.833,
     'b_qn': 8.0,
     'b_kn': 8.0,
     'b_idx_kn': 4.736,
     'c_qn': 8.0,
     'c_kn': 8.0,
     's5_lam_re': 8.0,
     's5_b_re': 3.101,
     's5_b_im': 2.923,
     's5_c_im': 2.917,
     's5_glu_w': 4.624,
     's5_glu_b': 8.0}
    for name, (base, spread) in spreads.items():
        noise = np.random.default_rng([zlib.crc32(name.encode()), seed]).standard_normal(out[name].shape)
        drawn = base * np.exp(spread * noise) if base else spread * noise
        out[name] = __import__('jax').numpy.asarray(drawn.astype(out[name].dtype))
    for name, factor in factors.items():
        out[name] = (out[name] * factor).astype(out[name].dtype)
    return out
```

```python
from contextlib import ExitStack

import concourse.bass as bass
from concourse import mybir

F32 = mybir.dt.float32
I32 = mybir.dt.int32
ALU = mybir.AluOpType
ACT = mybir.ActivationFunctionType
AX = mybir.AxisListType.X

P = 128
D = 1024
KD = D // P
TOK = 256
TT = TOK // P
LAYERS = 2
NE, NG, EPG = 32, 4, 8
FF = 512
KF = FF // P
EPS = 1e-6
BIG = 1.0e30
SENT = -3.0e38
HD = 64
TOPK = TOK // 4
SETW = 1024
EV_IN = 3368
OD_QKV = 1536
MAGIC = 12582912.0
TWO_PI = 6.283185307179586
SIN_SCALE = 6.2831845
C1 = 6.28125
C2 = 0.0019353071795864769
GELU_C = 0.7978845608028654

RING = 6
SLOT = 4096
IN0_ORDER = [6, 3, 4, 0, 1, 5, 2]
ADA1_AFTER = [1, 4, 5]
IN1_ORDER = [0, 1, 3, 2]
N_ADA0 = 0
N_IN0 = N_ADA0 + 12
N_OUT0 = N_IN0 + 7 + 12


def n_in0(q):
    return N_IN0 + q + 4 * sum(q > x for x in ADA1_AFTER)


def n_ada(l, r):
    return N_ADA0 + 4 * r if l == 0 else n_in0(ADA1_AFTER[r]) + 1


N_MOE0 = N_OUT0 + 2
N_IN1 = N_MOE0 + 3 * NE
N_GLU = N_IN1 + 4
N_OUT1 = N_GLU + 1
N_MOE1 = N_OUT1 + 2
N_MOE = [N_MOE0, N_MOE1]
N_OUT = [N_OUT0, N_OUT1]

CH = 64
GE = 4
TURNS = NE // (2 * GE)
NP5 = 5
PADE = NE + 2 * GE


def const_layout():
    at, n = {}, 0
    for name, w in (("ident", P), ("ones", P), ("tri", P), ("cb2", 2 * P), ("iota", CH), ("rc", 2 * 16),
                    ("rs", 2 * 16), ("ic", 2 * 8), ("is", 2 * 8), ("time", TOK), ("desc4", NG),
                    ("desc32", NE), ("par", 2)):
        at[name] = (n, n + w)
        n += w
    return at, n


CONST_AT, CONST_W = const_layout()


def build(nc, a, cst_d, out_d):
    ctx = ExitStack()
    with ctx:
        def sb(name, shape, dt=F32):
            return ctx.enter_context(nc.sbuf_tensor(name, shape, dt))

        def sem(name):
            return ctx.enter_context(nc.semaphore(name))

        ring = sb("ring", [P, RING, SLOT])
        cst = sb("cst", [P, CONST_W])
        xT = sb("xT", [P, KD, TOK])
        hT = sb("hT", [P, KD, TOK])
        htok = sb("htok", [P, TT, D])
        modrow = sb("modrow", [P, 512])
        brow = sb("brow", [P, 3, 512])
        modc = sb("modc", [P, LAYERS, 48])
        crep = sb("crep", [P, KD, 32])
        ccol = sb("ccol", [P, KD])
        ctmp = sb("ctmp", [P, 2, KD])
        gqk = sb("gqk", [P, 3, 2, HD])
        gidx = sb("gidx", [P, 32])
        subln = sb("subln", [P, 2 * HD])
        lrow = sb("lrow", [P, 4, HD])
        lamt = sb("lamt", [P, 8])
        wge = sb("wge", [P, LAYERS, KD, NG + NE])
        bge = sb("bge", [P, LAYERS, NG + NE])
        s5row = sb("s5row", [32, P])
        logdt = sb("logdt", [P, 16])
        s5b = sb("s5b", [P, 2, 16, 16])
        s5c = sb("s5c", [P, 2, 4, HD])
        s5d = sb("s5d", [P, 4])
        glub = sb("glub", [P, 4])
        s5p = sb("s5p", [P, 24, 16])
        rstd = sb("rstd", [P, TOK])
        small = sb("small", [P, 256])
        rankm = sb("rankm", [P, TT, PADE])
        wt = sb("wt", [P, TT, PADE])
        cnti = sb("cnti", [P, LAYERS], I32)
        WORK = 14336
        work = sb("work", [P, WORK])

        def C(name):
            lo, hi = CONST_AT[name]
            return cst[:, lo:hi]

        ident, ones, tri = C("ident"), C("ones"), C("tri")

        class Carve:

            def __init__(self, at=0):
                self.at = at

            def __call__(self, *dims):
                n = 1
                for d in dims:
                    n *= d
                ap = work[:, self.at:self.at + n]
                self.at += n
                assert self.at <= WORK, self.at
                if len(dims) == 2:
                    ap = ap.rearrange("p (a b) -> p a b", a=dims[0])
                elif len(dims) == 3:
                    ap = ap.rearrange("p (a b c) -> p a b c", a=dims[0], b=dims[1])
                return ap

        c = Carve()
        z0 = c(TT, EV_IN)
        qkT0 = c(16, TOK)
        idxT = c(3, TOK)
        selb = c(TT, TOK)
        at0 = c.at
        sqs = c(16, HD)
        c.at = at0
        sc_sb = c(2, 2, TOK)
        prob = hT[:, 0:4, :].rearrange("p (a b) c -> p a b c", a=2)
        PT = hT[:, 4:8, :].rearrange("p (a b) c -> p a (b c)", a=2).rearrange("p a (b c) -> p a b c", b=4)
        ikrep = c(TT, P)
        relu_sb = [sc_sb.rearrange("p a b c -> p (a b) c"), hT[:, 4:8, :]]
        idx_acc = prob[:, 0, 0, :]
        tmp16 = c(2, 16, 16)
        c = Carve()
        z1 = c(TT, OD_QKV)
        uT = c(4, TOK)
        BT = c(2, 4, P)
        CT = c(3, 4, P)
        tmp16_1 = c(2, 16, 16)
        at1 = c.at
        tab5 = c(2, 4, TOK)
        ph = c(2, 4, TOK)
        phr = c(4, TOK)
        vv = c(2, 4, TOK)
        mm = htok[:, :, :].rearrange("p t (a b) -> p t a b", b=TOK)
        y5 = hT[:, 0:4, :]
        gy = tab5[:, 0]
        sqs1 = vv[:, 0].rearrange("p a b -> p (a b)").rearrange("p (a b) -> p a b", a=16)
        c.at = at1
        Bbar = c(2, 16, 16)
        Bd = c(2, 16, 32)
        Cd = c(2, 4, P)
        Btmp = c(16, 16)
        c.at = at1
        qkT1 = c(8, TOK)
        sc_sb1 = c(2, 2, TOK)
        prob1 = c(2, 2, TOK)
        PT1 = c(2, 4, P)
        c = Carve()
        xgT = c(2, KD, GE * CH)
        Sd = c(4, GE * CH)
        Sw = c(4, GE * CH)
        SwT = c(2, 2, TOK)
        silu_a = c(2, FF)
        hid = c(2, FF)
        hidTb = c(2, KF, CH)
        y2 = c(2, D)
        rt = c(16, TT, NE)
        Sd = Sd.rearrange("p (g t) s -> p g t s", g=2)
        Sw = Sw.rearrange("p (g t) s -> p g t s", g=2)

        PARAMS = []
        for s_, (qn, kn) in enumerate((("a_qn", "a_kn"), ("b_qn", "b_kn"), ("c_qn", "c_kn"))):
            PARAMS += [(gqk[:, s_, 0, :], a[qn][0].partition_broadcast(P), False),
                       (gqk[:, s_, 1, :], a[kn][0].partition_broadcast(P), False)]
        PARAMS += [(lrow[:, m, :], a[nm][0].partition_broadcast(P), False)
                   for m, nm in enumerate(("a_lq1", "a_lk1", "a_lq2", "a_lk2"))]
        PARAMS += [(gidx[:, :], a["b_idx_kn"][0].partition_broadcast(P), False),
                   (subln[:, :], a["a_subln"][0].partition_broadcast(P), False)]
        for l_ in range(LAYERS):
            PARAMS += [(wge[:, l_, :, 0:NG], a["moe_wg"][l_].rearrange("(k p) n -> p k n", p=P), False),
                       (wge[:, l_, :, NG:], a["moe_we"][l_].rearrange("(k p) n -> p k n", p=P), False),
                       (bge[:, l_, 0:NG], a["moe_bg"][l_].partition_broadcast(P), False),
                       (bge[:, l_, NG:], a["moe_be"][l_].partition_broadcast(P), False)]
        PARAMS += [(s5row[0:16, :], a["s5_lam_re"][0].rearrange("(j g) p -> j (g p)", g=2), False),
                   (s5row[16:32, :], a["s5_lam_im"][0].rearrange("(j g) p -> j (g p)", g=2), False)]
        for g_ in range(2):
            PARAMS.append((logdt[64 * g_:64 * g_ + 64, :],
                           a["s5_log_dt"][0].rearrange("(j g) -> g j", g=2)[g_].partition_broadcast(64), True))
        for v_, (bn, cn) in enumerate((("s5_b_re", "s5_c_re"), ("s5_b_im", "s5_c_im"))):
            PARAMS += [(s5b[:, v_], a[bn][0].rearrange("(j g) p c -> (g p) j c", g=2), False),
                       (s5c[:, v_], a[cn][0].rearrange("(q g) c p -> (g c) q p", g=8), False)]
        PARAMS += [(s5d[:, :], a["s5_d"][0].rearrange("(q g) c -> (g c) q", g=8), True),
                   (glub[:, :], a["s5_glu_b"][0].rearrange("(q p) -> p q", p=P), True)]
        N_PAR = len(PARAMS)

        A4 = ctx.enter_context(nc.psum_tensor("A4", [P, 4, 512], F32))
        B4, B5, B6, B7 = (ctx.enter_context(nc.psum_tensor(f"B{i}", [P, 512], F32)) for i in (4, 5, 6, 7))
        TRB = [B6, B7]
        OB = [B4, B5]

        slot_full = [sem(f"slot_full{i}") for i in range(RING)]
        slot_used = sem("slot_used")
        in_cst, in_x, in_c, in_par = sem("in_cst"), sem("in_x"), sem("in_c"), sem("in_par")
        in_brow = sem("in_brow")
        s_dve, s_act, s_pool = sem("dve_chain"), sem("act_chain"), sem("pool_chain")
        x_tr = sem("x_transposed")
        x_ev = sem("xT_written")
        c_exp, c_ready = sem("c_exp"), sem("c_ready")
        ada_done, row_ready, modT_done, mod_ready = sem("ada_done"), sem("row_ready"), sem("modT_done"), sem("mod_ready")
        sq_ready, ssq_done, var_ready, sd_ready, h_ready = (sem(n) for n in ("sq_ready", "ssq_done", "var_ready", "sd_ready", "h_ready"))
        proj_done, z_ready = sem("proj_done"), sem("z_ready")
        ms_ready, sq_root = sem("ms_ready"), sem("sq_root")
        tr_done, tr_ev = sem("tr_done"), sem("tr_evacuated")
        qk_ready = sem("qk_ready")
        idx_s, idx_relu, idx_acc_s = sem("idx_logits"), sem("idx_relu"), sem("idx_accumulated")
        score, score_read, negmax, expd, attn_ready = (sem(n) for n in ("score", "score_read", "negmax", "exp_done", "attn_ready"))
        pv_done, o_ready = sem("pv_done"), sem("o_ready")
        wout_done, x_upd = sem("wout_done"), sem("x_updated")
        lam_s, lam_e = sem("lam_sums"), sem("lam_exps")
        logit_done, route_d, route_e, mask_ready, rank_done = (sem(n) for n in (
            "logit_done", "route_diff", "route_exp", "mask_ready", "rank_done"))

        class MoeSems:

            def __init__(self, tag):
                def own(name):
                    return sem(name + tag)

                self.mat = own("slot_matrix")
                self.ready = own("matrices_ready")
                self.disp = own("dispatched")
                self.disp_ev = own("dispatch_copied")
                self.ab = own("ab_done")
                self.silu = own("silu_done")
                self.hid = own("hid_ready")
                self.hidT_ps = own("hid_transposed")
                self.hidT = own("hidT_ready")
                self.y = own("y_done")
                self.y_lo = own("y_copied_lo")
                self.y_hi = own("y_copied_hi")
                self.comb = own("combined")

        main = MoeSems("")
        more = [MoeSems(f"_more{l}") for l in range(LAYERS)]
        more_full = [[sem(f"more_full{l}_{m}") for m in range(3)] for l in range(LAYERS)]
        ranks_down = [sem(f"ranks_lowered{l}") for l in range(LAYERS)]
        cnt_ready = sem("chunks_counted")
        more_over = sem("more_steps_over")
        out_s = sem("out_written")
        p5_tr, p5_dt, p5_arg, p5_sc, p5_bt, p5_lam = (sem(n) for n in ("s5_lam_T", "s5_dt", "s5_arg", "s5_sincos", "s5_bt_in", "s5_turns"))
        ph_ready, tab_ready, bu_done, bu_read, prod_ready, y5_done, tab_used = (sem(n) for n in (
            "phase_ready", "tab_ready", "bu_done", "bu_read", "prod_ready", "y5_done", "tab_used"))
        u_ready = sem("u_ready")
        tanh_in, tanh_out, gy_ready, glu_done, sig_ready, yo_ready = (sem(n) for n in (
            "tanh_in", "tanh_out", "gy_ready", "glu_done", "sig_ready", "yo_ready"))

        def slot(n):
            return n % RING

        def fills(n):
            return 16 * (n // RING + 1)

        def used_after(n):
            return n + 1 - (3 * NE if n >= N_IN1 else 0)

        def slot8(n):
            return ring[:, slot(n), :].rearrange("p (k n) -> p k n", k=KD)

        def slot4(n):
            return ring[:, slot(n), :].rearrange("p (k n) -> p k n", k=4)

        L0_UNITS = [(1, b, t) for t in range(TT) for b in range(4)] + [(0, b, t) for t in range(TT) for b in range(4)]
        L1_UNITS = [(2, b, t) for t in range(TT) for b in range(4)]
        U_IDX, U_B, U_A = 0, 2, 6
        U_ATT0 = 10
        U_OT0 = U_ATT0 + len(L0_UNITS)
        U_HT0 = U_OT0 + 4
        U_S5 = U_HT0 + 4
        U_C = U_S5 + 5
        U_ATT1 = U_C + 4
        U_OT1 = U_ATT1 + len(L1_UNITS)
        U_HT1 = U_OT1 + 2
        U_END = U_HT1 + 4

        def n_maps(s):
            return 1 if s == 0 else 2

        MORE = TOK // CH - 1

        def more_chunks(eng, l, body, before=None, after=None):
            eng.wait_ge(cnt_ready, l + 1)
            extra = eng.value_load(cnti[0:1, l:l + 1], min_val=0, max_val=MORE)
            with eng.Fori(0, MORE) as c:
                with eng.If(c < extra):
                    if before:
                        before(c)
                    with eng.Fori(0, NE // GE) as i:
                        body(c * (NE // GE) + i, i)
                    if after:
                        after(c)

        block = ctx.enter_context(nc.Block())

        @block.sync
        def _(sp):
            def slot_free(n):
                old = n - RING
                if old < 0:
                    return
                for l in range(LAYERS):
                    e, m = divmod(old - N_MOE[l], 3)
                    if 0 <= e < NE:
                        sp.wait_ge(main.ab if m < 2 else main.y, NE * l + e + 1 + m // 2)
                        return
                sp.wait_ge(slot_used, used_after(old))

            def load(n, dst, src):
                slot_free(n)
                sp.dma_start(dst, src).then_inc(slot_full[slot(n)], 16)

            def load_ada(l, j):
                n = n_ada(l, j // 4) + j % 4
                load(n, slot8(n),
                     a["ada_w"][l, :, 512 * j:512 * j + 512].rearrange("(k p) n -> p k n", p=P))

            def load_out(l, w):
                for cc in range(2):
                    load(N_OUT[l] + cc, slot4(N_OUT[l] + cc),
                         w[0, 512 * cc:512 * cc + 512, :].rearrange("(k p) n -> p k n", p=P))

            def load_moe(l):
                w1 = a["moe_w1"].rearrange("l e (k p) n -> (l e) p k n", p=P)
                w3 = a["moe_w3"].rearrange("l e (k p) n -> (l e) p k n", p=P)
                w2 = a["moe_w2"].rearrange("l e (k p) n -> (l e) p k n", p=P)

                def expert(e):
                    for m, w in enumerate((w1, w3, w2)):
                        n = N_MOE[l] + 3 * e + m
                        load(n, (slot8 if m < 2 else slot4)(n), w[NE * l + e])

                T = 2 * GE
                for e in range(2):
                    expert(e)
                with sp.Fori(0, TURNS - 1) as i:
                    for q in range(T):
                        for m, w in enumerate((w1, w3, w2)):
                            n = N_MOE[l] + 3 * (q + 2) + m
                            sp.wait_ge(main.ab if m < 2 else main.y, i * T + (NE * l + q + 1 + m // 2))
                            src = w[bass.ds(i * T + (NE * l + q + 2), 1)].rearrange("e p k n -> p (e k) n")
                            sp.dma_start((slot8 if m < 2 else slot4)(n), src).then_inc(slot_full[slot(n)], 16)
                for e in range(NE - T + 2, NE):
                    expert(e)

                def more_loads(gb, i):
                    for j in range(GE):
                        for m, w in enumerate((w1, w3, w2)):
                            sp.wait_ge(more[l].y, gb * GE + (j + 1))
                            src = w[bass.ds(i * GE + (NE * l + j), 1)].rearrange("e p k n -> p (e k) n")
                            sp.dma_start((slot8 if m < 2 else slot4)(m), src).then_inc(more_full[l][m], 16)

                def ring_empty(c):
                    sp.wait_ge(main.y, NE * (l + 1) + 1)

                def ring_free(c):
                    sp.wait_ge(more[l].y, c * NE + (NE + 1))
                    sp.sem_inc(more_over, 1)

                more_chunks(sp, l, more_loads, before=ring_empty, after=ring_free)

            for j in range(12):
                load_ada(0, j)
            for q, ch in enumerate(IN0_ORDER):
                w = min(512, EV_IN - 512 * ch)
                load(n_in0(q), slot8(n_in0(q))[:, :, 0:w],
                     a["ev_w_in"][0, :, 512 * ch:512 * ch + w].rearrange("(k p) n -> p k n", p=P))
                if q in ADA1_AFTER:
                    for j in range(4):
                        load_ada(1, 4 * ADA1_AFTER.index(q) + j)
            load_out(0, a["ev_w_out"])
            load_moe(0)
            for q, ch in enumerate(IN1_ORDER):
                load(N_IN1 + q, slot8(N_IN1 + q),
                     a["od_w_in"][0, :, 512 * ch:512 * ch + 512].rearrange("(k p) n -> p k n", p=P))
            load(N_GLU, slot8(N_GLU)[:, 0:4, :], a["s5_glu_w"][0].rearrange("(k p) n -> p k n", p=P))
            load_out(1, a["od_w_out"])
            load_moe(1)

        @block.tensor
        def _(pe):
            def full(n):
                pe.wait_ge(slot_full[slot(n)], fills(n))

            units = [0]

            def tr_unit(u, parts, waits=()):
                assert u == units[0], (u, units[0])
                units[0] += 1
                for s, v in waits:
                    pe.wait_ge(s, v)
                if u >= 2:
                    pe.wait_ge(tr_ev, u - 1)
                for b, src in enumerate(parts):
                    n = src.shape[0]
                    ins = pe.transpose(TRB[u % 2][:, P * b:P * b + n], src, ident[0:n, 0:n])
                ins.then_inc(tr_done, 1)

            def ada_round(l, r):
                n0 = n_ada(l, r)
                for g in range(4):
                    full(n0 + g)
                if l or r:
                    pe.wait_ge(row_ready, 3 * l + r)
                else:
                    pe.wait_ge(c_ready, 1)
                for k in range(KD):
                    for g in range(4):
                        ins = pe.matmul(B4[32 * g:32 * g + 32, :], crep[:, k, :], slot8(n0 + g)[:, k, :],
                                        start=(k == 0), stop=(k == KD - 1))
                        if k == KD - 1:
                            ins.then_inc(slot_used, 1)
                pe.wait_ge(slot_used, used_after(n0 + 3))
                pe.nop().then_inc(ada_done, 1)

            def ada_columns(l, r):
                pe.wait_ge(row_ready, 3 * l + r + 1)
                if l or r:
                    pe.wait_ge(mod_ready, 3 * l + r)
                for b in range(4):
                    ins = pe.transpose(B5[:, P * b:P * b + P], modrow[:, P * b:P * b + P], ident)
                ins.then_inc(modT_done, 1)

            def sum_squares(q):
                pe.wait_ge(sq_ready, q + 1)
                for k in range(KD):
                    ins = pe.matmul(B5[:, 0:TOK], ones, htok[:, :, :].rearrange("p t (a b) -> p (t a) b", b=TOK)[:, k, :],
                                    start=(k == 0), stop=(k == KD - 1))
                ins.then_inc(ssq_done, 1)

            def project(l, q, ch, n, done):
                full(n)
                w = min(512, EV_IN - 512 * ch) if l == 0 else 512
                for t in range(TT):
                    if done + t >= 4:
                        pe.wait_ge(z_ready, done + t - 3)
                    for k in range(KD):
                        ins = pe.matmul(A4[:, (done + t) % 4, 0:w], hT[:, k, P * t:P * t + P], slot8(n)[:, k, 0:w],
                                        start=(k == 0), stop=(k == KD - 1))
                    ins.then_inc(proj_done, 1)
                pe.wait_ge(proj_done, done + TT)
                pe.nop().then_inc(slot_used, 1)

            def att_score(l, base, j, s, b, t):
                blk = (0, 8, 0)[s] + b
                qk = qkT0 if l == 0 else qkT1
                u = base + j
                if u >= 2:
                    pe.wait_ge(score_read, u - 1)
                w = P * (t + 1)
                for m in range(2):
                    ins = pe.matmul(A4[:, 2 * (u % 2) + m, 0:w], qk[64 * m:64 * m + 64, blk, P * t:P * t + P],
                                    qk[64 * m:64 * m + 64, blk + 4, 0:w], start=True, stop=True)
                ins.then_inc(score, 1)

            def att_pt(base, ub, j, s, b, t):
                parts = [prob[:, (base + j) % 2, m, P * kt:P * kt + P] for m in range(n_maps(s)) for kt in range(t + 1)]
                if base:
                    parts = [prob1[:, (base + j) % 2, m, P * kt:P * kt + P] for m in range(n_maps(s)) for kt in range(t + 1)]
                w = [(expd, base + j + 1)]
                if s == 0:
                    w = [(attn_ready, b + 4 * t + 1)]
                tr_unit(ub + j, parts, w)

            def att_pv(base, ub, j, s, b, t):
                pe.wait_ge(tr_ev, ub + j + 1)
                z, vcol = ((z0, 1024), (z0, 2560), (z1, 1024))[s]
                pt = PT if base == 0 else PT1
                nm, hw = (1, 2 * HD) if s == 0 else (2, HD)
                for m in range(nm):
                    h = b * nm + m
                    for kt in range(t + 1):
                        ins = pe.matmul(OB[t][:, hw * h:hw * h + hw], pt[:, (base + j) % 2, m * (t + 1) + kt, :],
                                        z[:, kt, vcol + hw * h:vcol + hw * h + hw], start=(kt == 0), stop=(kt == t))
                ins.then_inc(pv_done, 1)

            def out_proj(l):
                for cc in range(2):
                    n = N_OUT[l] + cc
                    full(n)
                    for k in range(4):
                        for f in range(KD):
                            ins = pe.matmul(A4[:, f // 2, TOK * (f % 2):TOK * (f % 2) + TOK],
                                            slot4(n)[:, k, P * f:P * f + P], hT[:, 4 * cc + k, :],
                                            start=(cc == 0 and k == 0 and f % 2 == 0), stop=(cc == 1 and k == 3),
                                            skip_group_check=True)
                    ins.then_inc(slot_used, 1)
                pe.wait_ge(slot_used, used_after(N_OUT[l] + 1))
                pe.nop().then_inc(wout_done, 1)

            def moe(l):
                ub = (U_HT0, U_HT1)[l]
                for t in range(TT):
                    for h in range(2):
                        tr_unit(ub + 2 * t + h, [hT[:, 4 * h + b, P * t:P * t + P] for b in range(4)],
                                [(h_ready, 2 * l + 2)])
                for t in range(TT):
                    for k in range(KD):
                        ins = pe.matmul(B5[:, 36 * t:36 * t + 36], hT[:, k, P * t:P * t + P], wge[:, l, k, :],
                                        start=(k == 0), stop=(k == KD - 1))
                ins.then_inc(logit_done, 1)
                pe.wait_ge(x_upd, 2 * l + 1)
                for bank in range(4):
                    for q in range(4):
                        ins = pe.matmul(A4[:, bank, P * q:P * q + P], ident, C("cb2")[:, 0:P], start=(q == 0),
                                        stop=False, skip_group_check=True)
                pe.wait_ge(mask_ready, l + 1)
                M = [rt[:, 0, t, :] for t in range(TT)]
                pe.matmul(B5[:, 0:NE], tri, M[0], start=True, stop=True)
                pe.matmul(B5[:, NE:2 * NE], ones, M[0], start=True, stop=False)
                pe.matmul(B5[:, NE:2 * NE], tri, M[1], start=False, stop=True)
                pe.matmul(B5[:, 2 * NE:3 * NE], ones, M[0], start=True, stop=False)
                pe.matmul(B5[:, 2 * NE:3 * NE], ones, M[1], start=False, stop=True).then_inc(rank_done, 1)

                dbase, sbase, ebase = l * NP5 * (2 * GE + 1), l * (2 * GE + 2), l * NE

                def dispatch(sm, g, part, ready, copied):
                    if part == 0:
                        pe.wait_ge(sm.ready, ready)
                    pe.wait_ge(sm.disp_ev, copied + 1)
                    if part < 4:
                        for q in range(2):
                            f = 2 * part + q
                            for t in range(TT):
                                ins = pe.matmul(B4[:, 256 * q:256 * q + 256], htok[:, t, P * f:P * f + P], Sd[:, g, t, :],
                                                start=(t == 0), stop=(t == 1))
                    else:
                        for pr in range(2):
                            for t in range(TT):
                                ins = pe.transpose(B4[:, 256 * pr + P * t:256 * pr + P * t + P],
                                                   Sw[:, g, t, P * pr:P * pr + P], ident)
                    ins.then_inc(sm.disp, 1)

                def gate_up(sm, g, j, e1, wa, wb):
                    pe.wait_ge(sm.hid, e1 + 1)
                    for k in range(KD):
                        for m, w in enumerate((wa, wb)):
                            ins = pe.matmul(B5[64 * m:64 * m + 64, :], xgT[:, g, k, CH * j:CH * j + CH], w[:, k, :],
                                            start=(k == 0), stop=(k == KD - 1))
                    ins.then_inc(sm.ab, 1)

                def hidden_transposed(sm, q, e1):
                    pe.wait_ge(sm.hid, e1 + 2)
                    for k in range(KF):
                        ins = pe.transpose(B6[:, P * k:P * k + P], hid[:, q % 2, P * k:P * k + P], ident)
                    ins.then_inc(sm.hidT_ps, 1)

                def down(sm, q, e1, w):
                    pe.wait_ge(sm.y_lo, e1 + 1)
                    pe.wait_ge(sm.y_hi, e1 + 1)
                    pe.wait_ge(sm.hidT, e1 + 1)
                    for k in range(KF):
                        for m in range(2):
                            ins = pe.matmul(B7[64 * m:64 * m + 64, :], hidTb[:, q % 2, k, :],
                                            w[:, k, 512 * m:512 * m + 512], start=(k == 0), stop=(k == KF - 1))
                    ins.then_inc(sm.y, 1)

                def combine(sm, g, q, e1):
                    pe.wait_ge(sm.y_lo, e1 + 2)
                    pe.wait_ge(sm.y_hi, e1 + 2)
                    pr = q // 2
                    for f in range(KD):
                        ins = pe.matmul(A4[:, f // 2, TOK * (f % 2):TOK * (f % 2) + TOK],
                                        y2[:, pr % 2, P * f:P * f + P], SwT[:, g, pr % 2, :],
                                        start=False, stop=False, skip_group_check=True)
                    ins.then_inc(sm.comb, 1)

                pe.wait_ge(tr_ev, ub + 4)
                for part in range(NP5):
                    dispatch(main, 0, part, sbase + 1, dbase + part)
                with pe.Fori(0, TURNS) as i:
                    for g in range(2):
                        for j in range(GE):
                            q = GE * g + j
                            n = N_MOE[l] + 3 * q
                            e1 = i * (2 * GE) + (ebase + q)
                            gi = i * 2 + g
                            fill = i * (16 * (6 * GE // RING))

                            def ahead(part):
                                dispatch(main, 1 - g, part, gi + (sbase + 2), gi * NP5 + (dbase + NP5 + part))

                            if j == 0:
                                pe.wait_ge(main.disp_ev, gi * NP5 + (dbase + NP5 + 1))
                            pe.wait_ge(slot_full[slot(n)], fill + fills(n))
                            pe.wait_ge(slot_full[slot(n + 1)], fill + fills(n + 1))
                            gate_up(main, g, j, e1, slot8(n), slot8(n + 1))
                            ahead(j)
                            hidden_transposed(main, q, e1)
                            if j == 3:
                                ahead(4)
                            pe.wait_ge(slot_full[slot(n + 2)], fill + fills(n + 2))
                            down(main, q, e1, slot4(n + 2))
                            if j % 2 == 1:
                                combine(main, g, q, e1)

                def more_experts(gb, i):
                    sm = more[l]
                    for part in range(NP5):
                        dispatch(sm, 0, part, gb + 1, gb * NP5 + part)
                    pe.wait_ge(sm.disp_ev, gb * NP5 + (NP5 + 1))
                    for j in range(GE):
                        e1 = gb * GE + j
                        pe.wait_ge(more_full[l][0], e1 * 16 + 16)
                        pe.wait_ge(more_full[l][1], e1 * 16 + 16)
                        gate_up(sm, 0, j, e1, slot8(0), slot8(1))
                        hidden_transposed(sm, j, e1)
                        pe.wait_ge(more_full[l][2], e1 * 16 + 16)
                        down(sm, j, e1, slot4(2))
                        if j % 2 == 1:
                            combine(sm, 0, j, e1)

                more_chunks(pe, l, more_experts)

            for sm in (main, *more):
                pe.nop().then_inc(sm.y, 1)
            pe.wait_ge(in_cst, 16)
            pe.wait_ge(in_x, 16)
            for t in range(TT):
                for h in range(2):
                    for b in range(4):
                        ins = pe.transpose(A4[:, 2 * t + h, P * b:P * b + P], htok[:, t, 512 * h + P * b:512 * h + P * b + P], ident)
                    ins.then_inc(x_tr, 1)
            for r in range(3):
                ada_round(0, r)
                ada_columns(0, r)
            sum_squares(0)
            pe.wait_ge(h_ready, 1)
            pe.wait_ge(x_ev, 4)
            for q, ch in enumerate(IN0_ORDER):
                project(0, q, ch, n_in0(q), TT * q)
                if q == 3:
                    for t in range(TT):
                        tr_unit(U_IDX + t, [z0[:, t, 3072:3200], z0[:, t, 3200:3328], ikrep[:, t, :]], [(qk_ready, t + 1)])
                if q == 4:
                    for t in range(TT):
                        for h in range(2):
                            tr_unit(U_B + 2 * t + h, [z0[:, t, 1536 + 512 * h + P * b:1536 + 512 * h + P * b + P] for b in range(4)],
                                    [(qk_ready, 3 + t)])
                if q in ADA1_AFTER:
                    ada_round(1, ADA1_AFTER.index(q))
                    ada_columns(1, ADA1_AFTER.index(q))
            for t in range(TT):
                for h in range(2):
                    tr_unit(U_A + 2 * t + h, [z0[:, t, 512 * h + P * b:512 * h + P * b + P] for b in range(4)], [(qk_ready, 5 + t)])
            pe.wait_ge(z_ready, 14)
            pe.wait_ge(tr_ev, U_IDX + 2)
            for t in range(TT):
                if t:
                    pe.wait_ge(idx_relu, 2)
                for half in range(2):
                    w = P * (t + 1)
                    for m in range(4):
                        ins = pe.matmul(A4[:, m, TOK * half:TOK * half + w], idxT[32 * m:32 * m + 32, half, P * t:P * t + P],
                                        idxT[32 * m:32 * m + 32, 2, 0:w], start=True, stop=True)
                ins.then_inc(idx_s, 1)
            pe.wait_ge(idx_relu, 4)
            pe.wait_ge(tr_ev, U_ATT0)
            N0 = len(L0_UNITS)
            att_score(0, 0, 0, *L0_UNITS[0])
            att_score(0, 0, 1, *L0_UNITS[1])
            for j, (s, b, t) in enumerate(L0_UNITS):
                att_pt(0, U_ATT0, j, s, b, t)
                if j + 2 < N0:
                    att_score(0, 0, j + 2, *L0_UNITS[j + 2])
                if j in (8, 12) :
                    pe.wait_ge(o_ready, 1 + (j == 12))
                att_pv(0, U_ATT0, j, s, b, t)
            for t in range(TT):
                for h in range(2):
                    tr_unit(U_OT0 + 2 * t + h, [htok[:, t, 512 * h + P * b:512 * h + P * b + P] for b in range(4)],
                            [(o_ready, 3 + t)])
            pe.wait_ge(tr_ev, U_OT0 + 4)
            out_proj(0)
            sum_squares(1)
            moe(0)
            tr_unit(U_S5, [s5row[:, :]], [(in_par, 16 * N_PAR)])
            sum_squares(2)
            pe.wait_ge(h_ready, 3)
            pe.wait_ge(x_upd, 2)
            PD = 14
            for q, ch in enumerate(IN1_ORDER):
                n = N_IN1 + q
                if ch != 3:
                    project(1, q, ch, n, PD)
                    PD += 2
                else:
                    full(n)
                    for f in range(4):
                        pe.wait_ge(z_ready, PD - 3)
                        for k in range(KD):
                            ins = pe.matmul(A4[:, PD % 4, 0:TOK], slot8(n)[:, k, P * f:P * f + P], hT[:, k, :],
                                            start=(k == 0), stop=(k == KD - 1))
                        ins.then_inc(proj_done, 1)
                        PD += 1
                    pe.wait_ge(proj_done, PD)
                    pe.nop().then_inc(slot_used, 1)
            for v in range(2):
                tr_unit(U_S5 + 1 + v, [Bd[:, v, 4 * q4:4 * q4 + 4, :].rearrange("p a b -> p (a b)") for q4 in range(4)], [(p5_bt, 1)])
            for v in range(2):
                tr_unit(U_S5 + 3 + v, [Cd[:, v, q4, :] for q4 in range(4)], [(p5_bt, 1)])
            pe.wait_ge(z_ready, PD)
            pe.wait_ge(tr_ev, U_S5 + 5)
            for q4 in range(4):
                if q4:
                    pe.wait_ge(bu_read, q4)
                for v in range(2):
                    for jj in range(4):
                        ins = pe.matmul(A4[:, jj, TOK * v:TOK * v + TOK],
                                        BT[32 * jj:32 * jj + 32, v, q4, :], uT[32 * jj:32 * jj + 32, q4, :],
                                        start=True, stop=True)
                ins.then_inc(bu_done, 1)
                for half in range(2):
                    pe.wait_ge(prod_ready, 2 * q4 + half + 1)
                    for v in range(2):
                        for jj in range(4):
                            which = (0, 1)[v] if half == 0 else 2
                            ins = pe.matmul(B4[32 * jj:32 * jj + 32, 0:TOK], CT[:, which, q4, 32 * jj:32 * jj + 32],
                                            mm[:, v, jj, :], start=(half == 0 and v == 0), stop=(half == 1 and v == 1),
                                            skip_group_check=True)
                    ins.then_inc(y5_done, 1)
            pe.wait_ge(gy_ready, 1)
            full(N_GLU)
            for f in range(4):
                for k in range(4):
                    ins = pe.matmul(A4[:, f // 2, TOK * (f % 2):TOK * (f % 2) + TOK], slot8(N_GLU)[:, k, P * f:P * f + P],
                                    gy[:, k, :], start=(k == 0), stop=(k == 3))
            ins.then_inc(slot_used, 1)
            pe.wait_ge(slot_used, used_after(N_GLU))
            pe.nop().then_inc(glu_done, 1)
            pe.wait_ge(yo_ready, 1)
            for t in range(TT):
                for h in range(2):
                    tr_unit(U_C + 2 * t + h, [z1[:, t, 512 * h + P * b:512 * h + P * b + P] for b in range(4)], [(qk_ready, 7 + t)])
            pe.wait_ge(tr_ev, U_C + 4)
            att_score(1, N0, 0, *L1_UNITS[0])
            att_score(1, N0, 1, *L1_UNITS[1])
            for j, (s, b, t) in enumerate(L1_UNITS):
                att_pt(N0, U_ATT1, j, s, b, t)
                if j + 2 < len(L1_UNITS):
                    att_score(1, N0, j + 2, *L1_UNITS[j + 2])
                att_pv(N0, U_ATT1, j, s, b, t)
            for t in range(TT):
                tr_unit(U_OT1 + t, [htok[:, t, P * b:P * b + P] for b in range(4)], [(o_ready, 5 + t)])
            pe.wait_ge(tr_ev, U_OT1 + 2)
            out_proj(1)
            sum_squares(3)
            moe(1)
            pe.wait_ge(x_upd, 4)
            for t in range(TT):
                for h in range(2):
                    for b in range(4):
                        ins = pe.transpose(A4[:, 2 * t + h, P * b:P * b + P], xT[:, 4 * h + b, P * t:P * t + P], ident)
                    ins.then_inc(x_tr, 1)

        @block.vector
        def _(dve):
            count = [0]

            def link(ins):
                count[0] += 1
                ins.then_inc(s_dve, 1)
                dve.wait_ge(s_dve, count[0])

            def tt(out, a0, a1, op):
                link(dve.tensor_tensor(out, a0, a1, op))

            def ts(out, a0, s1, s2, o0, o1=ALU.bypass):
                link(dve.tensor_scalar(out, a0, s1, s2, o0, o1) if s2 is not None else dve.tensor_scalar(out, a0, s1, None, o0))

            def stt(out, a0, s, a1, o0, o1):
                link(dve.scalar_tensor_tensor(out, a0, s, a1, o0, o1))

            def tell(s, n=1):
                dve.nop().then_inc(s, n)

            roots = [0]

            def rsqrt(x):
                tell(ms_ready)
                roots[0] += 1
                dve.wait_ge(sq_root, roots[0])
                link(dve.reciprocal(x, x))

            def norm_modulate(q):
                l, w = q // 2, q % 2
                sq = htok[:, :, :].rearrange("p t (a b) -> p (t a) b", b=TOK)
                tt(sq, xT[:, :, :], xT[:, :, :], ALU.mult)
                tell(sq_ready)
                dve.wait_ge(ssq_done, q + 1)
                ts(rstd[:, :], B5[:, 0:TOK], 1.0 / D, EPS, ALU.mult, ALU.add)
                tell(var_ready)
                dve.wait_ge(sd_ready, q + 1)
                link(dve.reciprocal(rstd[:, :], rstd[:, :]))
                tt(hT[:, :, :], xT[:, :, :], rstd[:, :].unsqueeze(1).to_broadcast([P, KD, TOK]), ALU.mult)
                for k in range(KD):
                    ins = dve.tensor_scalar(hT[:, k, :], hT[:, k, :], modc[:, l, 24 * w + 8 + k:24 * w + 9 + k],
                                            modc[:, l, 24 * w + k:24 * w + k + 1], ALU.mult, ALU.add)
                link(ins)
                tell(h_ready)

            def ada_rows(l, r):
                dve.wait_ge(ada_done, 3 * l + r + 1)
                if l or r:
                    dve.wait_ge(modT_done, 3 * l + r)
                if r == 0:
                    dve.wait_ge(in_brow, 64 * (l + 1))
                tt(modrow[:, :], B4[:, :], brow[:, r, :], ALU.add)
                tell(row_ready)
                dve.wait_ge(modT_done, 3 * l + r + 1)
                link(dve.tensor_copy(modc[:, l, 16 * r:16 * r + 16].rearrange("p (g b) -> p g b", g=4),
                                     B5[:, :].rearrange("p (b g x) -> p g b x", b=4, g=4)[:, :, :, 0]))
                if r == 0:
                    ts(modc[:, l, 8:16], modc[:, l, 8:16], 1.0, None, ALU.add)
                if r == 2:
                    ts(modc[:, l, 32:40], modc[:, l, 32:40], 1.0, None, ALU.add)
                tell(mod_ready)

            def rope(v, t, n, half, cn, sn, tmp):
                cc = C(cn).rearrange("p (t a) -> p t a", t=2)[:, t, :].unsqueeze(1).to_broadcast([P, n, 2 * half])
                ss = C(sn).rearrange("p (t a) -> p t a", t=2)[:, t, :].unsqueeze(1).to_broadcast([P, n, 2 * half])
                ta, tb = tmp[:, 0, 0:n, 0:2 * half], tmp[:, 1, 0:n, 0:2 * half]
                dve.tensor_tensor(ta, v[:, :, 0:2 * half], cc, ALU.mult)
                tt(tb, v[:, :, 0:2 * half], ss, ALU.mult)
                dve.tensor_tensor(v[:, :, 0:half], ta[:, :, 0:half], tb[:, :, half:2 * half], ALU.subtract)
                tt(v[:, :, half:2 * half], ta[:, :, half:2 * half], tb[:, :, 0:half], ALU.add)

            def norm_rope(v, t, gi, sq, tmp):
                tt(sq, v, v, ALU.mult)
                ms = small[:, 0:16]
                link(dve.tensor_reduce(ms, sq, AX, ALU.add))
                ts(ms, ms, 1.0 / HD, EPS, ALU.mult, ALU.add)
                rsqrt(ms)
                tt(v, v, ms.unsqueeze(2).to_broadcast([P, 16, HD]), ALU.mult)
                v4 = v.rearrange("p (q h) d -> p q h d", q=2)
                tt(v4, v4, gqk[:, gi, :, :].unsqueeze(2).to_broadcast([P, 2, 8, HD]), ALU.mult)
                rope(v, t, 16, 8, "rc", "rs", tmp)
                tell(qk_ready)

            def softmax_unit(base, j, s, b, t, buf, pr):
                u = base + j
                w = P * (t + 1)
                dve.wait_ge(score, u + 1)
                if u >= 2:
                    dve.wait_ge(expd, u - 1)
                src = A4[:, 2 * (u % 2):2 * (u % 2) + 2, 0:w]
                mask = selb[:, t, 0:w] if s == 1 else C("cb2")[:, 2 * P - w:2 * P]
                stt(buf[:, u % 2, :, 0:w], src, HD ** -0.5, mask.unsqueeze(1).to_broadcast([P, 2, w]), ALU.mult, ALU.add)
                tell(score_read)
                nm = small[:, 16 + 2 * (u % 4):18 + 2 * (u % 4)]
                link(dve.tensor_reduce(nm, buf[:, u % 2, :, 0:w], AX, ALU.max))
                ts(nm, nm, -1.0, None, ALU.mult)
                tell(negmax)

            def sums(u):
                return small[:, 32 + 2 * u:34 + 2 * u]

            def combine_unit(j, b, t):
                w = P * (t + 1)
                dve.wait_ge(expd, j + 1)
                su = sums(j)
                link(dve.reciprocal(su, su))
                tt(su[:, 1:2], su[:, 1:2], lamt[:, 4:5], ALU.mult)
                ts(prob[:, j % 2, 1, 0:w], prob[:, j % 2, 1, 0:w], su[:, 1:2], None, ALU.mult)
                stt(prob[:, j % 2, 0, 0:w], prob[:, j % 2, 0, 0:w], su[:, 0:1], prob[:, j % 2, 1, 0:w], ALU.mult, ALU.subtract)
                tell(attn_ready)

            def out_rows(base, t, s, pv, first):
                dve.wait_ge(pv_done, pv)
                su = small[:, 32 + 2 * (base + 4 * t):40 + 2 * (base + 4 * t)]
                link(dve.reciprocal(su, su))
                tt(htok[:, t, first:first + 512].rearrange("p (h d) -> p h d", h=8),
                   OB[t][:, :].rearrange("p (h d) -> p h d", h=8), su.unsqueeze(2).to_broadcast([P, 8, HD]), ALU.mult)
                tell(o_ready)

            def out_rows_a(t, pv):
                dve.wait_ge(pv_done, pv)
                o = htok[:, t, 0:512].rearrange("p (h d) -> p h d", h=4)
                link(dve.tensor_copy(o, OB[t][:, :].rearrange("p (h d) -> p h d", h=4)))
                sq = sc_sb[:, t % 2].rearrange("p a b -> p (a b)").rearrange("p (h d) -> p h d", h=4)
                tt(sq, o, o, ALU.mult)
                ms = small[:, 0:4]
                link(dve.tensor_reduce(ms, sq, AX, ALU.add))
                ts(ms, ms, 1.0 / (2 * HD), EPS, ALU.mult, ALU.add)
                rsqrt(ms)
                tt(o, o, ms.unsqueeze(2).to_broadcast([P, 4, 2 * HD]), ALU.mult)
                tt(o, o, subln[:, :].unsqueeze(1).to_broadcast([P, 4, 2 * HD]), ALU.mult)
                ts(o, o, 0.8, None, ALU.mult)
                tell(o_ready)

            def residual(l, w):
                for f in range(KD):
                    ins = dve.scalar_tensor_tensor(xT[:, f, :], A4[:, f // 2, TOK * (f % 2):TOK * (f % 2) + TOK],
                                                   modc[:, l, 24 * w + 16 + f:24 * w + 17 + f], xT[:, f, :], ALU.mult, ALU.add)
                link(ins)
                tell(x_upd)

            def route(l):
                M, lg, oh, dif, t1, t2, fine, oh2 = (rt[:, q] for q in range(8))
                dve.wait_ge(logit_done, l + 1)
                L = rt[:, 8:11].rearrange("p a t e -> p (a t e)")[:, 0:72].rearrange("p (t c) -> p t c", t=2)
                tt(L, B5[:, 0:72].rearrange("p (t c) -> p t c", t=2), bge[:, l, :].unsqueeze(1).to_broadcast([P, TT, 36]), ALU.add)
                co, fi = L[:, :, 0:NG], L[:, :, NG:]
                sc = rt[:, 12]
                mx, k1, m1, m2, den, w1, w2 = (sc[:, :, q:q + 1] for q in range(7))
                g4, e4 = sc[:, :, 8:12], sc[:, :, 12:16]
                link(dve.tensor_reduce(mx[:, :, 0], co, AX, ALU.max))
                tt(e4, co, mx.to_broadcast([P, TT, NG]), ALU.subtract)
                ts(g4, e4, 0.0, None, ALU.is_equal)
                tt(g4, g4, C("desc4").unsqueeze(1).to_broadcast([P, TT, NG]), ALU.mult)
                link(dve.tensor_reduce(k1[:, :, 0], g4, AX, ALU.max))
                tt(g4, g4, k1.to_broadcast([P, TT, NG]), ALU.is_equal)
                ts(g4, g4, BIG, -BIG, ALU.mult, ALU.add)
                f4 = fine.rearrange("p t (g e) -> p t g e", g=NG)
                tt(f4, fi.rearrange("p t (g e) -> p t g e", g=NG), g4.unsqueeze(3).to_broadcast([P, TT, NG, EPG]), ALU.add)

                def first_max(v, m, out):
                    link(dve.tensor_reduce(m[:, :, 0], v, AX, ALU.max))
                    tt(out, v, m.to_broadcast([P, TT, NE]), ALU.is_equal)
                    tt(out, out, C("desc32").unsqueeze(1).to_broadcast([P, TT, NE]), ALU.mult)
                    link(dve.tensor_reduce(k1[:, :, 0], out, AX, ALU.max))
                    tt(out, out, k1.to_broadcast([P, TT, NE]), ALU.is_equal)

                first_max(fine, m1, oh)
                stt(t1, oh, -3.0 * BIG, fine, ALU.mult, ALU.add)
                first_max(t1, m2, oh2)
                tt(M, oh, oh2, ALU.add)
                tell(mask_ready)
                tt(w2, m2, m1, ALU.subtract)
                tell(route_d)
                dve.wait_ge(route_e, l + 1)
                link(dve.tensor_reduce(den[:, :, 0], e4, AX, ALU.add))
                ts(w1, w2, 1.0, None, ALU.add)
                tt(den, den, w1, ALU.mult)
                link(dve.reciprocal(w1, den))
                tt(w2, w1, w2, ALU.mult)
                tt(oh, oh, w1.to_broadcast([P, TT, NE]), ALU.mult)
                tt(oh2, oh2, w2.to_broadcast([P, TT, NE]), ALU.mult)
                tt(wt[:, :, 0:NE], oh, oh2, ALU.add)
                dve.wait_ge(rank_done, l + 1)
                R = B5[:, 0:2 * NE].rearrange("p (t e) -> p t e", t=2)
                stt(rankm[:, :, 0:NE], R, 1.0, M, ALU.add, ALU.mult)
                ts(rankm[:, :, 0:NE], rankm[:, :, 0:NE], -1.0, None, ALU.add)
                n_tok, n_more = small[:, 250:251], small[:, 251:252]
                link(dve.tensor_reduce(n_tok, B5[:, 2 * NE:3 * NE], AX, ALU.max))
                ts(n_more, n_tok, CH + 0.5, None, ALU.is_ge)
                for q in range(2, MORE + 1):
                    stt(n_more, n_tok, q * CH + 0.5, n_more, ALU.is_ge, ALU.add)
                dve.tensor_copy(cnti[:, l:l + 1], n_more).then_inc(cnt_ready, 1)

            def moe(l):
                route(l)
                dbase, sbase, ebase, mbase = l * NP5 * (2 * GE + 1), l * (2 * GE + 2), l * NE, l * TT * (2 * GE + 2)

                def matrices(sm, col, g, made):
                    io = C("iota").unsqueeze(1).to_broadcast([P, GE, CH])
                    for t in range(TT):
                        r = rankm[:, t, bass.ds(col, GE)].unsqueeze(2).to_broadcast([P, GE, CH])
                        dve.tensor_tensor(Sd[:, g, t, :].rearrange("p (e s) -> p e s", e=GE), io, r, ALU.is_equal).then_inc(sm.mat, 1)
                    dve.wait_ge(sm.mat, made + TT)
                    for t in range(TT):
                        w = wt[:, t, bass.ds(col, GE)].unsqueeze(2).to_broadcast([P, GE, CH])
                        ins = dve.tensor_tensor(Sw[:, g, t, :].rearrange("p (e s) -> p e s", e=GE),
                                                Sd[:, g, t, :].rearrange("p (e s) -> p e s", e=GE), w, ALU.mult)
                    ins.then_inc(sm.ready, 1)

                def copy_dispatched(sm, g, part, before):
                    dve.wait_ge(sm.disp, before + 1)
                    dst = xgT[:, g, 2 * part:2 * part + 2, :] if part < 4 else SwT[:, g, :, :]
                    dve.tensor_copy(dst, B4[:, :].rearrange("p (a b) -> p a b", a=2)).then_inc(sm.disp_ev, 1)

                def gated(sm, q, e1):
                    dve.wait_ge(sm.silu, e1 + 1)
                    dve.tensor_tensor(hid[64:128, q % 2, :], silu_a[64:128, q % 2, :], B5[64:128, :],
                                      ALU.mult).then_inc(sm.hid, 1)

                def copy_y(sm, q, e1):
                    dve.wait_ge(sm.y, e1 + 2)
                    dve.tensor_copy(y2[64 * (q % 2):64 * (q % 2) + 64, (q // 2) % 2, 0:512], B7[0:64, :]).then_inc(sm.y_lo, 1)

                for g in range(2):
                    matrices(main, GE * g, g, mbase + TT * g)
                link(dve.memset(hid[0:64, :, :], 0.0))
                for part in range(NP5):
                    copy_dispatched(main, 0, part, dbase + part)
                with dve.Fori(0, TURNS) as i:
                    for g in range(2):
                        gi = i * 2 + g
                        dve.wait_ge(main.disp, gi * NP5 + (dbase + NP5))
                        matrices(main, gi * GE + 2 * GE, g, gi * TT + (mbase + 2 * TT))
                        for j in range(GE):
                            q = GE * g + j
                            e1 = i * (2 * GE) + (ebase + q)
                            gated(main, q, e1)
                            copy_dispatched(main, 1 - g, j, gi * NP5 + (dbase + NP5 + j))
                            if j == 3:
                                copy_dispatched(main, 1 - g, 4, gi * NP5 + (dbase + NP5 + 4))
                            copy_y(main, q, e1)

                def more_experts(gb, i):
                    sm = more[l]
                    matrices(sm, i * GE, 0, gb * TT)
                    for part in range(NP5):
                        copy_dispatched(sm, 0, part, gb * NP5 + part)
                    for j in range(GE):
                        e1 = gb * GE + j
                        gated(sm, j, e1)
                        copy_y(sm, j, e1)

                def lower_ranks(c):
                    dve.tensor_scalar(rankm[:, :, :], rankm[:, :, :], float(CH), None, ALU.subtract).then_inc(ranks_down[l], 1)
                    dve.wait_ge(ranks_down[l], c + 1)
                    dve.sem_inc(more_over, 1)

                def all_combined(c):
                    dve.wait_ge(more[l].comb, (c + 1) * (NE // 2))
                    dve.sem_inc(more_over, 1)

                dve.wait_ge(main.disp, dbase + NP5 * (2 * GE + 1))
                dve.wait_ge(main.comb, (l + 1) * (NE // 2))
                more_chunks(dve, l, more_experts, before=lower_ranks, after=all_combined)
                residual(l, 1)

            for sm in (main, *more):
                for s in (sm.disp_ev, sm.hid, sm.y_lo):
                    tell(s)
            dve.wait_ge(in_cst, 16)
            dve.memset(rankm[:, :, NE:], -1.0)
            dve.memset(wt[:, :, NE:], 0.0)
            dve.wait_ge(c_exp, 1)
            ts(ctmp[:, 0, :], ctmp[:, 0, :], 1.0, None, ALU.add)
            link(dve.reciprocal(ctmp[:, 0, :], ctmp[:, 0, :]))
            tt(ctmp[:, 0, :], ctmp[:, 0, :], ccol[:, :], ALU.mult)
            link(dve.tensor_copy(crep[:, :, :], ctmp[:, 0, :].unsqueeze(2).to_broadcast([P, KD, 32])))
            tell(c_ready)
            for t in range(TT):
                for h in range(2):
                    dve.wait_ge(x_tr, 2 * t + h + 1)
                    link(dve.tensor_copy(xT[:, 4 * h:4 * h + 4, P * t:P * t + P], A4[:, 2 * t + h, :].rearrange("p (a b) -> p a b", a=4)))
                    tell(x_ev)
            dve.wait_ge(in_par, 16 * N_PAR)
            lp = small[:, 64:192].rearrange("p (a b) -> p a b", a=2)
            tt(lp, lrow[:, 0:4:2, :], lrow[:, 1:4:2, :], ALU.mult)
            link(dve.tensor_reduce(lamt[:, 0:2], lp, AX, ALU.add))
            tell(lam_s)
            dve.wait_ge(lam_e, 1)
            tt(lamt[:, 4:5], lamt[:, 2:3], lamt[:, 3:4], ALU.subtract)
            ts(lamt[:, 4:5], lamt[:, 4:5], 0.2, None, ALU.add)
            for r in range(3):
                ada_rows(0, r)
            norm_modulate(0)
            for t in range(TT):
                dve.wait_ge(z_ready, t + 1)
                iq = z0[:, t, 3072:3328].rearrange("p (h d) -> p h d", h=8)
                ik = z0[:, t, 3328:3360]
                tt(sqs[:, 0, 0:32], ik, ik, ALU.mult)
                ms = small[:, 0:1]
                link(dve.tensor_reduce(ms, sqs[:, 0, 0:32], AX, ALU.add))
                ts(ms, ms, 1.0 / 32, EPS, ALU.mult, ALU.add)
                rsqrt(ms)
                stt(ik, ik, ms, gidx[:, :], ALU.mult, ALU.mult)
                rope(iq, t, 8, 4, "ic", "is", tmp16)
                rope(ik.unsqueeze(1), t, 1, 4, "ic", "is", tmp16)
                link(dve.tensor_copy(ikrep[:, t, :].rearrange("p (r d) -> p r d", r=4), ik.unsqueeze(1).to_broadcast([P, 4, 32])))
                tell(qk_ready)
            ada_rows(1, 0)
            for s, zr, col in ((1, 6, 1536), (0, 10, 0)):
                for t in range(TT):
                    dve.wait_ge(z_ready, zr - 1 + t)
                    norm_rope(z0[:, t, col:col + SETW].rearrange("p (h d) -> p h d", h=16), t, s, sqs, tmp16)
                ada_rows(1, 2 - s)
            dve.wait_ge(z_ready, 14)
            for t in range(TT):
                w = P * (t + 1)
                acc = idx_acc[:, 0:w]
                for u in range(2 * t, 2 * t + 2):
                    dve.wait_ge(idx_relu, u + 1)
                    for m in range(4):
                        h = 4 * (u % 2) + m
                        prev = C("cb2")[:, 2 * P - w:2 * P] if h == 0 else acc
                        stt(acc, relu_sb[u % 2][:, m, 0:w], z0[:, t, 3360 + h:3361 + h], prev, ALU.mult, ALU.add)
                    tell(idx_acc_s)
                m8 = small[:, 240:248]
                for _ in range(TOPK // 8):
                    link(dve.max(m8, acc))
                    link(dve.match_replace(acc, m8, acc, SENT))
                ts(selb[:, t, 0:w], acc, SENT, -BIG, ALU.not_equal, ALU.mult)
                tt(selb[:, t, 0:w], selb[:, t, 0:w], C("cb2")[:, 2 * P - w:2 * P], ALU.add)
            units = L0_UNITS
            for j, (s, b, t) in enumerate(units):
                softmax_unit(0, j, s, b, t, sc_sb, prob)
                if j - 1 >= 8:
                    combine_unit(j - 1, *units[j - 1][1:])
                if j in (5, 9):
                    out_rows(0, (j - 5) // 4, 1, j - 1, 512)
                if j == 13:
                    out_rows_a(0, 12)
            combine_unit(15, *units[15][1:])
            out_rows_a(1, 16)
            dve.wait_ge(wout_done, 1)
            residual(0, 0)
            norm_modulate(1)
            moe(0)
            norm_modulate(2)

            def q(n):
                return s5p[:, n, :]

            LRE, LIM, DT, TH, ARG, MAG, K, TURN, TC, SN, CS, ABR, ABI, DEN, CRE, CIM, T1, T2 = range(18)
            dve.wait_ge(tr_ev, U_S5 + 1)
            dve.wait_ge(p5_dt, 1)
            tt(q(TH), q(LIM), q(DT), ALU.mult)
            tt(q(ARG), q(LRE), q(DT), ALU.mult)
            ts(q(K), q(TH), 1.0 / TWO_PI, None, ALU.mult)
            ts(q(K), q(K), MAGIC, None, ALU.add)
            ts(q(K), q(K), -MAGIC, None, ALU.add)
            stt(q(TURN), q(K), -C1, q(TH), ALU.mult, ALU.add)
            stt(q(TURN), q(K), -C2, q(TURN), ALU.mult, ALU.add)
            ts(q(TURN), q(TURN), 1.0 / TWO_PI, None, ALU.mult)
            ts(q(TC), q(TURN), 0.25, None, ALU.add)
            for x in (TURN, TC):
                y = T1
                ts(q(T1), q(x), MAGIC, None, ALU.add)
                ts(q(T1), q(T1), -MAGIC, None, ALU.add)
                tt(q(x), q(x), q(T1), ALU.subtract)
            tell(p5_arg)
            dve.wait_ge(p5_sc, 1)
            tt(q(ABR), q(MAG), q(CS), ALU.mult)
            tt(q(ABI), q(MAG), q(SN), ALU.mult)
            ts(q(ABR), q(ABR), -1.0, None, ALU.add)
            tt(q(T1), q(LRE), q(LRE), ALU.mult)
            tt(q(T2), q(LIM), q(LIM), ALU.mult)
            tt(q(DEN), q(T1), q(T2), ALU.add)
            link(dve.reciprocal(q(DEN), q(DEN)))
            tt(q(T1), q(ABR), q(LRE), ALU.mult)
            tt(q(T2), q(ABI), q(LIM), ALU.mult)
            tt(q(CRE), q(T1), q(T2), ALU.add)
            tt(q(CRE), q(CRE), q(DEN), ALU.mult)
            tt(q(T1), q(ABI), q(LRE), ALU.mult)
            tt(q(T2), q(ABR), q(LIM), ALU.mult)
            tt(q(CIM), q(T1), q(T2), ALU.subtract)
            tt(q(CIM), q(CIM), q(DEN), ALU.mult)
            cre = q(CRE).unsqueeze(2).to_broadcast([P, 16, 16])
            cim = q(CIM).unsqueeze(2).to_broadcast([P, 16, 16])
            tt(Bbar[:, 0], s5b[:, 0], cre, ALU.mult)
            tt(Btmp, s5b[:, 1], cim, ALU.mult)
            tt(Bbar[:, 0], Bbar[:, 0], Btmp, ALU.subtract)
            tt(Bbar[:, 1], s5b[:, 1], cre, ALU.mult)
            tt(Btmp, s5b[:, 0], cim, ALU.mult)
            tt(Bbar[:, 1], Bbar[:, 1], Btmp, ALU.add)
            link(dve.memset(Bd, 0.0))
            for v in range(2):
                for gp in range(2):
                    link(dve.tensor_copy(Bd[64 * gp:64 * gp + 64, v, :, 16 * gp:16 * gp + 16], Bbar[64 * gp:64 * gp + 64, v]))
                for gp in range(2):
                    ts(Cd[:, v, :, 64 * gp:64 * gp + 64], s5c[:, v], C("par")[:, gp:gp + 1], (1.0, -1.0)[v], ALU.mult, ALU.mult)
            tell(p5_bt)
            for t in range(TT):
                dve.wait_ge(z_ready, 17 + t)
                dve.wait_ge(tr_ev, U_S5 + 5)
                norm_rope(z1[:, t, 0:SETW].rearrange("p (h d) -> p h d", h=16), t, 2, sqs1, tmp16_1)
            link(dve.tensor_scalar(CT[:, 1], CT[:, 0], -1.0, None, ALU.mult))
            tell(p5_lam)
            for q4 in range(4):
                dve.wait_ge(tab_ready, q4 + 1)
                dve.wait_ge(bu_done, q4 + 1)
                cs, sn = tab5[:, 0], tab5[:, 1]
                bur, bui = A4[:, :, 0:TOK], A4[:, :, TOK:2 * TOK]
                if q4:
                    dve.wait_ge(y5_done, 2 * q4)
                tt(mm[:, 0], cs, bur, ALU.mult)
                tt(mm[:, 1], sn, bui, ALU.mult)
                tt(vv[:, 0], mm[:, 0], mm[:, 1], ALU.add)
                tt(mm[:, 0], cs, bui, ALU.mult)
                tt(mm[:, 1], sn, bur, ALU.mult)
                tell(bu_read)
                tt(vv[:, 1], mm[:, 0], mm[:, 1], ALU.subtract)
                for v in range(2):
                    for jj in range(4):
                        mg = s5p[:, MAG, 4 * q4 + jj:4 * q4 + jj + 1].to_broadcast([P, TOK])
                        ins = dve.tensor_tensor_scan(vv[:, v, jj, :], mg, vv[:, v, jj, :], 0.0, ALU.mult, ALU.add)
                link(ins)
                tt(mm[:, 0], cs, vv[:, 0], ALU.mult)
                tt(mm[:, 1], sn, vv[:, 1], ALU.mult)
                tell(prod_ready)
                dve.wait_ge(y5_done, 2 * q4 + 1)
                tt(mm[:, 0], sn, vv[:, 0], ALU.mult)
                tt(mm[:, 1], cs, vv[:, 1], ALU.mult)
                tell(prod_ready)
                tell(tab_used)
                dve.wait_ge(y5_done, 2 * q4 + 2)
                stt(y5[:, q4, :], uT[:, q4, :], s5d[:, q4:q4 + 1], B4[:, 0:TOK], ALU.mult, ALU.add)
            w0 = vv[:, 0]
            tt(w0, y5, y5, ALU.mult)
            ts(w0, w0, 0.044715, 1.0, ALU.mult, ALU.add)
            tt(w0, w0, y5, ALU.mult)
            tell(tanh_in)
            dve.wait_ge(tanh_out, 1)
            ts(w0, w0, 0.5, 0.5, ALU.mult, ALU.add)
            tt(gy, w0, y5, ALU.mult)
            tell(gy_ready)
            dve.wait_ge(sig_ready, 1)
            tt(hT[:, 4:8, :], gy, vv[:, 1], ALU.mult)
            tell(yo_ready)
            for j, (s, b, t) in enumerate(L1_UNITS):
                softmax_unit(16, j, s, b, t, sc_sb1, prob1)
                if j == 5:
                    out_rows(16, 0, 2, 20, 0)
            out_rows(16, 1, 2, 24, 0)
            dve.wait_ge(wout_done, 2)
            residual(1, 0)
            norm_modulate(3)
            moe(1)
            for t in range(TT):
                for h in range(2):
                    dve.wait_ge(x_tr, 4 + 2 * t + h + 1)
                    link(dve.tensor_copy(htok[:, t, 512 * h:512 * h + 512], A4[:, 2 * t + h, :]))
                tell(x_ev)

        @block.scalar
        def _(act):
            count = [0]

            def link(ins):
                count[0] += 1
                ins.then_inc(s_act, 1)
                act.wait_ge(s_act, count[0])

            for sm in (main, *more):
                act.nop().then_inc(sm.y_hi, 1)
            act.dma_start(cst[:, :], cst_d).then_inc(in_cst, 16)
            act.dma_start(htok[:, :, :], a["x"][0].rearrange("(t p) d -> p t d", p=P)).then_inc(in_x, 16)
            act.dma_start(ccol[:, :], a["c"][0].rearrange("(k p) -> p k", p=P), allow_slow_non_contiguous=True).then_inc(in_c, 16)
            bsrc = a["ada_b"].rearrange("l (r g n) -> l g r n", r=3, g=4)

            def load_brow(l):
                for g in range(4):
                    act.dma_start(brow[32 * g:32 * g + 32, :, :], bsrc[l, g].partition_broadcast(32)).then_inc(in_brow, 16)

            load_brow(0)
            for dst, src, slow in PARAMS:
                act.dma_start(dst, src, allow_slow_non_contiguous=slow).then_inc(in_par, 16)
            act.wait_ge(in_c, 16)
            act.activation(ctmp[:, 0, :], ccol[:, :], ACT.Exp, scale=-1.0).then_inc(c_exp, 1)
            act.wait_ge(lam_s, 1)
            act.activation(lamt[:, 2:4], lamt[:, 0:2], ACT.Exp).then_inc(lam_e, 1)

            def tr_evac(u, dst, nb):
                act.wait_ge(tr_done, u + 1)
                src = TRB[u % 2][:, 0:P * nb].rearrange("p (a b) -> p a b", a=nb)
                act.copy(dst, src).then_inc(tr_ev, 1)

            def root(n, x):
                act.wait_ge(ms_ready, n)
                act.activation(x, x, ACT.Sqrt).then_inc(sq_root, 1)

            def norm_root(q):
                act.wait_ge(var_ready, q + 1)
                act.activation(rstd[:, :], rstd[:, :], ACT.Sqrt).then_inc(sd_ready, 1)

            def att_exp(base, ub, j, s, b, t, buf, pr):
                u = base + j
                w = P * (t + 1)
                act.wait_ge(negmax, u + 1)
                if j >= 2:
                    act.wait_ge(tr_done, ub + j - 1)
                for m in range(2):
                    ins = act.activation(pr[:, u % 2, m, 0:w], buf[:, u % 2, m, 0:w], ACT.Exp,
                                         bias=small[:, 16 + 2 * (u % 4) + m:17 + 2 * (u % 4) + m],
                                         accum_out=small[:, 32 + 2 * u + m:33 + 2 * u + m])
                    link(ins)
                act.nop().then_inc(expd, 1)

            def att_pt(base, ub, j, s, b, t, pt):
                if j >= 2:
                    act.wait_ge(pv_done, base + j - 1)
                nb = n_maps(s) * (t + 1)
                tr_evac(ub + j, pt[:, (base + j) % 2, 0:nb, :], nb)

            def moe(l):
                ub = (U_HT0, U_HT1)[l]
                for t in range(TT):
                    for h in range(2):
                        tr_evac(ub + 2 * t + h, htok[:, t, 512 * h:512 * h + 512].rearrange("p (a b) -> p a b", a=4), 4)
                act.wait_ge(route_d, l + 1)
                link(act.activation(rt[:, 12, :, 12:16], rt[:, 12, :, 12:16], ACT.Exp))
                act.activation(rt[:, 12, :, 6:7], rt[:, 12, :, 6:7], ACT.Exp).then_inc(route_e, 1)
                ebase = l * NE

                def silu(sm, q, e1):
                    act.wait_ge(sm.ab, e1 + 1)
                    act.activation(silu_a[64:128, q % 2, :], B5[0:64, :], ACT.Silu).then_inc(sm.silu, 1)

                def copy_hidT(sm, q, e1):
                    act.wait_ge(sm.hidT_ps, e1 + 1)
                    act.copy(hidTb[:, q % 2, :, :], B6[:, :].rearrange("p (a b) -> p a b", a=KF)[:, :, P - CH:]).then_inc(sm.hidT, 1)

                def copy_y(sm, q, e1):
                    act.wait_ge(sm.y, e1 + 2)
                    act.copy(y2[64 * (q % 2):64 * (q % 2) + 64, (q // 2) % 2, 512:1024], B7[64:128, :]).then_inc(sm.y_hi, 1)

                with act.Fori(0, TURNS) as i:
                    for q in range(2 * GE):
                        e1 = i * (2 * GE) + (ebase + q)
                        silu(main, q, e1)
                        copy_hidT(main, q, e1)
                        copy_y(main, q, e1)

                def more_experts(gb, i):
                    for j in range(GE):
                        e1 = gb * GE + j
                        silu(more[l], j, e1)
                        copy_hidT(more[l], j, e1)
                        copy_y(more[l], j, e1)

                act.wait_ge(main.comb, (l + 1) * (NE // 2))
                more_chunks(act, l, more_experts)

            norm_root(0)
            act.wait_ge(mod_ready, 3)
            load_brow(1)
            ev = [(("z", q, t)) for q in range(7) for t in range(TT)]
            rn = 0

            def z_evac(q, t):
                ch = IN0_ORDER[q]
                w = min(512, EV_IN - 512 * ch)
                act.wait_ge(proj_done, TT * q + t + 1)
                act.copy(z0[:, t, 512 * ch:512 * ch + w], A4[:, (TT * q + t) % 4, 0:w]).then_inc(z_ready, 1)

            for q in range(7):
                for t in range(TT):
                    z_evac(q, t)
                if q == 1:
                    root(1, small[:, 0:1])
                    root(2, small[:, 0:1])
                if q == 3:
                    for t in range(TT):
                        tr_evac(U_IDX + t, idxT, 3) if False else tr_evac(U_IDX + t, idxT[:, :, P * t:P * t + P], 3)
                    root(3, small[:, 0:16])
                    root(4, small[:, 0:16])
                if q == 4:
                    for t in range(TT):
                        for h in range(2):
                            tr_evac(U_B + 2 * t + h, qkT0[:, 8 + 4 * h:12 + 4 * h, P * t:P * t + P], 4)
                    root(5, small[:, 0:16])
                    root(6, small[:, 0:16])
            for t in range(TT):
                for h in range(2):
                    tr_evac(U_A + 2 * t + h, qkT0[:, 4 * h:4 * h + 4, P * t:P * t + P], 4)
            for u in range(4):
                t, half, w = u // 2, u % 2, P * (u // 2 + 1)
                act.wait_ge(idx_s, t + 1)
                if u >= 2:
                    act.wait_ge(idx_acc_s, u - 1)
                act.activation(relu_sb[u % 2][:, :, 0:w], A4[:, :, TOK * half:TOK * half + w], ACT.Relu).then_inc(idx_relu, 1)
            for j, (s, b, t) in enumerate(L0_UNITS):
                att_exp(0, U_ATT0, j, s, b, t, sc_sb, prob)
                if j >= 1:
                    att_pt(0, U_ATT0, j - 1, *L0_UNITS[j - 1], PT)
                if j == 13:
                    root(7, small[:, 0:4])
            att_pt(0, U_ATT0, 15, *L0_UNITS[15], PT)
            root(8, small[:, 0:4])
            for t in range(TT):
                for h in range(2):
                    tr_evac(U_OT0 + 2 * t + h, hT[:, 4 * h:4 * h + 4, P * t:P * t + P], 4)
            norm_root(1)
            moe(0)
            tr_done_s5 = U_S5
            act.wait_ge(tr_done, U_S5 + 1)
            act.copy(s5p[:, 0:2, :], TRB[U_S5 % 2][:, 0:32].rearrange("p (a b) -> p a b", a=2)).then_inc(tr_ev, 1)
            act.wait_ge(in_par, 16 * N_PAR)
            act.activation(s5p[:, 2, :], logdt[:, :], ACT.Exp).then_inc(p5_dt, 1)
            norm_root(2)
            act.wait_ge(p5_arg, 1)
            act.activation(s5p[:, 5, :], s5p[:, 4, :], ACT.Exp)
            act.activation(s5p[:, 9, :], s5p[:, 7, :], ACT.Sin, scale=SIN_SCALE)
            act.activation(s5p[:, 10, :], s5p[:, 8, :], ACT.Sin, scale=SIN_SCALE).then_inc(p5_sc, 1)
            pd = 14
            for ch in IN1_ORDER:
                for t in range(4 if ch == 3 else TT):
                    act.wait_ge(proj_done, pd + 1)
                    if ch == 3:
                        act.copy(uT[:, t, :], A4[:, pd % 4, 0:TOK]).then_inc(z_ready, 1)
                    else:
                        act.copy(z1[:, t, 512 * ch:512 * ch + 512], A4[:, pd % 4, :]).then_inc(z_ready, 1)
                    pd += 1
            for v in range(2):
                tr_evac(U_S5 + 1 + v, BT[:, v], 4)
            for v in range(2):
                tr_evac(U_S5 + 3 + v, CT[:, 2 * v], 4)
            root(9, small[:, 0:16])
            root(10, small[:, 0:16])
            for q4 in range(4):
                if q4:
                    act.wait_ge(tab_used, q4)
                for v in range(2):
                    act.wait_ge(ph_ready, 2 * q4 + v + 1)
                    link(act.activation(tab5[:, v], ph[:, v], ACT.Sin, scale=SIN_SCALE))
                act.nop().then_inc(tab_ready, 1)
            act.wait_ge(tanh_in, 1)
            act.activation(vv[:, 0], vv[:, 0], ACT.Tanh, scale=GELU_C).then_inc(tanh_out, 1)
            act.wait_ge(glu_done, 1)
            for f in range(4):
                link(act.activation(vv[:, 1, f, :], A4[:, f // 2, TOK * (f % 2):TOK * (f % 2) + TOK], ACT.Sigmoid, bias=glub[:, f:f + 1]))
            act.nop().then_inc(sig_ready, 1)
            for t in range(TT):
                for h in range(2):
                    tr_evac(U_C + 2 * t + h, qkT1[:, 4 * h:4 * h + 4, P * t:P * t + P], 4)
            for j, (s, b, t) in enumerate(L1_UNITS):
                att_exp(16, U_ATT1, j, s, b, t, sc_sb1, prob1)
                if j >= 1:
                    att_pt(16, U_ATT1, j - 1, *L1_UNITS[j - 1], PT1)
            att_pt(16, U_ATT1, 7, *L1_UNITS[7], PT1)
            for t in range(TT):
                tr_evac(U_OT1 + t, hT[:, 0:4, P * t:P * t + P], 4)
            norm_root(3)
            moe(1)
            for t in range(TT):
                act.wait_ge(x_ev, 4 + t + 1)
                act.dma_start(out_d[0, P * t:P * t + P, :], htok[:, t, :]).then_inc(out_s, 16)
            act.wait_ge(out_s, 32)

        @block.gpsimd
        def _(pool):
            count = [0]

            def link(ins):
                count[0] += 1
                ins.then_inc(s_pool, 1)
                pool.wait_ge(s_pool, count[0])

            pool.wait_ge(p5_lam, 1)
            for q4 in range(4):
                if q4:
                    pool.wait_ge(tab_ready, q4)
                turn = s5p[:, 7, 4 * q4:4 * q4 + 4].unsqueeze(2).to_broadcast([P, 4, TOK])
                time = C("time").unsqueeze(1).to_broadcast([P, 4, TOK])
                link(pool.tensor_tensor(ph[:, 1], time, turn, ALU.mult))
                link(pool.tensor_scalar(ph[:, 0], ph[:, 1], 0.25, None, ALU.add))
                for v in range(2):
                    link(pool.tensor_scalar(phr, ph[:, v], MAGIC, None, ALU.add))
                    link(pool.tensor_scalar(phr, phr, -MAGIC, None, ALU.add))
                    link(pool.tensor_tensor(ph[:, v], ph[:, v], phr, ALU.subtract))
                    pool.nop().then_inc(ph_ready, 1)


_INS = ["x", "c", "ada_w", "ada_b", "moe_wg", "moe_bg", "moe_we", "moe_be", "moe_w1", "moe_w3", "moe_w2",
        "ev_w_in", "ev_w_out", "a_qn", "a_kn", "a_lq1", "a_lk1", "a_lq2", "a_lk2", "a_subln", "b_qn", "b_kn",
        "b_idx_kn", "od_w_in", "od_w_out", "c_qn", "c_kn", "s5_lam_re", "s5_lam_im", "s5_b_re", "s5_b_im",
        "s5_c_re", "s5_c_im", "s5_d", "s5_log_dt", "s5_glu_w", "s5_glu_b"]


def constants():
    import numpy as np

    t = np.zeros((P, CONST_W), np.float32)

    def put(name, v):
        lo, hi = CONST_AT[name]
        t[:, lo:hi] = v

    i = np.arange(P)
    put("ident", np.eye(P))
    put("ones", 1.0)
    put("tri", (i[:, None] < i[None, :]) * 1.0)
    put("cb2", np.concatenate([np.zeros((P, P)), np.where(i[None, :] <= i[:, None], 0.0, -BIG)], axis=1))
    put("iota", np.arange(CH)[None, :])
    put("time", np.arange(TOK)[None, :])
    put("desc4", np.arange(NG, 0, -1)[None, :])
    put("desc32", np.arange(NE, 0, -1)[None, :])
    put("par", np.stack([(i // 16) % 2 == 0, (i // 16) % 2 == 1], axis=1) * 1.0)
    for cn, sn, rot in (("rc", "rs", 16), ("ic", "is", 8)):
        inv = np.float32(500000.0) ** (-(np.arange(0, rot, 2, dtype=np.float32) / np.float32(rot)))
        ang = np.arange(TOK, dtype=np.float32)[:, None] * inv[None, :].astype(np.float32)
        for name, f in ((cn, np.cos), (sn, np.sin)):
            v = f(ang.astype(np.float32)).astype(np.float32)
            v = np.concatenate([v, v], axis=1)
            put(name, v.reshape(TT, P, rot).transpose(1, 0, 2).reshape(P, TT * rot))
    return t


def kernel(**inputs):
    import numpy as np
    import concourse.bacc as bacc
    from concourse.bass_utils import run_bass_kernel_spmd

    nc = bacc.Bacc("TRN2", target_bir_lowering=False, num_devices=1)
    arrays, aps = {}, {}
    for name in _INS:
        arrays[f"in_{name}"] = np.ascontiguousarray(inputs[name])
        aps[name] = nc.dram_tensor(f"in_{name}", arrays[f"in_{name}"].shape, F32, kind="ExternalInput").ap()
    arrays["in_const"] = constants()
    cst_d = nc.dram_tensor("in_const", (P, CONST_W), F32, kind="ExternalInput").ap()
    out_d = nc.dram_tensor("out_x", (1, TOK, D), F32, kind="ExternalOutput").ap()
    build(nc, aps, cst_d, out_d)
    r = run_bass_kernel_spmd(nc, [arrays], core_ids=[0])
    return r.results[0]["out_x"]
```

```python
from contextlib import ExitStack

import concourse.bass as bass
from concourse import mybir

F32 = mybir.dt.float32
I32 = mybir.dt.int32
ALU = mybir.AluOpType
ACT = mybir.ActivationFunctionType
AX = mybir.AxisListType.X

P = 128
D = 1024
KD = D // P
TOK = 256
TT = TOK // P
LAYERS = 2
NE, NG, EPG = 32, 4, 8
FF = 512
KF = FF // P
EPS = 1e-6
BIG = 1.0e30
SENT = -3.0e38
HD = 64
TOPK = TOK // 4
SETW = 1024
EV_IN = 3368
OD_QKV = 1536
MAGIC = 12582912.0
TWO_PI = 6.283185307179586
SIN_SCALE = 6.2831845
C1 = 6.28125
C2 = 0.0019353071795864769
GELU_C = 0.7978845608028654

RING = 6
SLOT = 4096
IN0_ORDER = [6, 3, 4, 0, 1, 5, 2]
IN1_ORDER = [3, 0, 1, 2]

LOADS0 = ([("ada", 0, j) for j in range(4)] + [("in", 0), ("in", 1)] + [("ada", 0, j) for j in range(4, 8)]
          + [("in", 2), ("in", 3)] + [("ada", 0, j) for j in range(8, 12)] + [("in", 4), ("in", 5), ("in", 6)]
          + [("ada", 1, j) for j in range(12)] + [("out", 0), ("out", 1)])
LOADS1 = [("in", q) for q in range(4)] + [("glu",), ("out", 0), ("out", 1)]
N_MOE = [len(LOADS0), len(LOADS0) + 3 * 32 + len(LOADS1)]
N_MIX1 = N_MOE[0] + 3 * 32
N_ALL = N_MOE[1] + 3 * 32


def n_of(l, *what):
    return LOADS0.index(what) if l == 0 else N_MIX1 + LOADS1.index(what)


def stream():
    slot, fill, old, last, count, at = [], [], [], {}, [0] * RING, 0
    for n in range(N_ALL):
        size = RING - 2 if N_MOE[0] <= n < N_MOE[1] else RING
        if n in (N_MOE[0], N_MOE[1]):
            at = 0
        s = at % size
        at += 1
        count[s] += 1
        slot.append(s)
        fill.append(count[s])
        old.append(last.get(s))
        last[s] = n
    return slot, fill, old


SLOT_OF, FILL_OF, OLD_OF = stream()

CH = 64
GE = 4
TURNS = NE // (2 * GE)
NP5 = 5
PADE = NE + 2 * GE


def const_layout():
    at, n = {}, 0
    for name, w in (("ident", P), ("ones", P), ("tri", P), ("cb2", 2 * P), ("iota", CH), ("rc", 2 * 16),
                    ("rs", 2 * 16), ("ic", 2 * 8), ("is", 2 * 8), ("time", TOK), ("desc4", NG),
                    ("desc32", NE), ("par", 2)):
        at[name] = (n, n + w)
        n += w
    return at, n


CONST_AT, CONST_W = const_layout()


def build(nc, a, cst_d, out_d):
    ctx = ExitStack()
    with ctx:
        def sb(name, shape, dt=F32):
            return ctx.enter_context(nc.sbuf_tensor(name, shape, dt))

        def sem(name):
            return ctx.enter_context(nc.semaphore(name))

        ring = sb("ring", [P, RING, SLOT])
        cst = sb("cst", [P, CONST_W])
        xT = sb("xT", [P, KD, TOK])
        hT = sb("hT", [P, KD, TOK])
        htok = sb("htok", [P, TT, D])
        modrow = sb("modrow", [P, 512])
        brow = sb("brow", [P, 512])
        modc = sb("modc", [P, LAYERS, 48])
        crep = sb("crep", [P, KD, 32])
        ccol = sb("ccol", [P, KD])
        ctmp = sb("ctmp", [P, 2, KD])
        gqk = sb("gqk", [P, 3, 2, HD])
        gidx = sb("gidx", [P, 32])
        subln = sb("subln", [P, 2 * HD])
        lrow = sb("lrow", [P, 4, HD])
        lamt = sb("lamt", [P, 8])
        wge = sb("wge", [P, LAYERS, KD, NG + NE])
        bge = sb("bge", [P, LAYERS, NG + NE])
        s5row = sb("s5row", [32, P])
        logdt = sb("logdt", [P, 16])
        BT = sb("BT", [P, 2, 4, P])
        CT = sb("CT", [P, 3, 4, P])
        modp = sb("modp", [P, 2 * LAYERS, KD])
        s5d = sb("s5d", [P, 4])
        glub = sb("glub", [P, 4])
        s5p = sb("s5p", [P, 24, 16])
        rstd = sb("rstd", [P, TOK])
        small = sb("small", [P, 256])
        rankm = sb("rankm", [P, TT, PADE])
        wt = sb("wt", [P, TT, PADE])
        cnti = sb("cnti", [P, LAYERS], I32)
        WORK = 14336
        work = sb("work", [P, WORK])

        def C(name):
            lo, hi = CONST_AT[name]
            return cst[:, lo:hi]

        ident, ones, tri = C("ident"), C("ones"), C("tri")

        class Carve:

            def __init__(self, at=0):
                self.at = at

            def __call__(self, *dims):
                n = 1
                for d in dims:
                    n *= d
                ap = work[:, self.at:self.at + n]
                self.at += n
                assert self.at <= WORK, self.at
                if len(dims) == 2:
                    ap = ap.rearrange("p (a b) -> p a b", a=dims[0])
                elif len(dims) == 3:
                    ap = ap.rearrange("p (a b c) -> p a b c", a=dims[0], b=dims[1])
                return ap

        c = Carve()
        s5b = c(2, 16, 16)
        s5c = c(2, 4, HD)
        Bbar = c(2, 16, 16)
        Bd = c(2, 16, 32)
        Cd = c(2, 4, P)
        Btmp = c(16, 16)
        c = Carve()
        z0 = c(TT, EV_IN)
        qkT0 = c(16, TOK)
        idxT = c(3, TOK)
        selb = c(TT, TOK)
        at0 = c.at
        sqs = c(16, HD)
        c.at = at0
        sc_sb = c(2, 2, TOK)
        prob = hT[:, 0:4, :].rearrange("p (a b) c -> p a b c", a=2)
        PT = hT[:, 4:8, :].rearrange("p (a b) c -> p a (b c)", a=2).rearrange("p a (b c) -> p a b c", b=4)
        ikrep = c(TT, P)
        relu_sb = [sc_sb.rearrange("p a b c -> p (a b) c"), hT[:, 4:8, :]]
        idx_acc = prob[:, 0, 0, :]
        tmp16 = c(2, 16, 16)
        c = Carve()
        z1 = c(TT, OD_QKV)
        uT = c(4, TOK)
        tmp16_1 = c(2, 16, 16)
        sqs1 = c(16, HD)
        vv = c(2, 4, TOK)
        gy = c(4, TOK)
        tabs = ring[:, RING - 2:RING, :].rearrange("p v (j t) -> p v j t", t=TOK)
        mm = htok[:, :, :].rearrange("p t (a b) -> p t a b", b=TOK)
        y5 = c(4, TOK)
        qkT1 = c(8, TOK)
        sc_sb1 = vv.rearrange("p a b c -> p (a b) c")[:, 0:4, :].rearrange("p (a b) c -> p a b c", a=2)
        prob1 = vv.rearrange("p a b c -> p (a b) c")[:, 4:8, :].rearrange("p (a b) c -> p a b c", a=2)
        PT1 = c(2, 4, P)
        c = Carve()
        xgT = c(2, KD, GE * CH)
        Sd = c(4, GE * CH)
        Sw = c(4, GE * CH)
        SwT = c(2, 2, TOK)
        silu_a = c(2, FF)
        hid = c(2, FF)
        hidTb = c(2, KF, CH)
        y2 = c(2, D)
        rt = c(16, TT, NE)
        ph = c(2, 2, TOK)
        phr = c(2, TOK)
        Sd = Sd.rearrange("p (g t) s -> p g t s", g=2)
        Sw = Sw.rearrange("p (g t) s -> p g t s", g=2)

        PARAMS = []
        for s_, (qn, kn) in enumerate((("a_qn", "a_kn"), ("b_qn", "b_kn"), ("c_qn", "c_kn"))):
            PARAMS += [(gqk[:, s_, 0, :], a[qn][0].partition_broadcast(P), False),
                       (gqk[:, s_, 1, :], a[kn][0].partition_broadcast(P), False)]
        PARAMS += [(lrow[:, m, :], a[nm][0].partition_broadcast(P), False)
                   for m, nm in enumerate(("a_lq1", "a_lk1", "a_lq2", "a_lk2"))]
        PARAMS += [(gidx[:, :], a["b_idx_kn"][0].partition_broadcast(P), False),
                   (subln[:, :], a["a_subln"][0].partition_broadcast(P), False)]
        for l_ in range(LAYERS):
            PARAMS += [(wge[:, l_, :, 0:NG], a["moe_wg"][l_].rearrange("(k p) n -> p k n", p=P), False),
                       (wge[:, l_, :, NG:], a["moe_we"][l_].rearrange("(k p) n -> p k n", p=P), False),
                       (bge[:, l_, 0:NG], a["moe_bg"][l_].partition_broadcast(P), False),
                       (bge[:, l_, NG:], a["moe_be"][l_].partition_broadcast(P), False)]
        S5_PARAMS = [(s5row[0:16, :], a["s5_lam_re"][0].rearrange("(j g) p -> j (g p)", g=2), False),
                   (s5row[16:32, :], a["s5_lam_im"][0].rearrange("(j g) p -> j (g p)", g=2), False)]
        for g_ in range(2):
            S5_PARAMS.append((logdt[64 * g_:64 * g_ + 64, :],
                           a["s5_log_dt"][0].rearrange("(j g) -> g j", g=2)[g_].partition_broadcast(64), True))
        for v_, (bn, cn) in enumerate((("s5_b_re", "s5_c_re"), ("s5_b_im", "s5_c_im"))):
            S5_PARAMS += [(s5b[:, v_], a[bn][0].rearrange("(j g) p c -> (g p) j c", g=2), False),
                       (s5c[:, v_], a[cn][0].rearrange("(q g) c p -> (g c) q p", g=8), False)]
        PARAMS += [(s5d[:, :], a["s5_d"][0].rearrange("(q g) c -> (g c) q", g=8), True),
                   (glub[:, :], a["s5_glu_b"][0].rearrange("(q p) -> p q", p=P), True)]
        N_PAR, N_S5 = len(PARAMS), len(S5_PARAMS)

        A4 = ctx.enter_context(nc.psum_tensor("A4", [P, 4, 512], F32))
        B4, B5, B6, B7 = (ctx.enter_context(nc.psum_tensor(f"B{i}", [P, 512], F32)) for i in (4, 5, 6, 7))
        TRB = [B6, B7]
        OB = [B4, B5]

        slot_full = [sem(f"slot_full{i}") for i in range(RING)]
        slot_used = sem("slot_used")
        in_cst, in_x, in_c, in_par = sem("in_cst"), sem("in_x"), sem("in_c"), sem("in_par")
        in_brow, brow_zero = sem("in_brow"), sem("brow_zero")
        s_dve, s_act, s_pool = sem("dve_chain"), sem("act_chain"), sem("pool_chain")
        x_tr = sem("x_transposed")
        x_ev = sem("output_rows")
        c_exp, c_ready = sem("c_exp"), sem("c_ready")
        ada_done, row_ready, modT_done, mod_ready = sem("ada_done"), sem("row_ready"), sem("modT_done"), sem("mod_ready")
        sq_ready, ssq_done, var_ready, sd_ready, h_ready = (sem(n) for n in ("sq_ready", "ssq_done", "var_ready", "sd_ready", "h_ready"))
        proj_done, z_ready = sem("proj_done"), sem("z_ready")
        ms_ready, sq_root = sem("ms_ready"), sem("sq_root")
        tr_done, tr_ev = sem("tr_done"), sem("tr_evacuated")
        qk_ready = sem("qk_ready")
        idx_s, idx_relu, idx_acc_s = sem("idx_logits"), sem("idx_relu"), sem("idx_accumulated")
        score, score_read, negmax, expd, attn_ready = (sem(n) for n in ("score", "score_read", "negmax", "exp_done", "attn_ready"))
        pv_done, o_ready = sem("pv_done"), sem("o_ready")
        wout_done, x_upd = sem("wout_done"), sem("x_updated")
        lam_s, lam_e = sem("lam_sums"), sem("lam_exps")
        logit_done, route_d, route_e, mask_ready, rank_done = (sem(n) for n in (
            "logit_done", "route_diff", "route_exp", "mask_ready", "rank_done"))

        class MoeSems:

            def __init__(self, tag):
                def own(name):
                    return sem(name + tag)

                self.mat = own("slot_matrix")
                self.ready = own("matrices_ready")
                self.disp = own("dispatched")
                self.disp_ev = own("dispatch_copied")
                self.ab = own("ab_done")
                self.silu = own("silu_done")
                self.hid = own("hid_ready")
                self.hidT_ps = own("hid_transposed")
                self.hidT = own("hidT_ready")
                self.y = own("y_done")
                self.y_lo = own("y_copied_lo")
                self.y_hi = own("y_copied_hi")
                self.comb = own("combined")

        main = MoeSems("")
        more = [MoeSems(f"_more{l}") for l in range(LAYERS)]
        more_full = [[sem(f"more_full{l}_{m}") for m in range(3)] for l in range(LAYERS)]
        ranks_down = [sem(f"ranks_lowered{l}") for l in range(LAYERS)]
        cnt_ready = sem("chunks_counted")
        more_over = sem("more_steps_over")
        out_s = sem("out_written")
        p5_tr, p5_dt, p5_arg, p5_sc, p5_bt, p5_lam = (sem(n) for n in ("s5_lam_T", "s5_dt", "s5_arg", "s5_sincos", "s5_bt_in", "s5_turns"))
        ph_ready, tab_ready, bu_done, bu_read, prod_ready, y5_done, tab_used = (sem(n) for n in (
            "phase_ready", "tab_ready", "bu_done", "bu_read", "prod_ready", "y5_done", "tab_used"))
        y5_read, tab_done, in_s5 = sem("y5_read"), sem("tables_written"), sem("in_s5")
        tanh_in, tanh_out, gy_ready, glu_done, sig_ready, yo_ready = (sem(n) for n in (
            "tanh_in", "tanh_out", "gy_ready", "glu_done", "sig_ready", "yo_ready"))

        def slot(n):
            return SLOT_OF[n]

        def fills(n):
            return 16 * FILL_OF[n]

        def used_after(n):
            return n + 1 - (3 * NE if n >= N_MIX1 else 0)

        def slot8(n):
            return ring[:, slot(n), :].rearrange("p (k n) -> p k n", k=KD)

        def slot4(n):
            return ring[:, slot(n), :].rearrange("p (k n) -> p k n", k=4)

        L0_UNITS = [(1, b, t) for t in range(TT) for b in range(4)] + [(0, b, t) for t in range(TT) for b in range(4)]
        L1_UNITS = [(2, b, t) for t in range(TT) for b in range(4)]
        N0, N1 = len(L0_UNITS), len(L1_UNITS)
        LAG_PT, LAG_PV = 3, 4
        ADA1_AT = {4: "r0", 6: "c0", 9: "r1", 11: "c1", 14: "r2", 16: "c2"}

        ORDER = ["lam", "x0", "x1", "x2", "x3", "ada0r0", "ada0c0", "bt0", "bt1", "ct0", "ct1", "ada0r1", "ada0c1", "idx0", "idx1", "ada0r2",
                 "ada0c2", "B0", "B1", "B2", "B3", "A0", "A1", "A2", "A3"]
        for j in range(N0 + LAG_PT):
            if 0 <= j - LAG_PT < N0:
                ORDER.append(f"p{j - LAG_PT}")
            if j in ADA1_AT:
                ORDER.append("ada1" + ADA1_AT[j])
        ORDER += ["o0", "o1", "o2", "o3", "h0_0", "h0_1", "h0_2", "h0_3", "C0", "C1", "C2", "C3"]
        ORDER += [f"p{N0 + j}" for j in range(N1)] + ["o4", "o5", "h1_0", "h1_1", "h1_2", "h1_3"]
        U = {name: u for u, name in enumerate(ORDER)}

        def n_maps(s):
            return 1 if s == 0 else 2

        MORE = TOK // CH - 1

        def more_chunks(eng, l, body, before=None, after=None):
            eng.wait_ge(cnt_ready, l + 1)
            extra = eng.value_load(cnti[0:1, l:l + 1], min_val=0, max_val=MORE)
            with eng.Fori(0, MORE) as c:
                with eng.If(c < extra):
                    if before:
                        before(c)
                    with eng.Fori(0, NE // GE) as i:
                        body(c * (NE // GE) + i, i)
                    if after:
                        after(c)

        block = ctx.enter_context(nc.Block())

        @block.sync
        def _(sp):
            def slot_free(n):
                old = OLD_OF[n]
                if old is None:
                    return
                for l in range(LAYERS):
                    e, m = divmod(old - N_MOE[l], 3)
                    if 0 <= e < NE:
                        sp.wait_ge(main.ab if m < 2 else main.y, NE * l + e + 1 + m // 2)
                        return
                sp.wait_ge(slot_used, used_after(old))
                if n >= N_MOE[1] and old < N_MOE[0]:
                    sp.wait_ge(prod_ready, 8)

            def load(n, dst, src):
                slot_free(n)
                sp.dma_start(dst, src).then_inc(slot_full[slot(n)], 16)

            def load_mixer(l):
                w_in, w_out = (a["ev_w_in"], a["ev_w_out"]) if l == 0 else (a["od_w_in"], a["od_w_out"])
                for q, what in enumerate(LOADS0 if l == 0 else LOADS1):
                    n = q + (0, N_MIX1)[l]
                    if what[0] == "ada":
                        load(n, slot8(n), a["ada_w"][what[1], :, 512 * what[2]:512 * what[2] + 512]
                             .rearrange("(k p) n -> p k n", p=P))
                    elif what[0] == "in":
                        ch = (IN0_ORDER, IN1_ORDER)[l][what[1]]
                        w = min(512, EV_IN - 512 * ch) if l == 0 else 512
                        load(n, slot8(n)[:, :, 0:w], w_in[0, :, 512 * ch:512 * ch + w].rearrange("(k p) n -> p k n", p=P))
                    elif what[0] == "glu":
                        load(n, slot8(n)[:, 0:4, :], a["s5_glu_w"][0].rearrange("(k p) n -> p k n", p=P))
                    else:
                        load(n, slot4(n), w_out[0, 512 * what[1]:512 * what[1] + 512, :].rearrange("(k p) n -> p k n", p=P))

            def load_moe(l):
                w1 = a["moe_w1"].rearrange("l e (k p) n -> (l e) p k n", p=P)
                w3 = a["moe_w3"].rearrange("l e (k p) n -> (l e) p k n", p=P)
                w2 = a["moe_w2"].rearrange("l e (k p) n -> (l e) p k n", p=P)

                def expert(e):
                    for m, w in enumerate((w1, w3, w2)):
                        n = N_MOE[l] + 3 * e + m
                        load(n, (slot8 if m < 2 else slot4)(n), w[NE * l + e])

                T = 2 * GE
                for e in range(2):
                    expert(e)
                with sp.Fori(0, TURNS - 1) as i:
                    for q in range(2, T + 2):
                        for m, w in enumerate((w1, w3, w2)):
                            n = N_MOE[l] + 3 * q + m
                            e, m_old = divmod(3 * q + m - (n - OLD_OF[n]), 3)
                            sp.wait_ge(main.ab if m_old < 2 else main.y, i * T + (NE * l + e + 1 + m_old // 2))
                            src = w[bass.ds(i * T + (NE * l + q), 1)].rearrange("e p k n -> p (e k) n")
                            sp.dma_start((slot8 if m < 2 else slot4)(n), src).then_inc(slot_full[slot(n)], 16)
                for e in range(NE - T + 2, NE):
                    expert(e)

                def more_loads(gb, i):
                    for j in range(GE):
                        for m, w in enumerate((w1, w3, w2)):
                            sp.wait_ge(more[l].y, gb * GE + (j + 1))
                            src = w[bass.ds(i * GE + (NE * l + j), 1)].rearrange("e p k n -> p (e k) n")
                            sp.dma_start((slot8 if m < 2 else slot4)(m), src).then_inc(more_full[l][m], 16)

                def ring_empty(c):
                    sp.wait_ge(main.y, NE * (l + 1) + 1)

                def ring_free(c):
                    sp.wait_ge(more[l].y, c * NE + (NE + 1))
                    sp.sem_inc(more_over, 1)

                more_chunks(sp, l, more_loads, before=ring_empty, after=ring_free)

            for l in range(LAYERS):
                load_mixer(l)
                load_moe(l)

        @block.tensor
        def _(pe):
            def full(n):
                pe.wait_ge(slot_full[slot(n)], fills(n))

            units = [0]

            def pass_bank(name):
                u = units[0]
                assert ORDER[u] == name, (ORDER[u], name)
                units[0] += 1
                if u >= 2:
                    pe.wait_ge(tr_ev, u - 1)
                return TRB[u % 2]

            def tr_unit(name, parts, waits=()):
                for s, v in waits:
                    pe.wait_ge(s, v)
                bank = pass_bank(name)
                for b, src in enumerate(parts):
                    n = src.shape[0]
                    ins = pe.transpose(bank[:, P * b:P * b + n], src, ident[0:n, 0:n])
                ins.then_inc(tr_done, 1)

            def ada_rows(l, r):
                ns = [n_of(0, "ada", l, 4 * r + g) for g in range(4)]
                bank = pass_bank(f"ada{l}r{r}")
                if r == 0:
                    pe.wait_ge(in_brow, 16)
                for n in ns:
                    full(n)
                for g in range(4):
                    pe.matmul(bank[32 * g:32 * g + 32, :], ident[:, 12 * l + 4 * r + g:12 * l + 4 * r + g + 1].to_broadcast([P, 32]), brow[:, :],
                              start=True, stop=False)
                for k in range(KD):
                    for g in range(4):
                        ins = pe.matmul(bank[32 * g:32 * g + 32, :], crep[:, k, :], slot8(ns[g])[:, k, :],
                                        start=False, stop=(k == KD - 1))
                ins.then_inc(tr_done, 1)
                pe.wait_ge(tr_done, U[f"ada{l}r{r}"] + 1)
                pe.nop().then_inc(slot_used, 4)

            def ada_columns(l, r):
                tr_unit(f"ada{l}c{r}", [modrow[:, P * b:P * b + P] for b in range(4)], [(tr_ev, U[f"ada{l}r{r}"] + 1)])

            def sum_squares(q):
                pe.wait_ge(sq_ready, q + 1)
                for k in range(KD):
                    ins = pe.matmul(B5[:, 0:TOK], ones, htok[:, :, :].rearrange("p t (a b) -> p (t a) b", b=TOK)[:, k, :],
                                    start=(k == 0), stop=(k == KD - 1))
                ins.then_inc(ssq_done, 1)

            def project(l, q, ch, n, done, between=None):
                full(n)
                w = min(512, EV_IN - 512 * ch) if l == 0 else 512
                for t in range(TT):
                    if l or done + t >= 4:
                        pe.wait_ge(z_ready, done + t - 3 * (l == 0))
                    bank = A4[:, (done + t) % 4, :] if l == 0 else B5[:, :]
                    for k in range(KD):
                        ins = pe.matmul(bank[:, 0:w], hT[:, k, P * t:P * t + P], slot8(n)[:, k, 0:w],
                                        start=(k == 0), stop=(k == KD - 1))
                    ins.then_inc(proj_done, 1)
                    if between and t == 0:
                        between()
                pe.wait_ge(proj_done, done + TT)
                pe.nop().then_inc(slot_used, 1)

            def att_score(l, base, j, s, b, t):
                blk = (0, 8, 0)[s] + b
                qk = qkT0 if l == 0 else qkT1
                u = base + j
                if u >= 2:
                    pe.wait_ge(score_read, u - 1)
                w = P * (t + 1)
                for m in range(2):
                    ins = pe.matmul(A4[:, 2 * (u % 2) + m, 0:w], qk[64 * m:64 * m + 64, blk, P * t:P * t + P],
                                    qk[64 * m:64 * m + 64, blk + 4, 0:w], start=True, stop=True)
                ins.then_inc(score, 1)

            def att_pt(base, j, s, b, t):
                parts = [prob[:, (base + j) % 2, m, P * kt:P * kt + P] for m in range(n_maps(s)) for kt in range(t + 1)]
                if base:
                    parts = [prob1[:, (base + j) % 2, m, P * kt:P * kt + P] for m in range(n_maps(s)) for kt in range(t + 1)]
                w = [(expd, base + j + 1)]
                if s == 0:
                    w = [(attn_ready, b + 4 * t + 1)]
                tr_unit(f"p{base + j}", parts, w)

            def att_pv(base, j, s, b, t):
                pe.wait_ge(tr_ev, U[f"p{base + j}"] + 1)
                z, vcol = ((z0, 1024), (z0, 2560), (z1, 1024))[s]
                pt = PT if base == 0 else PT1
                nm, hw = (1, 2 * HD) if s == 0 else (2, HD)
                for m in range(nm):
                    h = b * nm + m
                    for kt in range(t + 1):
                        ins = pe.matmul(OB[t][:, hw * h:hw * h + hw], pt[:, (base + j) % 2, m * (t + 1) + kt, :],
                                        z[:, kt, vcol + hw * h:vcol + hw * h + hw], start=(kt == 0), stop=(kt == t))
                ins.then_inc(pv_done, 1)

            def attention(l, base, units, hook):
                n = len(units)
                for j in range(n + LAG_PV):
                    if j < n:
                        att_score(l, base, j, *units[j])
                    if 0 <= j - LAG_PT < n:
                        att_pt(base, j - LAG_PT, *units[j - LAG_PT])
                    if 0 <= j - LAG_PV:
                        if l == 0 and j - LAG_PV in (8, 12):
                            pe.wait_ge(o_ready, (j - LAG_PV) // 4 - 1)
                        att_pv(base, j - LAG_PV, *units[j - LAG_PV])
                    hook(j)

            def out_proj(l):
                for cc in range(2):
                    n = n_of(l, "out", cc)
                    full(n)
                    for k in range(4):
                        for f in range(KD):
                            ins = pe.matmul(A4[:, f // 2, TOK * (f % 2):TOK * (f % 2) + TOK],
                                            slot4(n)[:, k, P * f:P * f + P], hT[:, 4 * cc + k, :],
                                            start=(cc == 0 and k == 0 and f % 2 == 0), stop=(cc == 1 and k == 3),
                                            skip_group_check=True)
                    ins.then_inc(slot_used, 1)
                pe.wait_ge(slot_used, used_after(n))
                pe.nop().then_inc(wout_done, 1)

            def moe(l):
                for t in range(TT):
                    for h in range(2):
                        tr_unit(f"h{l}_{2 * t + h}", [hT[:, 4 * h + b, P * t:P * t + P] for b in range(4)],
                                [(h_ready, 2 * l + 2)])
                for t in range(TT):
                    for k in range(KD):
                        ins = pe.matmul(B5[:, 36 * t:36 * t + 36], hT[:, k, P * t:P * t + P], wge[:, l, k, :],
                                        start=(k == 0), stop=(k == KD - 1))
                ins.then_inc(logit_done, 1)
                pe.wait_ge(x_upd, 2 * l + 1)
                for bank in range(4):
                    for q in range(4):
                        ins = pe.matmul(A4[:, bank, P * q:P * q + P], ident, C("cb2")[:, 0:P], start=(q == 0),
                                        stop=False, skip_group_check=True)
                pe.wait_ge(mask_ready, l + 1)
                M = [rt[:, 0, t, :] for t in range(TT)]
                pe.matmul(B5[:, 0:NE], tri, M[0], start=True, stop=True)
                pe.matmul(B5[:, NE:2 * NE], ones, M[0], start=True, stop=False)
                pe.matmul(B5[:, NE:2 * NE], tri, M[1], start=False, stop=True)
                pe.matmul(B5[:, 2 * NE:3 * NE], ones, M[0], start=True, stop=False)
                pe.matmul(B5[:, 2 * NE:3 * NE], ones, M[1], start=False, stop=True).then_inc(rank_done, 1)

                dbase, sbase, ebase = l * NP5 * (2 * GE + 1), l * (2 * GE + 2), l * NE

                def dispatch(sm, g, part, ready, copied):
                    if part == 0:
                        pe.wait_ge(sm.ready, ready)
                    pe.wait_ge(sm.disp_ev, copied + 1)
                    if part < 4:
                        for q in range(2):
                            f = 2 * part + q
                            for t in range(TT):
                                ins = pe.matmul(B4[:, 256 * q:256 * q + 256], htok[:, t, P * f:P * f + P], Sd[:, g, t, :],
                                                start=(t == 0), stop=(t == 1))
                    else:
                        for pr in range(2):
                            for t in range(TT):
                                ins = pe.transpose(B4[:, 256 * pr + P * t:256 * pr + P * t + P],
                                                   Sw[:, g, t, P * pr:P * pr + P], ident)
                    ins.then_inc(sm.disp, 1)

                def gate_up(sm, g, j, e1, wa, wb):
                    pe.wait_ge(sm.hid, e1 + 1)
                    for k in range(KD):
                        for m, w in enumerate((wa, wb)):
                            ins = pe.matmul(B5[64 * m:64 * m + 64, :], xgT[:, g, k, CH * j:CH * j + CH], w[:, k, :],
                                            start=(k == 0), stop=(k == KD - 1))
                    ins.then_inc(sm.ab, 1)

                def hidden_transposed(sm, q, e1):
                    pe.wait_ge(sm.hid, e1 + 2)
                    for k in range(KF):
                        ins = pe.transpose(B6[:, P * k:P * k + P], hid[:, q % 2, P * k:P * k + P], ident)
                    ins.then_inc(sm.hidT_ps, 1)

                def down(sm, q, e1, w):
                    pe.wait_ge(sm.y_lo, e1 + 1)
                    pe.wait_ge(sm.y_hi, e1 + 1)
                    pe.wait_ge(sm.hidT, e1 + 1)
                    for k in range(KF):
                        for m in range(2):
                            ins = pe.matmul(B7[64 * m:64 * m + 64, :], hidTb[:, q % 2, k, :],
                                            w[:, k, 512 * m:512 * m + 512], start=(k == 0), stop=(k == KF - 1))
                    ins.then_inc(sm.y, 1)

                def combine(sm, g, q, e1):
                    pe.wait_ge(sm.y_lo, e1 + 2)
                    pe.wait_ge(sm.y_hi, e1 + 2)
                    pr = q // 2
                    for f in range(KD):
                        ins = pe.matmul(A4[:, f // 2, TOK * (f % 2):TOK * (f % 2) + TOK],
                                        y2[:, pr % 2, P * f:P * f + P], SwT[:, g, pr % 2, :],
                                        start=False, stop=False, skip_group_check=True)
                    ins.then_inc(sm.comb, 1)

                pe.wait_ge(tr_ev, U[f"h{l}_3"] + 1)
                for part in range(NP5):
                    dispatch(main, 0, part, sbase + 1, dbase + part)
                with pe.Fori(0, TURNS) as i:
                    for g in range(2):
                        for j in range(GE):
                            q = GE * g + j
                            n = N_MOE[l] + 3 * q
                            e1 = i * (2 * GE) + (ebase + q)
                            gi = i * 2 + g
                            fill = i * (16 * (6 * GE // (RING - 2 if l == 0 else RING)))

                            def ahead(part):
                                dispatch(main, 1 - g, part, gi + (sbase + 2), gi * NP5 + (dbase + NP5 + part))

                            if j == 0:
                                pe.wait_ge(main.disp_ev, gi * NP5 + (dbase + NP5 + 1))
                            pe.wait_ge(slot_full[slot(n)], fill + fills(n))
                            pe.wait_ge(slot_full[slot(n + 1)], fill + fills(n + 1))
                            gate_up(main, g, j, e1, slot8(n), slot8(n + 1))
                            ahead(j)
                            hidden_transposed(main, q, e1)
                            if j == 3:
                                ahead(4)
                            pe.wait_ge(slot_full[slot(n + 2)], fill + fills(n + 2))
                            down(main, q, e1, slot4(n + 2))
                            if j % 2 == 1:
                                combine(main, g, q, e1)

                def more_experts(gb, i):
                    sm = more[l]
                    for part in range(NP5):
                        dispatch(sm, 0, part, gb + 1, gb * NP5 + part)
                    pe.wait_ge(sm.disp_ev, gb * NP5 + (NP5 + 1))
                    for j in range(GE):
                        e1 = gb * GE + j
                        pe.wait_ge(more_full[l][0], e1 * 16 + 16)
                        pe.wait_ge(more_full[l][1], e1 * 16 + 16)
                        gate_up(sm, 0, j, e1, slot8(0), slot8(1))
                        hidden_transposed(sm, j, e1)
                        pe.wait_ge(more_full[l][2], e1 * 16 + 16)
                        down(sm, j, e1, slot4(2))
                        if j % 2 == 1:
                            combine(sm, 0, j, e1)

                more_chunks(pe, l, more_experts)

            for sm in (main, *more):
                pe.nop().then_inc(sm.y, 1)
            pe.wait_ge(in_cst, 16)
            tr_unit("lam", [s5row[:, :]], [(in_s5, 16 * N_S5)])
            for t in range(TT):
                for h in range(2):
                    tr_unit(f"x{2 * t + h}", [htok[:, t, 512 * h + P * b:512 * h + P * b + P] for b in range(4)], [(in_x, 16)])
            pe.wait_ge(c_ready, 1)
            ada_rows(0, 0)
            ada_columns(0, 0)
            for v in range(2):
                tr_unit(f"bt{v}", [Bd[:, v, 4 * q4:4 * q4 + 4, :].rearrange("p a b -> p (a b)") for q4 in range(4)], [(p5_bt, 1)])
            for v in range(2):
                tr_unit(f"ct{v}", [Cd[:, v, q4, :] for q4 in range(4)])
            sum_squares(0)
            pe.wait_ge(h_ready, 1)
            for q, ch in enumerate(IN0_ORDER):
                project(0, q, ch, n_of(0, "in", q), TT * q)
                if q == 1:
                    ada_rows(0, 1)
                if q == 2:
                    ada_columns(0, 1)
                if q == 3:
                    for t in range(TT):
                        tr_unit(f"idx{t}", [z0[:, t, 3072:3200], z0[:, t, 3200:3328], ikrep[:, t, :]], [(qk_ready, t + 1)])
                    ada_rows(0, 2)
                if q == 4:
                    ada_columns(0, 2)
                    for t in range(TT):
                        for h in range(2):
                            tr_unit(f"B{2 * t + h}", [z0[:, t, 1536 + 512 * h + P * b:1536 + 512 * h + P * b + P] for b in range(4)],
                                    [(qk_ready, 3 + t)])
            pe.wait_ge(z_ready, 14)
            for t in range(TT):
                if t:
                    pe.wait_ge(idx_relu, 2)
                for half in range(2):
                    w = P * (t + 1)
                    for m in range(4):
                        ins = pe.matmul(A4[:, m, TOK * half:TOK * half + w], idxT[32 * m:32 * m + 32, half, P * t:P * t + P],
                                        idxT[32 * m:32 * m + 32, 2, 0:w], start=True, stop=True)
                ins.then_inc(idx_s, 1)
            for t in range(TT):
                for h in range(2):
                    tr_unit(f"A{2 * t + h}", [z0[:, t, 512 * h + P * b:512 * h + P * b + P] for b in range(4)], [(qk_ready, 5 + t)])
            pe.wait_ge(idx_relu, 4)
            pe.wait_ge(tr_ev, U["A3"] + 1)

            def ada1(j):
                if j in ADA1_AT:
                    (ada_rows if ADA1_AT[j][0] == "r" else ada_columns)(1, int(ADA1_AT[j][1]))

            attention(0, 0, L0_UNITS, ada1)
            for t in range(TT):
                for h in range(2):
                    tr_unit(f"o{2 * t + h}", [htok[:, t, 512 * h + P * b:512 * h + P * b + P] for b in range(4)],
                            [(o_ready, 3 + t)])
            pe.wait_ge(tr_ev, U["o3"] + 1)
            out_proj(0)
            sum_squares(1)
            moe(0)
            sum_squares(2)
            pe.wait_ge(h_ready, 3)
            pe.wait_ge(x_upd, 2)
            PD = 14

            def s5_input(q4):
                if q4:
                    pe.wait_ge(bu_read, q4)
                for v in range(2):
                    for jj in range(4):
                        ins = pe.matmul(A4[:, jj, TOK * v:TOK * v + TOK],
                                        BT[32 * jj:32 * jj + 32, v, q4, :], uT[32 * jj:32 * jj + 32, q4, :],
                                        start=True, stop=True)
                ins.then_inc(bu_done, 1)

            def s5_output(q4):
                if q4:
                    pe.wait_ge(y5_read, q4)
                for half in range(2):
                    src = (mm, vv)[half]
                    pe.wait_ge(prod_ready, 2 * q4 + half + 1)
                    for v in range(2):
                        for jj in range(4):
                            which = (0, 1)[v] if half == 0 else 2
                            ins = pe.matmul(B4[32 * jj:32 * jj + 32, 0:TOK], CT[:, which, q4, 32 * jj:32 * jj + 32],
                                            src[:, v, jj, :], start=(half == 0 and v == 0), stop=(half == 1 and v == 1),
                                            skip_group_check=True)
                    ins.then_inc(y5_done, 1)

            for q, ch in enumerate(IN1_ORDER):
                n = n_of(1, "in", q)
                if ch != 3:
                    project(1, q, ch, n, PD, between=lambda: s5_input(q))
                    PD += 2
                    s5_output(q - 1)
                else:
                    full(n)
                    for f in range(4):
                        pe.wait_ge(z_ready, PD)
                        for k in range(KD):
                            ins = pe.matmul(B5[:, 0:TOK], slot8(n)[:, k, P * f:P * f + P], hT[:, k, :],
                                            start=(k == 0), stop=(k == KD - 1))
                        ins.then_inc(proj_done, 1)
                        PD += 1
                    pe.wait_ge(proj_done, PD)
                    pe.nop().then_inc(slot_used, 1)
                    pe.wait_ge(z_ready, PD)
                    s5_input(0)
            s5_output(3)
            for t in range(TT):
                for h in range(2):
                    tr_unit(f"C{2 * t + h}", [z1[:, t, 512 * h + P * b:512 * h + P * b + P] for b in range(4)], [(qk_ready, 7 + t)])
            pe.wait_ge(gy_ready, 1)
            n = n_of(1, "glu")
            full(n)
            for f in range(4):
                for k in range(4):
                    ins = pe.matmul(A4[:, f // 2, TOK * (f % 2):TOK * (f % 2) + TOK], slot8(n)[:, k, P * f:P * f + P],
                                    gy[:, k, :], start=(k == 0), stop=(k == 3))
            ins.then_inc(slot_used, 1)
            pe.wait_ge(slot_used, used_after(n))
            pe.nop().then_inc(glu_done, 1)
            pe.wait_ge(yo_ready, 1)
            pe.wait_ge(tr_ev, U["C3"] + 1)
            attention(1, N0, L1_UNITS, lambda j: None)
            for t in range(TT):
                tr_unit(f"o{4 + t}", [htok[:, t, P * b:P * b + P] for b in range(4)], [(o_ready, 5 + t)])
            pe.wait_ge(tr_ev, U["o5"] + 1)
            out_proj(1)
            sum_squares(3)
            moe(1)
            pe.wait_ge(x_upd, 4)
            for t in range(TT):
                for h in range(2):
                    for b in range(4):
                        ins = pe.transpose(A4[:, 2 * t + h, P * b:P * b + P], xT[:, 4 * h + b, P * t:P * t + P], ident)
                    ins.then_inc(x_tr, 1)

        @block.vector
        def _(dve):
            count = [0]

            def link(ins):
                count[0] += 1
                ins.then_inc(s_dve, 1)
                dve.wait_ge(s_dve, count[0])

            def tt(out, a0, a1, op):
                link(dve.tensor_tensor(out, a0, a1, op))

            def ts(out, a0, s1, s2, o0, o1=ALU.bypass):
                link(dve.tensor_scalar(out, a0, s1, s2, o0, o1) if s2 is not None else dve.tensor_scalar(out, a0, s1, None, o0))

            def stt(out, a0, s, a1, o0, o1):
                link(dve.scalar_tensor_tensor(out, a0, s, a1, o0, o1))

            def tell(s, n=1):
                dve.nop().then_inc(s, n)

            roots = [0]

            def rsqrt(x):
                tell(ms_ready)
                roots[0] += 1
                dve.wait_ge(sq_root, roots[0])
                link(dve.reciprocal(x, x))

            def norm_modulate(q):
                l, w = q // 2, q % 2
                dve.wait_ge(tr_ev, U[f"ada{l}c{2 * w}"] + 1)
                ts(modp[:, q, :], modc[:, l, 24 * w + 8:24 * w + 16], 1.0, None, ALU.add)
                sq = htok[:, :, :].rearrange("p t (a b) -> p (t a) b", b=TOK)
                tt(sq, xT[:, :, :], xT[:, :, :], ALU.mult)
                tell(sq_ready)
                dve.wait_ge(ssq_done, q + 1)
                ts(rstd[:, :], B5[:, 0:TOK], 1.0 / D, EPS, ALU.mult, ALU.add)
                tell(var_ready)
                dve.wait_ge(sd_ready, q + 1)
                link(dve.reciprocal(rstd[:, :], rstd[:, :]))
                tt(hT[:, :, :], xT[:, :, :], rstd[:, :].unsqueeze(1).to_broadcast([P, KD, TOK]), ALU.mult)
                for k in range(KD):
                    ins = dve.tensor_scalar(hT[:, k, :], hT[:, k, :], modp[:, q, k:k + 1],
                                            modc[:, l, 24 * w + k:24 * w + k + 1], ALU.mult, ALU.add)
                link(ins)
                tell(h_ready)

            def rope(v, t, n, half, cn, sn, tmp):
                cc = C(cn).rearrange("p (t a) -> p t a", t=2)[:, t, :].unsqueeze(1).to_broadcast([P, n, 2 * half])
                ss = C(sn).rearrange("p (t a) -> p t a", t=2)[:, t, :].unsqueeze(1).to_broadcast([P, n, 2 * half])
                ta, tb = tmp[:, 0, 0:n, 0:2 * half], tmp[:, 1, 0:n, 0:2 * half]
                dve.tensor_tensor(ta, v[:, :, 0:2 * half], cc, ALU.mult)
                tt(tb, v[:, :, 0:2 * half], ss, ALU.mult)
                dve.tensor_tensor(v[:, :, 0:half], ta[:, :, 0:half], tb[:, :, half:2 * half], ALU.subtract)
                tt(v[:, :, half:2 * half], ta[:, :, half:2 * half], tb[:, :, 0:half], ALU.add)

            def norm_rope(v, t, gi, sq, tmp):
                tt(sq, v, v, ALU.mult)
                ms = small[:, 0:16]
                link(dve.tensor_reduce(ms, sq, AX, ALU.add))
                ts(ms, ms, 1.0 / HD, EPS, ALU.mult, ALU.add)
                rsqrt(ms)
                tt(v, v, ms.unsqueeze(2).to_broadcast([P, 16, HD]), ALU.mult)
                v4 = v.rearrange("p (q h) d -> p q h d", q=2)
                tt(v4, v4, gqk[:, gi, :, :].unsqueeze(2).to_broadcast([P, 2, 8, HD]), ALU.mult)
                rope(v, t, 16, 8, "rc", "rs", tmp)
                tell(qk_ready)

            def softmax_unit(base, j, s, b, t, buf, pr):
                u = base + j
                w = P * (t + 1)
                dve.wait_ge(score, u + 1)
                if u >= 2:
                    dve.wait_ge(expd, u - 1)
                src = A4[:, 2 * (u % 2):2 * (u % 2) + 2, 0:w]
                mask = selb[:, t, 0:w] if s == 1 else C("cb2")[:, 2 * P - w:2 * P]
                stt(buf[:, u % 2, :, 0:w], src, HD ** -0.5, mask.unsqueeze(1).to_broadcast([P, 2, w]), ALU.mult, ALU.add)
                tell(score_read)
                nm = small[:, 16 + 2 * (u % 4):18 + 2 * (u % 4)]
                link(dve.tensor_reduce(nm, buf[:, u % 2, :, 0:w], AX, ALU.max))
                ts(nm, nm, -1.0, None, ALU.mult)
                tell(negmax)

            def sums(u):
                return small[:, 32 + 2 * u:34 + 2 * u]

            def combine_unit(j, b, t):
                w = P * (t + 1)
                dve.wait_ge(expd, j + 1)
                su = sums(j)
                link(dve.reciprocal(su, su))
                tt(su[:, 1:2], su[:, 1:2], lamt[:, 4:5], ALU.mult)
                ts(prob[:, j % 2, 1, 0:w], prob[:, j % 2, 1, 0:w], su[:, 1:2], None, ALU.mult)
                stt(prob[:, j % 2, 0, 0:w], prob[:, j % 2, 0, 0:w], su[:, 0:1], prob[:, j % 2, 1, 0:w], ALU.mult, ALU.subtract)
                tell(attn_ready)

            def out_rows(base, t, s, pv, first):
                dve.wait_ge(pv_done, pv)
                su = small[:, 32 + 2 * (base + 4 * t):40 + 2 * (base + 4 * t)]
                link(dve.reciprocal(su, su))
                tt(htok[:, t, first:first + 512].rearrange("p (h d) -> p h d", h=8),
                   OB[t][:, :].rearrange("p (h d) -> p h d", h=8), su.unsqueeze(2).to_broadcast([P, 8, HD]), ALU.mult)
                tell(o_ready)

            def out_rows_a(t, pv):
                dve.wait_ge(pv_done, pv)
                o = htok[:, t, 0:512].rearrange("p (h d) -> p h d", h=4)
                link(dve.tensor_copy(o, OB[t][:, :].rearrange("p (h d) -> p h d", h=4)))
                sq = sc_sb[:, t % 2].rearrange("p a b -> p (a b)").rearrange("p (h d) -> p h d", h=4)
                tt(sq, o, o, ALU.mult)
                ms = small[:, 0:4]
                link(dve.tensor_reduce(ms, sq, AX, ALU.add))
                ts(ms, ms, 1.0 / (2 * HD), EPS, ALU.mult, ALU.add)
                rsqrt(ms)
                tt(o, o, ms.unsqueeze(2).to_broadcast([P, 4, 2 * HD]), ALU.mult)
                tt(o, o, subln[:, :].unsqueeze(1).to_broadcast([P, 4, 2 * HD]), ALU.mult)
                ts(o, o, 0.8, None, ALU.mult)
                tell(o_ready)

            def residual(l, w):
                for f in range(KD):
                    ins = dve.scalar_tensor_tensor(xT[:, f, :], A4[:, f // 2, TOK * (f % 2):TOK * (f % 2) + TOK],
                                                   modc[:, l, 24 * w + 16 + f:24 * w + 17 + f], xT[:, f, :], ALU.mult, ALU.add)
                link(ins)
                tell(x_upd)

            def route(l):
                M, lg, oh, dif, t1, t2, fine, oh2 = (rt[:, q] for q in range(8))
                dve.wait_ge(logit_done, l + 1)
                L = rt[:, 8:11].rearrange("p a t e -> p (a t e)")[:, 0:72].rearrange("p (t c) -> p t c", t=2)
                tt(L, B5[:, 0:72].rearrange("p (t c) -> p t c", t=2), bge[:, l, :].unsqueeze(1).to_broadcast([P, TT, 36]), ALU.add)
                co, fi = L[:, :, 0:NG], L[:, :, NG:]
                sc = rt[:, 12]
                mx, k1, m1, m2, den, w1, w2 = (sc[:, :, q:q + 1] for q in range(7))
                g4, e4 = sc[:, :, 8:12], sc[:, :, 12:16]
                link(dve.tensor_reduce(mx[:, :, 0], co, AX, ALU.max))
                tt(e4, co, mx.to_broadcast([P, TT, NG]), ALU.subtract)
                ts(g4, e4, 0.0, None, ALU.is_equal)
                tt(g4, g4, C("desc4").unsqueeze(1).to_broadcast([P, TT, NG]), ALU.mult)
                link(dve.tensor_reduce(k1[:, :, 0], g4, AX, ALU.max))
                tt(g4, g4, k1.to_broadcast([P, TT, NG]), ALU.is_equal)
                ts(g4, g4, BIG, -BIG, ALU.mult, ALU.add)
                f4 = fine.rearrange("p t (g e) -> p t g e", g=NG)
                tt(f4, fi.rearrange("p t (g e) -> p t g e", g=NG), g4.unsqueeze(3).to_broadcast([P, TT, NG, EPG]), ALU.add)

                def first_max(v, m, out):
                    link(dve.tensor_reduce(m[:, :, 0], v, AX, ALU.max))
                    tt(out, v, m.to_broadcast([P, TT, NE]), ALU.is_equal)
                    tt(out, out, C("desc32").unsqueeze(1).to_broadcast([P, TT, NE]), ALU.mult)
                    link(dve.tensor_reduce(k1[:, :, 0], out, AX, ALU.max))
                    tt(out, out, k1.to_broadcast([P, TT, NE]), ALU.is_equal)

                first_max(fine, m1, oh)
                stt(t1, oh, -3.0 * BIG, fine, ALU.mult, ALU.add)
                first_max(t1, m2, oh2)
                tt(M, oh, oh2, ALU.add)
                tell(mask_ready)
                tt(w2, m2, m1, ALU.subtract)
                tell(route_d)
                dve.wait_ge(route_e, l + 1)
                link(dve.tensor_reduce(den[:, :, 0], e4, AX, ALU.add))
                ts(w1, w2, 1.0, None, ALU.add)
                tt(den, den, w1, ALU.mult)
                link(dve.reciprocal(w1, den))
                tt(w2, w1, w2, ALU.mult)
                tt(oh, oh, w1.to_broadcast([P, TT, NE]), ALU.mult)
                tt(oh2, oh2, w2.to_broadcast([P, TT, NE]), ALU.mult)
                tt(wt[:, :, 0:NE], oh, oh2, ALU.add)
                dve.wait_ge(rank_done, l + 1)
                R = B5[:, 0:2 * NE].rearrange("p (t e) -> p t e", t=2)
                stt(rankm[:, :, 0:NE], R, 1.0, M, ALU.add, ALU.mult)
                ts(rankm[:, :, 0:NE], rankm[:, :, 0:NE], -1.0, None, ALU.add)
                n_tok, n_more = small[:, 250:251], small[:, 251:252]
                link(dve.tensor_reduce(n_tok, B5[:, 2 * NE:3 * NE], AX, ALU.max))
                ts(n_more, n_tok, CH + 0.5, None, ALU.is_ge)
                for q in range(2, MORE + 1):
                    stt(n_more, n_tok, q * CH + 0.5, n_more, ALU.is_ge, ALU.add)
                dve.tensor_copy(cnti[:, l:l + 1], n_more).then_inc(cnt_ready, 1)

            def moe(l):
                route(l)
                dbase, sbase, ebase, mbase = l * NP5 * (2 * GE + 1), l * (2 * GE + 2), l * NE, l * TT * (2 * GE + 2)

                def matrices(sm, col, g, made):
                    io = C("iota").unsqueeze(1).to_broadcast([P, GE, CH])
                    for t in range(TT):
                        r = rankm[:, t, bass.ds(col, GE)].unsqueeze(2).to_broadcast([P, GE, CH])
                        dve.tensor_tensor(Sd[:, g, t, :].rearrange("p (e s) -> p e s", e=GE), io, r, ALU.is_equal).then_inc(sm.mat, 1)
                    dve.wait_ge(sm.mat, made + TT)
                    for t in range(TT):
                        w = wt[:, t, bass.ds(col, GE)].unsqueeze(2).to_broadcast([P, GE, CH])
                        ins = dve.tensor_tensor(Sw[:, g, t, :].rearrange("p (e s) -> p e s", e=GE),
                                                Sd[:, g, t, :].rearrange("p (e s) -> p e s", e=GE), w, ALU.mult)
                    ins.then_inc(sm.ready, 1)

                def copy_dispatched(sm, g, part, before):
                    dve.wait_ge(sm.disp, before + 1)
                    dst = xgT[:, g, 2 * part:2 * part + 2, :] if part < 4 else SwT[:, g, :, :]
                    dve.tensor_copy(dst, B4[:, :].rearrange("p (a b) -> p a b", a=2)).then_inc(sm.disp_ev, 1)

                def gated(sm, q, e1):
                    dve.wait_ge(sm.silu, e1 + 1)
                    dve.tensor_tensor(hid[64:128, q % 2, :], silu_a[64:128, q % 2, :], B5[64:128, :],
                                      ALU.mult).then_inc(sm.hid, 1)

                def copy_y(sm, q, e1):
                    dve.wait_ge(sm.y, e1 + 2)
                    dve.tensor_copy(y2[64 * (q % 2):64 * (q % 2) + 64, (q // 2) % 2, 0:512], B7[0:64, :]).then_inc(sm.y_lo, 1)

                for g in range(2):
                    matrices(main, GE * g, g, mbase + TT * g)
                link(dve.memset(hid[0:64, :, :], 0.0))
                for part in range(NP5):
                    copy_dispatched(main, 0, part, dbase + part)
                with dve.Fori(0, TURNS) as i:
                    for g in range(2):
                        gi = i * 2 + g
                        dve.wait_ge(main.disp, gi * NP5 + (dbase + NP5))
                        matrices(main, gi * GE + 2 * GE, g, gi * TT + (mbase + 2 * TT))
                        for j in range(GE):
                            q = GE * g + j
                            e1 = i * (2 * GE) + (ebase + q)
                            gated(main, q, e1)
                            copy_dispatched(main, 1 - g, j, gi * NP5 + (dbase + NP5 + j))
                            if j == 3:
                                copy_dispatched(main, 1 - g, 4, gi * NP5 + (dbase + NP5 + 4))
                            copy_y(main, q, e1)

                def more_experts(gb, i):
                    sm = more[l]
                    matrices(sm, i * GE, 0, gb * TT)
                    for part in range(NP5):
                        copy_dispatched(sm, 0, part, gb * NP5 + part)
                    for j in range(GE):
                        e1 = gb * GE + j
                        gated(sm, j, e1)
                        copy_y(sm, j, e1)

                def lower_ranks(c):
                    dve.tensor_scalar(rankm[:, :, :], rankm[:, :, :], float(CH), None, ALU.subtract).then_inc(ranks_down[l], 1)
                    dve.wait_ge(ranks_down[l], c + 1)
                    dve.sem_inc(more_over, 1)

                def all_combined(c):
                    dve.wait_ge(more[l].comb, (c + 1) * (NE // 2))
                    dve.sem_inc(more_over, 1)

                dve.wait_ge(main.disp, dbase + NP5 * (2 * GE + 1))
                dve.wait_ge(main.comb, (l + 1) * (NE // 2))
                more_chunks(dve, l, more_experts, before=lower_ranks, after=all_combined)
                residual(l, 1)

            dve.memset(brow[:, :], 0.0).then_inc(brow_zero, 1)
            for sm in (main, *more):
                for s in (sm.disp_ev, sm.hid, sm.y_lo):
                    tell(s)
            dve.wait_ge(in_cst, 16)
            dve.memset(rankm[:, :, NE:], -1.0)
            dve.memset(wt[:, :, NE:], 0.0)
            dve.wait_ge(c_exp, 1)
            ts(ctmp[:, 0, :], ctmp[:, 0, :], 1.0, None, ALU.add)
            link(dve.reciprocal(ctmp[:, 0, :], ctmp[:, 0, :]))
            tt(ctmp[:, 0, :], ctmp[:, 0, :], ccol[:, :], ALU.mult)
            link(dve.tensor_copy(crep[:, :, :], ctmp[:, 0, :].unsqueeze(2).to_broadcast([P, KD, 32])))
            tell(c_ready)
            dve.wait_ge(in_par, 16 * N_PAR)
            lp = small[:, 64:192].rearrange("p (a b) -> p a b", a=2)
            tt(lp, lrow[:, 0:4:2, :], lrow[:, 1:4:2, :], ALU.mult)
            link(dve.tensor_reduce(lamt[:, 0:2], lp, AX, ALU.add))
            tell(lam_s)
            dve.wait_ge(lam_e, 1)
            tt(lamt[:, 4:5], lamt[:, 2:3], lamt[:, 3:4], ALU.subtract)
            ts(lamt[:, 4:5], lamt[:, 4:5], 0.2, None, ALU.add)
            def q(n):
                return s5p[:, n, :]

            LRE, LIM, DT, TH, ARG, MAG, K, TURN, TC, SN, CS, ABR, ABI, DEN, CRE, CIM, T1, T2 = range(18)
            dve.wait_ge(in_s5, 16 * N_S5)
            dve.wait_ge(tr_ev, U["lam"] + 1)
            dve.wait_ge(p5_dt, 1)
            tt(q(TH), q(LIM), q(DT), ALU.mult)
            tt(q(ARG), q(LRE), q(DT), ALU.mult)
            ts(q(K), q(TH), 1.0 / TWO_PI, None, ALU.mult)
            ts(q(K), q(K), MAGIC, None, ALU.add)
            ts(q(K), q(K), -MAGIC, None, ALU.add)
            stt(q(TURN), q(K), -C1, q(TH), ALU.mult, ALU.add)
            stt(q(TURN), q(K), -C2, q(TURN), ALU.mult, ALU.add)
            ts(q(TURN), q(TURN), 1.0 / TWO_PI, None, ALU.mult)
            ts(q(TC), q(TURN), 0.25, None, ALU.add)
            for x in (TURN, TC):
                y = T1
                ts(q(T1), q(x), MAGIC, None, ALU.add)
                ts(q(T1), q(T1), -MAGIC, None, ALU.add)
                tt(q(x), q(x), q(T1), ALU.subtract)
            tell(p5_arg)
            dve.wait_ge(p5_sc, 1)
            tt(q(ABR), q(MAG), q(CS), ALU.mult)
            tt(q(ABI), q(MAG), q(SN), ALU.mult)
            ts(q(ABR), q(ABR), -1.0, None, ALU.add)
            tt(q(T1), q(LRE), q(LRE), ALU.mult)
            tt(q(T2), q(LIM), q(LIM), ALU.mult)
            tt(q(DEN), q(T1), q(T2), ALU.add)
            link(dve.reciprocal(q(DEN), q(DEN)))
            tt(q(T1), q(ABR), q(LRE), ALU.mult)
            tt(q(T2), q(ABI), q(LIM), ALU.mult)
            tt(q(CRE), q(T1), q(T2), ALU.add)
            tt(q(CRE), q(CRE), q(DEN), ALU.mult)
            tt(q(T1), q(ABI), q(LRE), ALU.mult)
            tt(q(T2), q(ABR), q(LIM), ALU.mult)
            tt(q(CIM), q(T1), q(T2), ALU.subtract)
            tt(q(CIM), q(CIM), q(DEN), ALU.mult)
            cre = q(CRE).unsqueeze(2).to_broadcast([P, 16, 16])
            cim = q(CIM).unsqueeze(2).to_broadcast([P, 16, 16])
            tt(Bbar[:, 0], s5b[:, 0], cre, ALU.mult)
            tt(Btmp, s5b[:, 1], cim, ALU.mult)
            tt(Bbar[:, 0], Bbar[:, 0], Btmp, ALU.subtract)
            tt(Bbar[:, 1], s5b[:, 1], cre, ALU.mult)
            tt(Btmp, s5b[:, 0], cim, ALU.mult)
            tt(Bbar[:, 1], Bbar[:, 1], Btmp, ALU.add)
            link(dve.memset(Bd, 0.0))
            for v in range(2):
                for gp in range(2):
                    link(dve.tensor_copy(Bd[64 * gp:64 * gp + 64, v, :, 16 * gp:16 * gp + 16], Bbar[64 * gp:64 * gp + 64, v]))
                for gp in range(2):
                    ts(Cd[:, v, :, 64 * gp:64 * gp + 64], s5c[:, v], C("par")[:, gp:gp + 1], (1.0, -1.0)[v], ALU.mult, ALU.mult)
            tell(p5_bt)
            dve.wait_ge(tr_ev, U["x3"] + 1)
            norm_modulate(0)
            dve.wait_ge(tr_ev, U["ct1"] + 1)
            link(dve.tensor_scalar(CT[:, 1], CT[:, 0], -1.0, None, ALU.mult))
            for t in range(TT):
                dve.wait_ge(z_ready, t + 1)
                iq = z0[:, t, 3072:3328].rearrange("p (h d) -> p h d", h=8)
                ik = z0[:, t, 3328:3360]
                tt(sqs[:, 0, 0:32], ik, ik, ALU.mult)
                ms = small[:, 0:1]
                link(dve.tensor_reduce(ms, sqs[:, 0, 0:32], AX, ALU.add))
                ts(ms, ms, 1.0 / 32, EPS, ALU.mult, ALU.add)
                rsqrt(ms)
                stt(ik, ik, ms, gidx[:, :], ALU.mult, ALU.mult)
                rope(iq, t, 8, 4, "ic", "is", tmp16)
                rope(ik.unsqueeze(1), t, 1, 4, "ic", "is", tmp16)
                link(dve.tensor_copy(ikrep[:, t, :].rearrange("p (r d) -> p r d", r=4), ik.unsqueeze(1).to_broadcast([P, 4, 32])))
                tell(qk_ready)
            for s, zr, col in ((1, 6, 1536), (0, 10, 0)):
                for t in range(TT):
                    dve.wait_ge(z_ready, zr - 1 + t)
                    norm_rope(z0[:, t, col:col + SETW].rearrange("p (h d) -> p h d", h=16), t, s, sqs, tmp16)
            dve.wait_ge(z_ready, 14)
            for t in range(TT):
                w = P * (t + 1)
                acc = idx_acc[:, 0:w]
                for u in range(2 * t, 2 * t + 2):
                    dve.wait_ge(idx_relu, u + 1)
                    for m in range(4):
                        h = 4 * (u % 2) + m
                        prev = C("cb2")[:, 2 * P - w:2 * P] if h == 0 else acc
                        stt(acc, relu_sb[u % 2][:, m, 0:w], z0[:, t, 3360 + h:3361 + h], prev, ALU.mult, ALU.add)
                    tell(idx_acc_s)
                m8 = small[:, 240:248]
                for _ in range(TOPK // 8):
                    link(dve.max(m8, acc))
                    link(dve.match_replace(acc, m8, acc, SENT))
                ts(selb[:, t, 0:w], acc, SENT, -BIG, ALU.not_equal, ALU.mult)
                tt(selb[:, t, 0:w], selb[:, t, 0:w], C("cb2")[:, 2 * P - w:2 * P], ALU.add)
            units = L0_UNITS
            for j in range(N0 + 1):
                if j < N0:
                    softmax_unit(0, j, *units[j], sc_sb, prob)
                if j - 1 >= 8:
                    combine_unit(j - 1, *units[j - 1][1:])
                if j in (3 + LAG_PV, 7 + LAG_PV):
                    out_rows(0, (j - 3 - LAG_PV) // 4, 1, j - LAG_PV + 1, 512)
            out_rows_a(0, 12)
            out_rows_a(1, 16)
            dve.wait_ge(wout_done, 1)
            residual(0, 0)
            norm_modulate(1)
            moe(0)
            norm_modulate(2)

            def s5_quad(q4):
                dve.wait_ge(bu_done, q4 + 1)
                cs, sn = tabs[:, 0, 4 * q4:4 * q4 + 4, :], tabs[:, 1, 4 * q4:4 * q4 + 4, :]
                bur, bui = A4[:, :, 0:TOK], A4[:, :, TOK:2 * TOK]
                if q4:
                    dve.wait_ge(y5_done, 2 * q4 - 1)
                dve.tensor_tensor(mm[:, 0], cs, bur, ALU.mult)
                tt(mm[:, 1], sn, bui, ALU.mult)
                if q4:
                    dve.wait_ge(y5_done, 2 * q4)
                tt(vv[:, 0], mm[:, 0], mm[:, 1], ALU.add)
                dve.tensor_tensor(mm[:, 0], cs, bui, ALU.mult)
                dve.tensor_tensor(mm[:, 1], sn, bur, ALU.mult).then_inc(bu_read, 1)
                dve.wait_ge(bu_read, q4 + 1)
                tt(vv[:, 1], mm[:, 0], mm[:, 1], ALU.subtract)
                for v in range(2):
                    for jj in range(4):
                        mg = s5p[:, MAG, 4 * q4 + jj:4 * q4 + jj + 1].to_broadcast([P, TOK])
                        ins = dve.tensor_tensor_scan(vv[:, v, jj, :], mg, vv[:, v, jj, :], 0.0, ALU.mult, ALU.add)
                link(ins)
                dve.tensor_tensor(mm[:, 0], cs, vv[:, 0], ALU.mult)
                dve.tensor_tensor(mm[:, 1], sn, vv[:, 1], ALU.mult).then_inc(prod_ready, 1)
                dve.wait_ge(prod_ready, 2 * q4 + 1)
                dve.tensor_tensor(vv[:, 0], sn, vv[:, 0], ALU.mult)
                dve.tensor_tensor(vv[:, 1], cs, vv[:, 1], ALU.mult).then_inc(prod_ready, 1)

            def s5_rows(q4):
                dve.wait_ge(y5_done, 2 * q4 + 2)
                ins = dve.scalar_tensor_tensor(y5[:, q4, :], uT[:, q4, :], s5d[:, q4:q4 + 1], B4[:, 0:TOK], ALU.mult, ALU.add)
                ins.then_inc(y5_read, 1)

            dve.wait_ge(tab_done, 2 * 16 // 2 + 1)
            for q4 in range(4):
                s5_quad(q4)
                if q4:
                    s5_rows(q4 - 1)
                if q4 >= 2:
                    t = q4 - 2
                    dve.wait_ge(z_ready, 21 + t)
                    norm_rope(z1[:, t, 0:SETW].rearrange("p (h d) -> p h d", h=16), t, 2, sqs1, tmp16_1)
            s5_rows(3)
            dve.wait_ge(y5_read, 4)
            w0 = vv[:, 0]
            tt(w0, y5, y5, ALU.mult)
            ts(w0, w0, 0.044715, 1.0, ALU.mult, ALU.add)
            tt(w0, w0, y5, ALU.mult)
            tell(tanh_in)
            dve.wait_ge(tanh_out, 1)
            ts(w0, w0, 0.5, 0.5, ALU.mult, ALU.add)
            tt(gy, w0, y5, ALU.mult)
            tell(gy_ready)
            dve.wait_ge(sig_ready, 1)
            tt(hT[:, 4:8, :], gy, vv[:, 1], ALU.mult)
            tell(yo_ready)
            for j, (s, b, t) in enumerate(L1_UNITS):
                softmax_unit(16, j, s, b, t, sc_sb1, prob1)
            out_rows(16, 0, 2, 20, 0)
            out_rows(16, 1, 2, 24, 0)
            dve.wait_ge(wout_done, 2)
            residual(1, 0)
            norm_modulate(3)
            moe(1)
            for t in range(TT):
                for h in range(2):
                    dve.wait_ge(x_tr, 2 * t + h + 1)
                    dve.tensor_copy(htok[:, t, 512 * h:512 * h + 512], A4[:, 2 * t + h, :]).then_inc(x_ev, 1)

        @block.scalar
        def _(act):
            count = [0]

            def link(ins):
                count[0] += 1
                ins.then_inc(s_act, 1)
                act.wait_ge(s_act, count[0])

            act.nop().then_inc(tab_done, 1)
            for sm in (main, *more):
                act.nop().then_inc(sm.y_hi, 1)
            act.dma_start(cst[:, :], cst_d).then_inc(in_cst, 16)
            act.dma_start(htok[:, :, :], a["x"][0].rearrange("(t p) d -> p t d", p=P)).then_inc(in_x, 16)
            act.dma_start(ccol[:, :], a["c"][0].rearrange("(k p) -> p k", p=P), allow_slow_non_contiguous=True).then_inc(in_c, 16)
            act.wait_ge(brow_zero, 1)
            act.dma_start(brow[0:12 * LAYERS, :], a["ada_b"].rearrange("l (q n) -> (l q) n", q=12)).then_inc(in_brow, 16)
            for dst, src, slow in S5_PARAMS:
                act.dma_start(dst, src, allow_slow_non_contiguous=slow).then_inc(in_s5, 16)
            for dst, src, slow in PARAMS:
                act.dma_start(dst, src, allow_slow_non_contiguous=slow).then_inc(in_par, 16)
            act.wait_ge(in_c, 16)
            act.activation(ctmp[:, 0, :], ccol[:, :], ACT.Exp, scale=-1.0).then_inc(c_exp, 1)
            passes = [0]

            def passed(name):
                u = passes[0]
                assert ORDER[u] == name, (ORDER[u], name)
                passes[0] += 1
                act.wait_ge(tr_done, u + 1)
                return TRB[u % 2]

            def tr_evac(name, dst, nb):
                src = passed(name)[:, 0:P * nb].rearrange("p (a b) -> p a b", a=nb)
                act.copy(dst, src).then_inc(tr_ev, 1)

            def ada_evac(l, what):
                if what[0] == "r":
                    act.copy(modrow[:, :], passed(f"ada{l}{what}")[:, :]).then_inc(tr_ev, 1)
                else:
                    r = int(what[1])
                    act.copy(modc[:, l, 16 * r:16 * r + 16].rearrange("p (g b) -> p g b", g=4),
                             passed(f"ada{l}{what}")[:, :].rearrange("p (b g x) -> p g b x", b=4, g=4)[:, :, :, 0]).then_inc(tr_ev, 1)

            def root(n, x):
                act.wait_ge(ms_ready, n)
                act.activation(x, x, ACT.Sqrt).then_inc(sq_root, 1)

            def norm_root(q):
                act.wait_ge(var_ready, q + 1)
                act.activation(rstd[:, :], rstd[:, :], ACT.Sqrt).then_inc(sd_ready, 1)

            def att_exp(base, j, s, b, t, buf, pr):
                u = base + j
                w = P * (t + 1)
                act.wait_ge(negmax, u + 1)
                if j >= 2:
                    act.wait_ge(tr_done, U[f"p{u - 2}"] + 1)
                for m in range(2):
                    ins = act.activation(pr[:, u % 2, m, 0:w], buf[:, u % 2, m, 0:w], ACT.Exp,
                                         bias=small[:, 16 + 2 * (u % 4) + m:17 + 2 * (u % 4) + m],
                                         accum_out=small[:, 32 + 2 * u + m:33 + 2 * u + m])
                ins.then_inc(expd, 1)

            def att_pt(base, j, s, b, t, pt):
                if j >= 2:
                    act.wait_ge(pv_done, base + j - 1)
                nb = n_maps(s) * (t + 1)
                tr_evac(f"p{base + j}", pt[:, (base + j) % 2, 0:nb, :], nb)

            def attention(base, units, buf, pr, pt, hook):
                n = len(units)
                for j in range(n + LAG_PT):
                    if 0 <= j - 1 < n:
                        att_exp(base, j - 1, *units[j - 1], buf, pr)
                    if 0 <= j - LAG_PT:
                        att_pt(base, j - LAG_PT, *units[j - LAG_PT], pt)
                    hook(j)

            def moe(l):
                for t in range(TT):
                    for h in range(2):
                        tr_evac(f"h{l}_{2 * t + h}", htok[:, t, 512 * h:512 * h + 512].rearrange("p (a b) -> p a b", a=4), 4)
                act.wait_ge(route_d, l + 1)
                link(act.activation(rt[:, 12, :, 12:16], rt[:, 12, :, 12:16], ACT.Exp))
                act.activation(rt[:, 12, :, 6:7], rt[:, 12, :, 6:7], ACT.Exp).then_inc(route_e, 1)
                ebase = l * NE

                def silu(sm, q, e1):
                    act.wait_ge(sm.ab, e1 + 1)
                    act.activation(silu_a[64:128, q % 2, :], B5[0:64, :], ACT.Silu).then_inc(sm.silu, 1)

                def copy_hidT(sm, q, e1):
                    act.wait_ge(sm.hidT_ps, e1 + 1)
                    act.copy(hidTb[:, q % 2, :, :], B6[:, :].rearrange("p (a b) -> p a b", a=KF)[:, :, P - CH:]).then_inc(sm.hidT, 1)

                def copy_y(sm, q, e1):
                    act.wait_ge(sm.y, e1 + 2)
                    act.copy(y2[64 * (q % 2):64 * (q % 2) + 64, (q // 2) % 2, 512:1024], B7[64:128, :]).then_inc(sm.y_hi, 1)

                if l == 0:
                    act.wait_ge(slot_used, used_after(n_of(0, "out", 1)))
                with act.Fori(0, TURNS) as i:
                    for q in range(2 * GE):
                        e1 = i * (2 * GE) + (ebase + q)
                        silu(main, q, e1)
                        copy_hidT(main, q, e1)
                        copy_y(main, q, e1)
                        if l == 0 and q % 2 == 1:
                            u, v = q // 4, q // 2 % 2
                            act.wait_ge(ph_ready, i * 4 + (2 * u + v + 1))
                            act.activation(tabs[:, v, bass.ds(i * 4 + 2 * u, 2), :], ph[:, v], ACT.Sin,
                                           scale=SIN_SCALE).then_inc(tab_done, 1)

                def more_experts(gb, i):
                    for j in range(GE):
                        e1 = gb * GE + j
                        silu(more[l], j, e1)
                        copy_hidT(more[l], j, e1)
                        copy_y(more[l], j, e1)

                act.wait_ge(main.comb, (l + 1) * (NE // 2))
                more_chunks(act, l, more_experts)

            act.copy(s5p[:, 0:2, :], passed("lam")[:, 0:32].rearrange("p (a b) -> p a b", a=2)).then_inc(tr_ev, 1)
            act.activation(s5p[:, 2, :], logdt[:, :], ACT.Exp).then_inc(p5_dt, 1)
            for t in range(TT):
                for h in range(2):
                    tr_evac(f"x{2 * t + h}", xT[:, 4 * h:4 * h + 4, P * t:P * t + P], 4)
            act.wait_ge(lam_s, 1)
            act.activation(lamt[:, 2:4], lamt[:, 0:2], ACT.Exp).then_inc(lam_e, 1)
            act.wait_ge(p5_arg, 1)
            act.activation(s5p[:, 5, :], s5p[:, 4, :], ACT.Exp)
            act.activation(s5p[:, 9, :], s5p[:, 7, :], ACT.Sin, scale=SIN_SCALE)
            act.activation(s5p[:, 10, :], s5p[:, 8, :], ACT.Sin, scale=SIN_SCALE).then_inc(p5_sc, 1)
            ada_evac(0, "r0")
            ada_evac(0, "c0")
            for v in range(2):
                tr_evac(f"bt{v}", BT[:, v], 4)
            for v in range(2):
                tr_evac(f"ct{v}", CT[:, 2 * v], 4)
            norm_root(0)

            def z_evac(q, t):
                ch = IN0_ORDER[q]
                w = min(512, EV_IN - 512 * ch)
                act.wait_ge(proj_done, TT * q + t + 1)
                act.copy(z0[:, t, 512 * ch:512 * ch + w], A4[:, (TT * q + t) % 4, 0:w]).then_inc(z_ready, 1)

            for q in range(7):
                for t in range(TT):
                    z_evac(q, t)
                if q == 1:
                    root(1, small[:, 0:1])
                    root(2, small[:, 0:1])
                    ada_evac(0, "r1")
                if q == 2:
                    ada_evac(0, "c1")
                if q == 3:
                    for t in range(TT):
                        tr_evac(f"idx{t}", idxT[:, :, P * t:P * t + P], 3)
                    root(3, small[:, 0:16])
                    root(4, small[:, 0:16])
                    ada_evac(0, "r2")
                if q == 4:
                    ada_evac(0, "c2")
                    for t in range(TT):
                        for h in range(2):
                            tr_evac(f"B{2 * t + h}", qkT0[:, 8 + 4 * h:12 + 4 * h, P * t:P * t + P], 4)
                if q >= 5:
                    root(q, small[:, 0:16])
            for u in range(4):
                t, half, w = u // 2, u % 2, P * (u // 2 + 1)
                act.wait_ge(idx_s, t + 1)
                if u >= 2:
                    act.wait_ge(idx_acc_s, u - 1)
                act.activation(relu_sb[u % 2][:, :, 0:w], A4[:, :, TOK * half:TOK * half + w], ACT.Relu).then_inc(idx_relu, 1)
            for t in range(TT):
                for h in range(2):
                    tr_evac(f"A{2 * t + h}", qkT0[:, 4 * h:4 * h + 4, P * t:P * t + P], 4)

            def ada1(j):
                if j in ADA1_AT:
                    ada_evac(1, ADA1_AT[j])

            attention(0, L0_UNITS, sc_sb, prob, PT, ada1)
            root(7, small[:, 0:4])
            root(8, small[:, 0:4])
            for t in range(TT):
                for h in range(2):
                    tr_evac(f"o{2 * t + h}", hT[:, 4 * h:4 * h + 4, P * t:P * t + P], 4)
            norm_root(1)
            moe(0)
            norm_root(2)
            pd = 14
            for ch in IN1_ORDER:
                for t in range(4 if ch == 3 else TT):
                    act.wait_ge(proj_done, pd + 1)
                    if ch == 3:
                        act.copy(uT[:, t, :], B5[:, 0:TOK]).then_inc(z_ready, 1)
                    else:
                        act.copy(z1[:, t, 512 * ch:512 * ch + 512], B5[:, :]).then_inc(z_ready, 1)
                    pd += 1
            root(9, small[:, 0:16])
            root(10, small[:, 0:16])
            for t in range(TT):
                for h in range(2):
                    tr_evac(f"C{2 * t + h}", qkT1[:, 4 * h:4 * h + 4, P * t:P * t + P], 4)
            act.wait_ge(tanh_in, 1)
            act.activation(vv[:, 0], vv[:, 0], ACT.Tanh, scale=GELU_C).then_inc(tanh_out, 1)
            act.wait_ge(glu_done, 1)
            for f in range(4):
                ins = act.activation(vv[:, 1, f, :], A4[:, f // 2, TOK * (f % 2):TOK * (f % 2) + TOK], ACT.Sigmoid, bias=glub[:, f:f + 1])
            ins.then_inc(sig_ready, 1)
            attention(N0, L1_UNITS, sc_sb1, prob1, PT1, lambda j: None)
            for t in range(TT):
                tr_evac(f"o{4 + t}", hT[:, 0:4, P * t:P * t + P], 4)
            norm_root(3)
            moe(1)
            for t in range(TT):
                act.wait_ge(x_ev, 2 * (t + 1))
                act.dma_start(out_d[0, P * t:P * t + P, :], htok[:, t, :]).then_inc(out_s, 16)
            act.wait_ge(out_s, 32)

        @block.gpsimd
        def _(pool):
            count = [0]

            def link(ins):
                count[0] += 1
                ins.then_inc(s_pool, 1)
                pool.wait_ge(s_pool, count[0])

            TURN = 7
            pool.wait_ge(x_upd, 1)
            time = C("time").unsqueeze(1).to_broadcast([P, 2, TOK])
            K = 7
            with pool.Fori(0, TURNS) as i:
                for u in range(2):
                    pool.wait_ge(tab_done, i * 4 + (2 * u + 1))
                    turn = s5p[:, TURN, bass.ds(i * 4 + 2 * u, 2)].unsqueeze(2).to_broadcast([P, 2, TOK])
                    step = [0]

                    def chained(ins):
                        step[0] += 1
                        ins.then_inc(s_pool, 1)
                        pool.wait_ge(s_pool, i * (2 * K) + (K * u + step[0]))
                        pool.sem_inc(more_over, 1)

                    chained(pool.tensor_tensor(ph[:, 1], time, turn, ALU.mult))
                    chained(pool.tensor_scalar(ph[:, 0], ph[:, 1], 0.25, None, ALU.add))
                    for v in range(2):
                        chained(pool.tensor_scalar(phr, ph[:, v], MAGIC, None, ALU.add))
                        chained(pool.tensor_scalar(phr, phr, -MAGIC, None, ALU.add))
                        if v == 0:
                            chained(pool.tensor_tensor(ph[:, v], ph[:, v], phr, ALU.subtract))
                            pool.nop().then_inc(ph_ready, 1)
                        else:
                            pool.tensor_tensor(ph[:, v], ph[:, v], phr, ALU.subtract).then_inc(ph_ready, 1)
                    assert step[0] <= K


_INS = ["x", "c", "ada_w", "ada_b", "moe_wg", "moe_bg", "moe_we", "moe_be", "moe_w1", "moe_w3", "moe_w2",
        "ev_w_in", "ev_w_out", "a_qn", "a_kn", "a_lq1", "a_lk1", "a_lq2", "a_lk2", "a_subln", "b_qn", "b_kn",
        "b_idx_kn", "od_w_in", "od_w_out", "c_qn", "c_kn", "s5_lam_re", "s5_lam_im", "s5_b_re", "s5_b_im",
        "s5_c_re", "s5_c_im", "s5_d", "s5_log_dt", "s5_glu_w", "s5_glu_b"]


def constants():
    import numpy as np

    t = np.zeros((P, CONST_W), np.float32)

    def put(name, v):
        lo, hi = CONST_AT[name]
        t[:, lo:hi] = v

    i = np.arange(P)
    put("ident", np.eye(P))
    put("ones", 1.0)
    put("tri", (i[:, None] < i[None, :]) * 1.0)
    put("cb2", np.concatenate([np.zeros((P, P)), np.where(i[None, :] <= i[:, None], 0.0, -BIG)], axis=1))
    put("iota", np.arange(CH)[None, :])
    put("time", np.arange(TOK)[None, :])
    put("desc4", np.arange(NG, 0, -1)[None, :])
    put("desc32", np.arange(NE, 0, -1)[None, :])
    put("par", np.stack([(i // 16) % 2 == 0, (i // 16) % 2 == 1], axis=1) * 1.0)
    for cn, sn, rot in (("rc", "rs", 16), ("ic", "is", 8)):
        inv = np.float32(500000.0) ** (-(np.arange(0, rot, 2, dtype=np.float32) / np.float32(rot)))
        ang = np.arange(TOK, dtype=np.float32)[:, None] * inv[None, :].astype(np.float32)
        for name, f in ((cn, np.cos), (sn, np.sin)):
            v = f(ang.astype(np.float32)).astype(np.float32)
            v = np.concatenate([v, v], axis=1)
            put(name, v.reshape(TT, P, rot).transpose(1, 0, 2).reshape(P, TT * rot))
    return t


def kernel(**inputs):
    import numpy as np
    import concourse.bacc as bacc
    from concourse.bass_utils import run_bass_kernel_spmd

    nc = bacc.Bacc("TRN2", target_bir_lowering=False, num_devices=1)
    arrays, aps = {}, {}
    for name in _INS:
        arrays[f"in_{name}"] = np.ascontiguousarray(inputs[name])
        aps[name] = nc.dram_tensor(f"in_{name}", arrays[f"in_{name}"].shape, F32, kind="ExternalInput").ap()
    arrays["in_const"] = constants()
    cst_d = nc.dram_tensor("in_const", (P, CONST_W), F32, kind="ExternalInput").ap()
    out_d = nc.dram_tensor("out_x", (1, TOK, D), F32, kind="ExternalOutput").ap()
    build(nc, aps, cst_d, out_d)
    r = run_bass_kernel_spmd(nc, [arrays], core_ids=[0])
    return r.results[0]["out_x"]
```

```python
from contextlib import ExitStack

import concourse.bass as bass
from concourse import mybir

F32 = mybir.dt.float32
I32 = mybir.dt.int32
ALU = mybir.AluOpType
ACT = mybir.ActivationFunctionType
AX = mybir.AxisListType.X

P = 128
D = 1024
KD = D // P
TOK = 256
TT = TOK // P
LAYERS = 2
NE, NG, EPG = 32, 4, 8
FF = 512
KF = FF // P
EPS = 1e-6
BIG = 1.0e30
SENT = -3.0e38
HD = 64
TOPK = TOK // 4
SETW = 1024
EV_IN = 3368
OD_QKV = 1536
MAGIC = 12582912.0
TWO_PI = 6.283185307179586
SIN_SCALE = 6.2831845
C1 = 6.28125
C2 = 0.0019353071795864769
GELU_C = 0.7978845608028654

RING = 6
SLOT = 4096
IN0_ORDER = [6, 3, 4, 0, 1, 5, 2]
IN1_ORDER = [3, 0, 1, 2]

LOADS0 = ([("ada", 0, j) for j in range(4)] + [("in", 0), ("in", 1)] + [("ada", 0, j) for j in range(4, 8)]
          + [("in", 2), ("in", 3)] + [("ada", 0, j) for j in range(8, 12)] + [("in", 4), ("in", 5), ("in", 6)]
          + [("ada", 1, j) for j in range(12)] + [("out", 1), ("out", 0)])
LOADS1 = [("in", q) for q in range(4)] + [("glu",), ("out", 1), ("out", 0)]
N_MOE = [len(LOADS0), len(LOADS0) + 3 * 32 + len(LOADS1)]
N_MIX1 = N_MOE[0] + 3 * 32
N_ALL = N_MOE[1] + 3 * 32


def n_of(l, *what):
    return LOADS0.index(what) if l == 0 else N_MIX1 + LOADS1.index(what)


def stream():
    slot, fill, old, last, count, at = [], [], [], {}, [0] * RING, 0
    for n in range(N_ALL):
        size = RING - 2 if N_MOE[0] <= n < N_MOE[1] else RING
        if n in (N_MOE[0], N_MOE[1]):
            at = 0
        s = at % size
        at += 1
        count[s] += 1
        slot.append(s)
        fill.append(count[s])
        old.append(last.get(s))
        last[s] = n
    return slot, fill, old


SLOT_OF, FILL_OF, OLD_OF = stream()

CH = 64
GE = 4
TURNS = NE // (2 * GE)
NP5 = 5
PADE = NE + 2 * GE


def const_layout():
    at, n = {}, 0
    for name, w in (("ident", P), ("ones", P), ("tri", P), ("cb2", 2 * P), ("iota", CH), ("rc", 2 * 16),
                    ("rs", 2 * 16), ("ic", 2 * 8), ("is", 2 * 8), ("time", TOK), ("desc4", NG),
                    ("desc32", NE), ("par", 2)):
        at[name] = (n, n + w)
        n += w
    return at, n


CONST_AT, CONST_W = const_layout()


def build(nc, a, cst_d, out_d):
    ctx = ExitStack()
    with ctx:
        def sb(name, shape, dt=F32):
            return ctx.enter_context(nc.sbuf_tensor(name, shape, dt))

        def sem(name):
            return ctx.enter_context(nc.semaphore(name))

        ring = sb("ring", [P, RING, SLOT])
        cst = sb("cst", [P, CONST_W])
        xT = sb("xT", [P, KD, TOK])
        hT = sb("hT", [P, KD, TOK])
        htok = sb("htok", [P, TT, D])
        modrow = sb("modrow", [P, 512])
        brow = sb("brow", [P, 512])
        modc = sb("modc", [P, LAYERS, 48])
        crep = sb("crep", [P, KD, 32])
        ccol = sb("ccol", [P, KD])
        ctmp = sb("ctmp", [P, 2, KD])
        gqk = sb("gqk", [P, 3, 2, HD])
        gidx = sb("gidx", [P, 32])
        subln = sb("subln", [P, 2 * HD])
        lrow = sb("lrow", [P, 4, HD])
        lamt = sb("lamt", [P, 8])
        wge = sb("wge", [P, LAYERS, KD, NG + NE])
        bge = sb("bge", [P, LAYERS, NG + NE])
        s5row = sb("s5row", [32, P])
        logdt = sb("logdt", [P, 16])
        BT = sb("BT", [P, 2, 4, P])
        CT = sb("CT", [P, 3, 4, P])
        modp = sb("modp", [P, 2 * LAYERS, KD])
        s5d = sb("s5d", [P, 4])
        glub = sb("glub", [P, 4])
        s5p = sb("s5p", [P, 24, 16])
        rstd = sb("rstd", [P, TOK])
        small = sb("small", [P, 256])
        rankm = sb("rankm", [P, TT, PADE])
        wt = sb("wt", [P, TT, PADE])
        cnti = sb("cnti", [P, LAYERS], I32)
        WORK = 14336
        work = sb("work", [P, WORK])

        def C(name):
            lo, hi = CONST_AT[name]
            return cst[:, lo:hi]

        ident, ones, tri = C("ident"), C("ones"), C("tri")

        class Carve:

            def __init__(self, at=0):
                self.at = at

            def __call__(self, *dims):
                n = 1
                for d in dims:
                    n *= d
                ap = work[:, self.at:self.at + n]
                self.at += n
                assert self.at <= WORK, self.at
                if len(dims) == 2:
                    ap = ap.rearrange("p (a b) -> p a b", a=dims[0])
                elif len(dims) == 3:
                    ap = ap.rearrange("p (a b c) -> p a b c", a=dims[0], b=dims[1])
                return ap

        c = Carve(TT * EV_IN)
        s5b = c(2, 16, 16)
        s5c = c(2, 4, HD)
        Bbar = c(2, 16, 16)
        Bd = c(2, 16, 32)
        Cd = c(2, 4, P)
        Btmp = c(16, 16)
        c = Carve()
        z0 = c(TT, EV_IN)
        qkT0 = c(16, TOK)
        idxT = c(4, TOK)
        selb = c(TT, TOK)
        at0 = c.at
        sqs = c(16, HD)
        c.at = at0
        sc_sb = c(2, 2, TOK)
        prob = hT[:, 0:4, :].rearrange("p (a b) c -> p a b c", a=2)
        ikrep = c(TT, P)
        tmp16 = c(2, 16, 16)
        relu_sb = [htok[:, u_, :].rearrange("p (a b) -> p a b", a=4) for u_ in range(2)]
        c.at = TT * EV_IN + 16 * TOK
        PT = c(2, 4, P)
        c = Carve()
        z1 = c(TT, OD_QKV)
        uT = c(4, TOK)
        tmp16_1 = c(2, 16, 16)
        sqs1 = c(16, HD)
        vv = c(2, 4, TOK)
        gy = c(4, TOK)
        tabs = ring[:, RING - 2:RING, :].rearrange("p v (j t) -> p v j t", t=TOK)
        mm = htok[:, :, :].rearrange("p t (a b) -> p t a b", b=TOK)
        y5 = c(4, TOK)
        qkT1 = c(8, TOK)
        sc_sb1 = uT.rearrange("p (a b) c -> p a b c", a=2)
        prob1 = c(2, 2, TOK)
        PT1 = c(2, 4, P)
        c = Carve()
        xgT = c(2, KD, GE * CH)
        Sd = c(4, GE * CH)
        Sw = c(4, GE * CH)
        SwT = c(2, 2, TOK)
        silu_a = c(2, FF)
        hid = c(2, FF)
        hidTb = c(2, KF, CH)
        y2 = c(2, D)
        rt = c(16, TT, NE)
        ph = c(2, 2, TOK)
        phr = c(2, TOK)
        Sd = Sd.rearrange("p (g t) s -> p g t s", g=2)
        Sw = Sw.rearrange("p (g t) s -> p g t s", g=2)

        PARAMS = []
        for s_, (qn, kn) in enumerate((("a_qn", "a_kn"), ("b_qn", "b_kn"), ("c_qn", "c_kn"))):
            PARAMS += [(gqk[:, s_, 0, :], a[qn][0].partition_broadcast(P), False),
                       (gqk[:, s_, 1, :], a[kn][0].partition_broadcast(P), False)]
        PARAMS += [(lrow[:, m, :], a[nm][0].partition_broadcast(P), False)
                   for m, nm in enumerate(("a_lq1", "a_lk1", "a_lq2", "a_lk2"))]
        PARAMS += [(gidx[:, :], a["b_idx_kn"][0].partition_broadcast(P), False),
                   (subln[:, :], a["a_subln"][0].partition_broadcast(P), False)]
        for l_ in range(LAYERS):
            PARAMS += [(wge[:, l_, :, 0:NG], a["moe_wg"][l_].rearrange("(k p) n -> p k n", p=P), False),
                       (wge[:, l_, :, NG:], a["moe_we"][l_].rearrange("(k p) n -> p k n", p=P), False),
                       (bge[:, l_, 0:NG], a["moe_bg"][l_].partition_broadcast(P), False),
                       (bge[:, l_, NG:], a["moe_be"][l_].partition_broadcast(P), False)]
        S5_PARAMS = [(s5row[0:16, :], a["s5_lam_re"][0].rearrange("(j g) p -> j (g p)", g=2), False),
                   (s5row[16:32, :], a["s5_lam_im"][0].rearrange("(j g) p -> j (g p)", g=2), False)]
        for g_ in range(2):
            S5_PARAMS.append((logdt[64 * g_:64 * g_ + 64, :],
                           a["s5_log_dt"][0].rearrange("(j g) -> g j", g=2)[g_].partition_broadcast(64), True))
        for v_, (bn, cn) in enumerate((("s5_b_re", "s5_c_re"), ("s5_b_im", "s5_c_im"))):
            S5_PARAMS += [(s5b[:, v_], a[bn][0].rearrange("(j g) p c -> (g p) j c", g=2), False),
                       (s5c[:, v_], a[cn][0].rearrange("(q g) c p -> (g c) q p", g=8), False)]
        PARAMS += [(s5d[:, :], a["s5_d"][0].rearrange("(q g) c -> (g c) q", g=8), True),
                   (glub[:, :], a["s5_glu_b"][0].rearrange("(q p) -> p q", p=P), True)]
        N_PAR, N_S5 = len(PARAMS), len(S5_PARAMS)

        A4 = ctx.enter_context(nc.psum_tensor("A4", [P, 4, 512], F32))
        B4, B5, B6, B7 = (ctx.enter_context(nc.psum_tensor(f"B{i}", [P, 512], F32)) for i in (4, 5, 6, 7))
        TRB = [B6, B7]
        OB = [B4, B5]

        slot_full = [sem(f"slot_full{i}") for i in range(RING)]
        slot_used = sem("slot_used")
        in_cst, in_x, in_c, in_par = sem("in_cst"), sem("in_x"), sem("in_c"), sem("in_par")
        in_brow, brow_zero = sem("in_brow"), sem("brow_zero")
        s_dve, s_act, s_pool = sem("dve_chain"), sem("act_chain"), sem("pool_chain")
        x_tr = sem("x_transposed")
        x_ev = sem("output_rows")
        c_exp, c_ready = sem("c_exp"), sem("c_ready")
        ada_done, ada1_read = sem("ada_rows_done"), sem("ada1_rows_read")
        sq_ready, ssq_done, var_ready, sd_ready, h_ready = (sem(n) for n in ("sq_ready", "ssq_done", "var_ready", "sd_ready", "h_ready"))
        proj_done, z_ready = sem("proj_done"), sem("z_ready")
        ms_ready, sq_root = sem("ms_ready"), sem("sq_root")
        tr_done, tr_ev = sem("tr_done"), sem("tr_evacuated")
        qk_ready = sem("qk_ready")
        idx_s, idx_relu, idx_acc_s = sem("idx_logits"), sem("idx_relu"), sem("idx_accumulated")
        score, score_read, negmax, expd, attn_ready = (sem(n) for n in ("score", "score_read", "negmax", "exp_done", "attn_ready"))
        pv_done, o_ready = sem("pv_done"), sem("o_ready")
        wout_done, x_upd = sem("wout_done"), sem("x_updated")
        lam_s, lam_e = sem("lam_sums"), sem("lam_exps")
        logit_done, route_d, route_e, mask_ready, rank_done = (sem(n) for n in (
            "logit_done", "route_diff", "route_exp", "mask_ready", "rank_done"))

        class MoeSems:

            def __init__(self, tag):
                def own(name):
                    return sem(name + tag)

                self.mat = own("slot_matrix")
                self.ready = own("matrices_ready")
                self.disp = own("dispatched")
                self.disp_ev = own("dispatch_copied")
                self.ab = own("ab_done")
                self.silu = own("silu_done")
                self.hid = own("hid_ready")
                self.hidT_ps = own("hid_transposed")
                self.hidT = own("hidT_ready")
                self.y = own("y_done")
                self.y_lo = own("y_copied_lo")
                self.y_hi = own("y_copied_hi")
                self.comb = own("combined")

        main = MoeSems("")
        more = [MoeSems(f"_more{l}") for l in range(LAYERS)]
        more_full = [[sem(f"more_full{l}_{m}") for m in range(3)] for l in range(LAYERS)]
        ranks_down = [sem(f"ranks_lowered{l}") for l in range(LAYERS)]
        cnt_ready = sem("chunks_counted")
        more_over = sem("more_steps_over")
        out_s = sem("out_written")
        p5_dt, p5_arg, p5_sc, p5_bt = (sem(n) for n in ("s5_dt", "s5_arg", "s5_sincos", "s5_bt_in"))
        ph_ready, bu_done, bu_read, prod_ready, y5_done = (sem(n) for n in (
            "phase_ready", "bu_done", "bu_read", "prod_ready", "y5_done"))
        y5_read, tab_done, in_s5 = sem("y5_read"), sem("tables_written"), sem("in_s5")
        tanh_in, tanh_out, gy_ready, glu_done, sig_ready, yo_ready = (sem(n) for n in (
            "tanh_in", "tanh_out", "gy_ready", "glu_done", "sig_ready", "yo_ready"))

        def slot(n):
            return SLOT_OF[n]

        def fills(n):
            return 16 * FILL_OF[n]

        def used_after(n):
            return n + 1 - (3 * NE if n >= N_MIX1 else 0)

        def slot8(n):
            return ring[:, slot(n), :].rearrange("p (k n) -> p k n", k=KD)

        def slot4(n):
            return ring[:, slot(n), :].rearrange("p (k n) -> p k n", k=4)

        L0_UNITS = [(1, b, t) for t in range(TT) for b in range(4)] + [(0, b, t) for t in range(TT) for b in range(4)]
        L1_UNITS = [(2, b, t) for t in range(TT) for b in range(4)]
        N0, N1 = len(L0_UNITS), len(L1_UNITS)
        LAG_PT, LAG_PV = 3, 4
        ADA1_ROWS = {1: (4, 5, 6, 7), 2: (12, 13, 14, 15)}
        ADA1_COLS = {1: 0, 8: 1, 16: 2}

        GATE_AT = 1
        PROJ1 = [(0, 0), (1, 0), (0, 1), (1, 1), (2, 0), (2, 1)]

        ORDER = ["x0", "x1", "x2", "x3", "ada0r0", "ada0c0", "lam", "ada0r1", "ada0c1", "idx0", "idx1", "bt0", "bt1",
                 "ct0", "ct1", "ada0r2", "ada0c2", "B0", "B1", "B2", "B3", "ada1r0", "A0", "A1", "A2", "A3"]
        for j in range(N0 + LAG_PT):
            if 0 <= j - LAG_PT < N0:
                ORDER.append(f"p{j - LAG_PT}")
            if j in ADA1_COLS:
                ORDER.append(f"ada1c{ADA1_COLS[j]}")
        ORDER += ["oB0", "oB1", "oA0", "oA1", "h0_0", "h0_1", "h0_2", "h0_3", "C0", "C1", "C2", "C3"]
        ORDER += [f"p{N0 + j}" for j in range(N1)] + ["oC0", "oC1", "h1_0", "h1_1", "h1_2", "h1_3"]
        U = {name: u for u, name in enumerate(ORDER)}

        def n_maps(s):
            return 1 if s == 0 else 2

        MORE = TOK // CH - 1

        def more_chunks(eng, l, body, before=None, after=None):
            eng.wait_ge(cnt_ready, l + 1)
            extra = eng.value_load(cnti[0:1, l:l + 1], min_val=0, max_val=MORE)
            with eng.Fori(0, MORE) as c:
                with eng.If(c < extra):
                    if before:
                        before(c)
                    with eng.Fori(0, NE // GE) as i:
                        body(c * (NE // GE) + i, i)
                    if after:
                        after(c)

        block = ctx.enter_context(nc.Block())

        @block.sync
        def _(sp):
            def slot_free(n):
                old = OLD_OF[n]
                if old is None:
                    return
                for l in range(LAYERS):
                    e, m = divmod(old - N_MOE[l], 3)
                    if 0 <= e < NE:
                        sp.wait_ge(main.ab if m < 2 else main.y, NE * l + e + 1 + m // 2)
                        return
                sp.wait_ge(slot_used, used_after(old))
                if n >= N_MOE[1] and old < N_MOE[0]:
                    sp.wait_ge(prod_ready, 8)

            def load(n, dst, src):
                slot_free(n)
                sp.dma_start(dst, src).then_inc(slot_full[slot(n)], 16)

            def load_mixer(l):
                w_in, w_out = (a["ev_w_in"], a["ev_w_out"]) if l == 0 else (a["od_w_in"], a["od_w_out"])
                for q, what in enumerate(LOADS0 if l == 0 else LOADS1):
                    n = q + (0, N_MIX1)[l]
                    if what[0] == "ada":
                        load(n, slot8(n), a["ada_w"][what[1], :, 512 * what[2]:512 * what[2] + 512]
                             .rearrange("(k p) n -> p k n", p=P))
                    elif what[0] == "in":
                        ch = (IN0_ORDER, IN1_ORDER)[l][what[1]]
                        w = min(512, EV_IN - 512 * ch) if l == 0 else 512
                        load(n, slot8(n)[:, :, 0:w], w_in[0, :, 512 * ch:512 * ch + w].rearrange("(k p) n -> p k n", p=P))
                    elif what[0] == "glu":
                        load(n, slot8(n)[:, 0:4, :], a["s5_glu_w"][0].rearrange("(k p) n -> p k n", p=P))
                    else:
                        load(n, slot4(n), w_out[0, 512 * what[1]:512 * what[1] + 512, :].rearrange("(k p) n -> p k n", p=P))

            def load_moe(l):
                w1 = a["moe_w1"].rearrange("l e (k p) n -> (l e) p k n", p=P)
                w3 = a["moe_w3"].rearrange("l e (k p) n -> (l e) p k n", p=P)
                w2 = a["moe_w2"].rearrange("l e (k p) n -> (l e) p k n", p=P)

                def expert(e):
                    for m, w in enumerate((w1, w3, w2)):
                        n = N_MOE[l] + 3 * e + m
                        load(n, (slot8 if m < 2 else slot4)(n), w[NE * l + e])

                T = 2 * GE
                for e in range(2):
                    expert(e)
                with sp.Fori(0, TURNS - 1) as i:
                    for q in range(2, T + 2):
                        for m, w in enumerate((w1, w3, w2)):
                            n = N_MOE[l] + 3 * q + m
                            e, m_old = divmod(3 * q + m - (n - OLD_OF[n]), 3)
                            sp.wait_ge(main.ab if m_old < 2 else main.y, i * T + (NE * l + e + 1 + m_old // 2))
                            src = w[bass.ds(i * T + (NE * l + q), 1)].rearrange("e p k n -> p (e k) n")
                            sp.dma_start((slot8 if m < 2 else slot4)(n), src).then_inc(slot_full[slot(n)], 16)
                for e in range(NE - T + 2, NE):
                    expert(e)

                def more_loads(gb, i):
                    for j in range(GE):
                        for m, w in enumerate((w1, w3, w2)):
                            sp.wait_ge(more[l].y, gb * GE + (j + 1))
                            src = w[bass.ds(i * GE + (NE * l + j), 1)].rearrange("e p k n -> p (e k) n")
                            sp.dma_start((slot8 if m < 2 else slot4)(m), src).then_inc(more_full[l][m], 16)

                def ring_empty(c):
                    sp.wait_ge(main.y, NE * (l + 1) + 1)

                def ring_free(c):
                    sp.wait_ge(more[l].y, c * NE + (NE + 1))
                    sp.sem_inc(more_over, 1)

                more_chunks(sp, l, more_loads, before=ring_empty, after=ring_free)

            for l in range(LAYERS):
                load_mixer(l)
                load_moe(l)

        @block.tensor
        def _(pe):
            def full(n):
                pe.wait_ge(slot_full[slot(n)], fills(n))

            units = [0]

            def pass_bank(name):
                u = units[0]
                assert ORDER[u] == name, (ORDER[u], name)
                units[0] += 1
                if u >= 2:
                    pe.wait_ge(tr_ev, u - 1)
                return TRB[u % 2]

            def tr_unit(name, parts, waits=()):
                for s, v in waits:
                    pe.wait_ge(s, v)
                bank = pass_bank(name)
                for b, src in enumerate(parts):
                    n = src.shape[0]
                    ins = pe.transpose(bank[:, P * b:P * b + n], src, ident[0:n, 0:n])
                ins.then_inc(tr_done, 1)

            def ada_part(bank, l, r, ks):
                ns = [n_of(0, "ada", l, 4 * r + g) for g in range(4)]
                for k in ks:
                    if k == 0:
                        for n in ns:
                            full(n)
                        for g in range(4):
                            pe.matmul(bank[32 * g:32 * g + 32, :], ident[:, 12 * l + 4 * r + g:12 * l + 4 * r + g + 1].to_broadcast([P, 32]),
                                      brow[:, :], start=True, stop=False)
                    for g in range(4):
                        ins = pe.matmul(bank[32 * g:32 * g + 32, :], crep[:, k, :], slot8(ns[g])[:, k, :],
                                        start=False, stop=(k == KD - 1))
                if k == KD - 1:
                    ins.then_inc(ada_done, 1)
                    pe.wait_ge(ada_done, 3 * l + r + 1)

            def ada_rows(l, r):
                bank = pass_bank(f"ada{l}r{r}")
                if r == 0:
                    pe.wait_ge(in_brow, 16)
                ada_part(bank, l, r, range(KD))
                pe.nop().then_inc(tr_done, 1)
                pe.nop().then_inc(slot_used, 4)

            def ada_columns(r):
                tr_unit(f"ada0c{r}", [modrow[:, P * b:P * b + P] for b in range(4)], [(tr_ev, U[f"ada0r{r}"] + 1)])

            def sum_squares(q, b):
                pe.wait_ge(sq_ready, 4 * q + b + 1)
                for k in range(2 * b, 2 * b + 2):
                    ins = pe.matmul(B5[:, 0:TOK], ones, htok[:, :, :].rearrange("p t (a b) -> p (t a) b", b=TOK)[:, k, :],
                                    start=(k == 0), stop=(k == KD - 1), skip_group_check=True)
                if b == 3:
                    ins.then_inc(ssq_done, 1)

            def project0(ch, n, done):
                full(n)
                w = min(512, EV_IN - 512 * ch)
                for t in range(TT):
                    if done + t >= 2:
                        pe.wait_ge(z_ready, done + t - 1)
                    bank = OB[t]
                    for k in range(KD):
                        ins = pe.matmul(bank[:, 0:w], hT[:, k, P * t:P * t + P], slot8(n)[:, k, 0:w],
                                        start=(k == 0), stop=(k == KD - 1))
                    ins.then_inc(proj_done, 1)
                pe.wait_ge(proj_done, done + TT)
                pe.nop().then_inc(slot_used, 1)

            def project1(m):
                ch, t = PROJ1[m]
                n, done = n_of(1, "in", 1 + ch), 18 + m
                full(n)
                pe.wait_ge(z_ready, done)
                for k in range(KD):
                    ins = pe.matmul(B5[:, :], hT[:, k, P * t:P * t + P], slot8(n)[:, k, :], start=(k == 0), stop=(k == KD - 1))
                ins.then_inc(proj_done, 1)
                if t == 1:
                    pe.wait_ge(proj_done, done + 1)
                    pe.nop().then_inc(slot_used, 1)

            def att_score(l, base, j, s, b, t):
                blk = (0, 8, 0)[s] + b
                qk = qkT0 if l == 0 else qkT1
                u = base + j
                if u >= 2:
                    pe.wait_ge(score_read, u - 1)
                w = P * (t + 1)
                for m in range(2):
                    ins = pe.matmul(A4[:, 2 * (u % 2) + m, 0:w], qk[64 * m:64 * m + 64, blk, P * t:P * t + P],
                                    qk[64 * m:64 * m + 64, blk + 4, 0:w], start=True, stop=True)
                ins.then_inc(score, 1)

            def att_pt(base, j, s, b, t):
                parts = [prob[:, (base + j) % 2, m, P * kt:P * kt + P] for m in range(n_maps(s)) for kt in range(t + 1)]
                if base:
                    parts = [prob1[:, (base + j) % 2, m, P * kt:P * kt + P] for m in range(n_maps(s)) for kt in range(t + 1)]
                w = [(expd, base + j + 1)]
                if s == 0:
                    w = [(attn_ready, b + 4 * t + 1)]
                tr_unit(f"p{base + j}", parts, w)

            def att_pv(base, j, s, b, t):
                pe.wait_ge(tr_ev, U[f"p{base + j}"] + 1)
                z, vcol = ((z0, 1024), (z0, 2560), (z1, 1024))[s]
                pt = PT if base == 0 else PT1
                nm, hw = (1, 2 * HD) if s == 0 else (2, HD)
                for m in range(nm):
                    h = b * nm + m
                    for kt in range(t + 1):
                        ins = pe.matmul(OB[t][:, hw * h:hw * h + hw], pt[:, (base + j) % 2, m * (t + 1) + kt, :],
                                        z[:, kt, vcol + hw * h:vcol + hw * h + hw], start=(kt == 0), stop=(kt == t))
                ins.then_inc(pv_done, 1)

            def attention(l, base, units, hook):
                n = len(units)
                for j in range(n + LAG_PV):
                    if j < n:
                        att_score(l, base, j, *units[j])
                    if 0 <= j - LAG_PT < n:
                        att_pt(base, j - LAG_PT, *units[j - LAG_PT])
                    if 0 <= j - LAG_PV:
                        if l == 1 and j == LAG_PV:
                            pe.wait_ge(sig_ready, 1)
                        if l == 0 and j - LAG_PV in (4, 12):
                            pe.wait_ge(ada1_read, (1, 2)[j - LAG_PV > 4])
                        if l == 0 and j - LAG_PV in (8, 12):
                            pe.wait_ge(o_ready, (j - LAG_PV) // 4 - 1)
                        att_pv(base, j - LAG_PV, *units[j - LAG_PV])
                    hook(j)

            def out_proj(l, cc):
                n = n_of(l, "out", cc)
                full(n)
                if cc == 1:
                    pe.wait_ge(score_read, (N0, N0 + N1)[l])
                for b in range(4):
                    for k in range(4):
                        for f in (2 * b, 2 * b + 1):
                            ins = pe.matmul(A4[:, b, TOK * (f % 2):TOK * (f % 2) + TOK],
                                            slot4(n)[:, k, P * f:P * f + P], hT[:, 4 * cc + k, :],
                                            start=(cc == 1 and k == 0 and f % 2 == 0), stop=(cc == 0 and k == 3),
                                            skip_group_check=True)
                    if cc == 0:
                        ins.then_inc(wout_done, 1)
                        if b:
                            sum_squares(2 * l + 1, b - 1)
                if cc == 1:
                    ins.then_inc(slot_used, 1)
                else:
                    pe.wait_ge(wout_done, 4 * (l + 1))
                    pe.nop().then_inc(slot_used, 1)
                    sum_squares(2 * l + 1, 3)

            def moe(l):
                def token_major(h):
                    for t in range(TT):
                        tr_unit(f"h{l}_{2 * h + t}", [hT[:, 4 * h + b, P * t:P * t + P] for b in range(4)],
                                [(h_ready, 2 * (2 * l + 1) + h + 1)])

                token_major(0)
                pe.wait_ge(h_ready, 2 * (2 * l + 1) + 2)
                for t in range(TT):
                    for k in range(KD):
                        ins = pe.matmul(B5[:, 36 * t:36 * t + 36], hT[:, k, P * t:P * t + P], wge[:, l, k, :],
                                        start=(k == 0), stop=(k == KD - 1))
                ins.then_inc(logit_done, 1)
                token_major(1)
                pe.wait_ge(x_upd, 8 * l + 4)
                for bank in range(4):
                    for q in range(4):
                        ins = pe.matmul(A4[:, bank, P * q:P * q + P], ident, C("cb2")[:, 0:P], start=(q == 0),
                                        stop=False, skip_group_check=True)
                pe.wait_ge(mask_ready, l + 1)
                M = [rt[:, 0, t, :] for t in range(TT)]
                pe.matmul(B5[:, 0:NE], tri, M[0], start=True, stop=True)
                pe.matmul(B5[:, NE:2 * NE], ones, M[0], start=True, stop=False)
                pe.matmul(B5[:, NE:2 * NE], tri, M[1], start=False, stop=True)
                pe.matmul(B5[:, 2 * NE:3 * NE], ones, M[0], start=True, stop=False)
                pe.matmul(B5[:, 2 * NE:3 * NE], ones, M[1], start=False, stop=True).then_inc(rank_done, 1)

                dbase, sbase, ebase = l * NP5 * (2 * GE + 1), l * (2 * GE + 2), l * NE

                def dispatch(sm, g, part, ready, copied, bank=B4):
                    if part == 0:
                        pe.wait_ge(sm.ready, ready)
                    pe.wait_ge(sm.disp_ev, copied + 1)
                    if part < 4:
                        for q in range(2):
                            f = 2 * part + q
                            for t in range(TT):
                                ins = pe.matmul(bank[:, 256 * q:256 * q + 256], htok[:, t, P * f:P * f + P], Sd[:, g, t, :],
                                                start=(t == 0), stop=(t == 1))
                    else:
                        for pr in range(2):
                            for t in range(TT):
                                ins = pe.transpose(bank[:, 256 * pr + P * t:256 * pr + P * t + P],
                                                   Sw[:, g, t, P * pr:P * pr + P], ident)
                    ins.then_inc(sm.disp, 1)

                def gate_up(sm, g, j, e1, wa, wb):
                    pe.wait_ge(sm.hid, e1 + 1)
                    for k in range(KD):
                        for m, w in enumerate((wa, wb)):
                            ins = pe.matmul(B5[64 * m:64 * m + 64, :], xgT[:, g, k, CH * j:CH * j + CH], w[:, k, :],
                                            start=(k == 0), stop=(k == KD - 1))
                    ins.then_inc(sm.ab, 1)

                def hidden_transposed(sm, q, e1):
                    pe.wait_ge(sm.hid, e1 + 2)
                    for k in range(KF):
                        ins = pe.transpose(B6[:, P * k:P * k + P], hid[:, q % 2, P * k:P * k + P], ident)
                    ins.then_inc(sm.hidT_ps, 1)

                def down(sm, q, e1, w):
                    pe.wait_ge(sm.y_lo, e1 + 1)
                    pe.wait_ge(sm.y_hi, e1 + 1)
                    pe.wait_ge(sm.hidT, e1 + 1)
                    for k in range(KF):
                        for m in range(2):
                            ins = pe.matmul(B7[64 * m:64 * m + 64, :], hidTb[:, q % 2, k, :],
                                            w[:, k, 512 * m:512 * m + 512], start=(k == 0), stop=(k == KF - 1))
                    ins.then_inc(sm.y, 1)

                def combine(sm, g, q, e1):
                    pe.wait_ge(sm.y_lo, e1 + 2)
                    pe.wait_ge(sm.y_hi, e1 + 2)
                    pr = q // 2
                    for f in range(KD):
                        ins = pe.matmul(A4[:, f // 2, TOK * (f % 2):TOK * (f % 2) + TOK],
                                        y2[:, pr % 2, P * f:P * f + P], SwT[:, g, pr % 2, :],
                                        start=False, stop=False, skip_group_check=True)
                    ins.then_inc(sm.comb, 1)

                pe.wait_ge(tr_ev, U[f"h{l}_3"] + 1)
                for part in range(NP5):
                    dispatch(main, 0, part, sbase + 1, dbase + max(part - 1, 0), (B4, B5)[part % 2])
                with pe.Fori(0, TURNS) as i:
                    for g in range(2):
                        for j in range(GE):
                            q = GE * g + j
                            n = N_MOE[l] + 3 * q
                            e1 = i * (2 * GE) + (ebase + q)
                            gi = i * 2 + g
                            fill = i * (16 * (6 * GE // (RING - 2 if l == 0 else RING)))

                            def ahead(part):
                                dispatch(main, 1 - g, part, gi + (sbase + 2), gi * NP5 + (dbase + NP5 + part))

                            if j == 0:
                                pe.wait_ge(main.disp_ev, gi * NP5 + (dbase + NP5 + 1))
                            pe.wait_ge(slot_full[slot(n)], fill + fills(n))
                            pe.wait_ge(slot_full[slot(n + 1)], fill + fills(n + 1))
                            gate_up(main, g, j, e1, slot8(n), slot8(n + 1))
                            ahead(j)
                            hidden_transposed(main, q, e1)
                            if j == 3:
                                ahead(4)
                            pe.wait_ge(slot_full[slot(n + 2)], fill + fills(n + 2))
                            down(main, q, e1, slot4(n + 2))
                            if j % 2 == 1:
                                combine(main, g, q, e1)

                def more_experts(gb, i):
                    sm = more[l]
                    for part in range(NP5):
                        dispatch(sm, 0, part, gb + 1, gb * NP5 + part)
                    pe.wait_ge(sm.disp_ev, gb * NP5 + (NP5 + 1))
                    for j in range(GE):
                        e1 = gb * GE + j
                        pe.wait_ge(more_full[l][0], e1 * 16 + 16)
                        pe.wait_ge(more_full[l][1], e1 * 16 + 16)
                        gate_up(sm, 0, j, e1, slot8(0), slot8(1))
                        hidden_transposed(sm, j, e1)
                        pe.wait_ge(more_full[l][2], e1 * 16 + 16)
                        down(sm, j, e1, slot4(2))
                        if j % 2 == 1:
                            combine(sm, 0, j, e1)

                more_chunks(pe, l, more_experts)

            for sm in (main, *more):
                pe.nop().then_inc(sm.y, 1)
            pe.wait_ge(in_cst, 16)
            for t in range(TT):
                for h in range(2):
                    tr_unit(f"x{2 * t + h}", [htok[:, t, 512 * h + P * b:512 * h + P * b + P] for b in range(4)], [(in_x, 16)])
            for b in range(4):
                sum_squares(0, b)
            pe.wait_ge(c_ready, 1)
            ada_rows(0, 0)
            ada_columns(0)
            def index_logits(t):
                pe.wait_ge(tr_ev, U["idx1"] + 1)
                if t:
                    pe.wait_ge(idx_relu, 2)
                for half in range(2):
                    w = P * (t + 1)
                    for m in range(4):
                        ins = pe.matmul(A4[:, m, TOK * half:TOK * half + w], idxT[32 * m:32 * m + 32, half, P * t:P * t + P],
                                        idxT[32 * m:32 * m + 32, 2, 0:w], start=True, stop=True)
                ins.then_inc(idx_s, 1)

            pe.wait_ge(h_ready, 2)
            for q, ch in enumerate(IN0_ORDER):
                project0(ch, n_of(0, "in", q), TT * q)
                if q == 0:
                    tr_unit("lam", [s5row[:, :]], [(in_s5, 16 * N_S5)])
                if q == 1:
                    ada_rows(0, 1)
                if q == 2:
                    ada_columns(1)
                    for t in range(TT):
                        tr_unit(f"idx{t}", [z0[:, t, 3072:3200], z0[:, t, 3200:3328], ikrep[:, t, :]], [(qk_ready, t + 1)])
                    for v in range(2):
                        tr_unit(f"bt{v}", [Bd[:, v, 4 * q4:4 * q4 + 4, :].rearrange("p a b -> p (a b)") for q4 in range(4)],
                                [(p5_bt, 1)])
                    for v in range(2):
                        tr_unit(f"ct{v}", [Cd[:, v, q4, :] for q4 in range(4)])
                if q == 3:
                    index_logits(0)
                    ada_rows(0, 2)
                if q == 4:
                    ada_columns(2)
                    for t in range(TT):
                        for h in range(2):
                            tr_unit(f"B{2 * t + h}", [z0[:, t, 1536 + 512 * h + P * b:1536 + 512 * h + P * b + P] for b in range(4)],
                                    [(qk_ready, 3 + t)])
                    index_logits(1)
            ada_rows(1, 0)
            for t in range(TT):
                for h in range(2):
                    tr_unit(f"A{2 * t + h}", [z0[:, t, 512 * h + P * b:512 * h + P * b + P] for b in range(4)], [(qk_ready, 5 + t)])
            pe.wait_ge(idx_relu, 4)
            pe.wait_ge(z_ready, 14)
            pe.wait_ge(tr_ev, U["A3"] + 1)

            def ada1(j):
                for r in (1, 2):
                    if j in ADA1_ROWS[r]:
                        part = ADA1_ROWS[r].index(j)
                        if part == 0 and r == 2:
                            pe.wait_ge(o_ready, 2)
                        ada_part(OB[1], 1, r, range(2 * part, 2 * part + 2))
                        if part == 3:
                            pe.nop().then_inc(slot_used, 4)
                if j in ADA1_COLS:
                    r = ADA1_COLS[j]
                    tr_unit(f"ada1c{r}", [modrow[:, P * b:P * b + P] for b in range(4)], [(ada1_read, r) if r else (tr_ev, U["ada1r0"] + 1)])

            attention(0, 0, L0_UNITS, ada1)
            for s, name in ((1, "oB"), (0, "oA")):
                for t in range(TT):
                    tr_unit(f"{name}{t}", [htok[:, t, 512 * s + P * b:512 * s + P * b + P] for b in range(4)],
                            [(o_ready, 3 - 2 * s + t)])
                pe.wait_ge(tr_ev, U[f"{name}1"] + 1)
                out_proj(0, s)
            moe(0)
            for b in range(4):
                sum_squares(2, b)
            pe.wait_ge(h_ready, 6)
            pe.wait_ge(x_upd, 8)
            def s5_input(q4):
                if q4:
                    pe.wait_ge(bu_read, q4)
                for v in range(2):
                    for jj in range(4):
                        ins = pe.matmul(A4[:, jj, TOK * v:TOK * v + TOK],
                                        BT[32 * jj:32 * jj + 32, v, q4, :], uT[32 * jj:32 * jj + 32, q4, :],
                                        start=True, stop=True)
                ins.then_inc(bu_done, 1)

            def s5_output(q4):
                if q4:
                    pe.wait_ge(y5_read, q4)
                for half in range(2):
                    src = (mm, vv)[half]
                    pe.wait_ge(prod_ready, 2 * q4 + half + 1)
                    for v in range(2):
                        for jj in range(4):
                            which = (0, 1)[v] if half == 0 else 2
                            ins = pe.matmul(B4[32 * jj:32 * jj + 32, 0:TOK], CT[:, which, q4, 32 * jj:32 * jj + 32],
                                            src[:, v, jj, :], start=(half == 0 and v == 0), stop=(half == 1 and v == 1),
                                            skip_group_check=True)
                    ins.then_inc(y5_done, 1)

            n = n_of(1, "in", 0)
            full(n)
            for f in range(4):
                pe.wait_ge(z_ready, 14 + f)
                for k in range(KD):
                    ins = pe.matmul(B5[:, 0:TOK], slot8(n)[:, k, P * f:P * f + P], hT[:, k, :],
                                    start=(k == 0), stop=(k == KD - 1))
                ins.then_inc(proj_done, 1)
            pe.wait_ge(proj_done, 18)
            pe.nop().then_inc(slot_used, 1)
            pe.wait_ge(z_ready, 18)
            s5_input(0)
            project1(0)
            for q4 in range(1, 4):
                s5_input(q4)
                s5_output(q4 - 1)
                project1(q4)
            project1(4)
            s5_output(3)
            project1(5)
            for h in range(2):
                tr_unit(f"C{h}", [z1[:, 0, 512 * h + P * b:512 * h + P * b + P] for b in range(4)], [(qk_ready, 7)])
            def gate(j):
                if j != GATE_AT:
                    return
                for h in range(2):
                    tr_unit(f"C{2 + h}", [z1[:, 1, 512 * h + P * b:512 * h + P * b + P] for b in range(4)], [(qk_ready, 8)])
                n = n_of(1, "glu")
                pe.wait_ge(gy_ready, 1)
                full(n)
                for f in range(4):
                    for k in range(4):
                        ins = pe.matmul(OB[f // 2][:, TOK * (f % 2):TOK * (f % 2) + TOK], slot8(n)[:, k, P * f:P * f + P],
                                        gy[:, k, :], start=(k == 0), stop=(k == 3))
                ins.then_inc(glu_done, 1)
                pe.wait_ge(glu_done, 1)
                pe.nop().then_inc(slot_used, 1)
                pe.wait_ge(tr_ev, U["C3"] + 1)

            pe.wait_ge(tr_ev, U["C1"] + 1)
            attention(1, N0, L1_UNITS, gate)
            pe.wait_ge(yo_ready, 1)
            out_proj(1, 1)
            for t in range(TT):
                tr_unit(f"oC{t}", [htok[:, t, P * b:P * b + P] for b in range(4)], [(o_ready, 5 + t)])
            pe.wait_ge(tr_ev, U["oC1"] + 1)
            out_proj(1, 0)
            moe(1)
            for h in range(2):
                pe.wait_ge(x_upd, 12 + 2 * (h + 1))
                for t in range(TT):
                    bank = (B4, B5, B6, B7)[2 * h + t]
                    for b in range(4):
                        ins = pe.transpose(bank[:, P * b:P * b + P], xT[:, 4 * h + b, P * t:P * t + P], ident)
                    ins.then_inc(x_tr, 1)

        @block.vector
        def _(dve):
            count = [0]

            def link(ins):
                count[0] += 1
                ins.then_inc(s_dve, 1)
                dve.wait_ge(s_dve, count[0])

            def tt(out, a0, a1, op):
                link(dve.tensor_tensor(out, a0, a1, op))

            def ts(out, a0, s1, s2, o0, o1=ALU.bypass):
                link(dve.tensor_scalar(out, a0, s1, s2, o0, o1) if s2 is not None else dve.tensor_scalar(out, a0, s1, None, o0))

            def stt(out, a0, s, a1, o0, o1):
                link(dve.scalar_tensor_tensor(out, a0, s, a1, o0, o1))

            def tell(s, n=1):
                dve.nop().then_inc(s, n)

            roots = [0]

            def rsqrt(x):
                tell(ms_ready)
                roots[0] += 1
                dve.wait_ge(sq_root, roots[0])
                link(dve.reciprocal(x, x))

            def square(b):
                sq = htok[:, :, :].rearrange("p t (a b) -> p (t a) b", b=TOK)
                dve.tensor_tensor(sq[:, 2 * b:2 * b + 2, :], xT[:, 2 * b:2 * b + 2, :], xT[:, 2 * b:2 * b + 2, :],
                                  ALU.mult).then_inc(sq_ready, 1)

            def norm_modulate(q):
                l, w = q // 2, q % 2
                dve.wait_ge(ssq_done, q + 1)
                dve.tensor_scalar(rstd[:, :], B5[:, 0:TOK], 1.0 / D, EPS, ALU.mult, ALU.add).then_inc(var_ready, 1)
                dve.wait_ge(sd_ready, q + 1)
                link(dve.reciprocal(rstd[:, :], rstd[:, :]))
                if q == 0:
                    tt(hT[:, :, :], xT[:, :, :], rstd[:, :].unsqueeze(1).to_broadcast([P, KD, TOK]), ALU.mult)
                dve.wait_ge(tr_ev, U[f"ada{l}c{2 * w}"] + 1)
                ts(modp[:, q, :], modc[:, l, 24 * w + 8:24 * w + 16], 1.0, None, ALU.add)
                for h in range(2):
                    if q:
                        tt(hT[:, 4 * h:4 * h + 4, :], xT[:, 4 * h:4 * h + 4, :], rstd[:, :].unsqueeze(1).to_broadcast([P, 4, TOK]), ALU.mult)
                    for k in range(4 * h, 4 * h + 4):
                        ins = dve.tensor_scalar(hT[:, k, :], hT[:, k, :], modp[:, q, k:k + 1],
                                                modc[:, l, 24 * w + k:24 * w + k + 1], ALU.mult, ALU.add)
                    ins.then_inc(h_ready, 1)

            def rope(v, t, n, half, cn, sn, tmp):
                cc = C(cn).rearrange("p (t a) -> p t a", t=2)[:, t, :].unsqueeze(1).to_broadcast([P, n, 2 * half])
                ss = C(sn).rearrange("p (t a) -> p t a", t=2)[:, t, :].unsqueeze(1).to_broadcast([P, n, 2 * half])
                ta, tb = tmp[:, 0, 0:n, 0:2 * half], tmp[:, 1, 0:n, 0:2 * half]
                dve.tensor_tensor(ta, v[:, :, 0:2 * half], cc, ALU.mult)
                tt(tb, v[:, :, 0:2 * half], ss, ALU.mult)
                dve.tensor_tensor(v[:, :, 0:half], ta[:, :, 0:half], tb[:, :, half:2 * half], ALU.subtract)
                tt(v[:, :, half:2 * half], ta[:, :, half:2 * half], tb[:, :, 0:half], ALU.add)

            def norm_rope(v, t, gi, sq, tmp):
                tt(sq, v, v, ALU.mult)
                ms = small[:, 0:16]
                link(dve.tensor_reduce(ms, sq, AX, ALU.add))
                ts(ms, ms, 1.0 / HD, EPS, ALU.mult, ALU.add)
                rsqrt(ms)
                tt(v, v, ms.unsqueeze(2).to_broadcast([P, 16, HD]), ALU.mult)
                v4 = v.rearrange("p (q h) d -> p q h d", q=2)
                tt(v4, v4, gqk[:, gi, :, :].unsqueeze(2).to_broadcast([P, 2, 8, HD]), ALU.mult)
                rope(v, t, 16, 8, "rc", "rs", tmp)
                tell(qk_ready)

            def softmax_unit(base, j, s, b, t, buf, pr):
                u = base + j
                w = P * (t + 1)
                dve.wait_ge(score, u + 1)
                if u >= 2:
                    dve.wait_ge(expd, u - 1)
                src = A4[:, 2 * (u % 2):2 * (u % 2) + 2, 0:w]
                mask = selb[:, t, 0:w] if s == 1 else C("cb2")[:, 2 * P - w:2 * P]
                stt(buf[:, u % 2, :, 0:w], src, HD ** -0.5, mask.unsqueeze(1).to_broadcast([P, 2, w]), ALU.mult, ALU.add)
                tell(score_read)
                nm = small[:, 16 + 2 * (u % 4):18 + 2 * (u % 4)]
                link(dve.tensor_reduce(nm, buf[:, u % 2, :, 0:w], AX, ALU.max))
                ts(nm, nm, -1.0, None, ALU.mult)
                tell(negmax)

            def sums(u):
                return small[:, 32 + 2 * u:34 + 2 * u]

            def combine_unit(j, b, t):
                w = P * (t + 1)
                dve.wait_ge(expd, j + 1)
                su = sums(j)
                link(dve.reciprocal(su, su))
                tt(su[:, 1:2], su[:, 1:2], lamt[:, 4:5], ALU.mult)
                ts(prob[:, j % 2, 1, 0:w], prob[:, j % 2, 1, 0:w], su[:, 1:2], None, ALU.mult)
                stt(prob[:, j % 2, 0, 0:w], prob[:, j % 2, 0, 0:w], su[:, 0:1], prob[:, j % 2, 1, 0:w], ALU.mult, ALU.subtract)
                tell(attn_ready)

            def out_rows(base, t, s, pv, first):
                dve.wait_ge(pv_done, pv)
                su = small[:, 32 + 2 * (base + 4 * t):40 + 2 * (base + 4 * t)]
                link(dve.reciprocal(su, su))
                tt(htok[:, t, first:first + 512].rearrange("p (h d) -> p h d", h=8),
                   OB[t][:, :].rearrange("p (h d) -> p h d", h=8), su.unsqueeze(2).to_broadcast([P, 8, HD]), ALU.mult)
                tell(o_ready)

            def out_rows_a(t, pv):
                dve.wait_ge(pv_done, pv)
                o = htok[:, t, 0:512].rearrange("p (h d) -> p h d", h=4)
                link(dve.tensor_copy(o, OB[t][:, :].rearrange("p (h d) -> p h d", h=4)))
                sq = sc_sb[:, t % 2].rearrange("p a b -> p (a b)").rearrange("p (h d) -> p h d", h=4)
                tt(sq, o, o, ALU.mult)
                ms = small[:, 0:4]
                link(dve.tensor_reduce(ms, sq, AX, ALU.add))
                ts(ms, ms, 1.0 / (2 * HD), EPS, ALU.mult, ALU.add)
                rsqrt(ms)
                tt(o, o, ms.unsqueeze(2).to_broadcast([P, 4, 2 * HD]), ALU.mult)
                tt(o, o, subln[:, :].unsqueeze(1).to_broadcast([P, 4, 2 * HD]), ALU.mult)
                ts(o, o, 0.8, None, ALU.mult)
                tell(o_ready)

            def residual(l, w):
                for b in range(4):
                    if w == 0:
                        dve.wait_ge(wout_done, 4 * l + b + 1)
                    for f in (2 * b, 2 * b + 1):
                        ins = dve.scalar_tensor_tensor(xT[:, f, :], A4[:, b, TOK * (f % 2):TOK * (f % 2) + TOK],
                                                       modc[:, l, 24 * w + 16 + f:24 * w + 17 + f], xT[:, f, :], ALU.mult, ALU.add)
                    ins.then_inc(x_upd, 1)
                    if (l, w) != (1, 1):
                        dve.wait_ge(x_upd, 4 * (2 * l + w) + b + 1)
                        square(b)

            def route(l):
                M, lg, oh, dif, t1, t2, fine, oh2 = (rt[:, q] for q in range(8))
                dve.wait_ge(logit_done, l + 1)
                L = rt[:, 8:11].rearrange("p a t e -> p (a t e)")[:, 0:72].rearrange("p (t c) -> p t c", t=2)
                tt(L, B5[:, 0:72].rearrange("p (t c) -> p t c", t=2), bge[:, l, :].unsqueeze(1).to_broadcast([P, TT, 36]), ALU.add)
                co, fi = L[:, :, 0:NG], L[:, :, NG:]
                sc = rt[:, 12]
                mx, k1, m1, m2, den, w1, w2 = (sc[:, :, q:q + 1] for q in range(7))
                g4, e4 = sc[:, :, 8:12], sc[:, :, 12:16]
                link(dve.tensor_reduce(mx[:, :, 0], co, AX, ALU.max))
                tt(e4, co, mx.to_broadcast([P, TT, NG]), ALU.subtract)
                ts(g4, e4, 0.0, None, ALU.is_equal)
                tt(g4, g4, C("desc4").unsqueeze(1).to_broadcast([P, TT, NG]), ALU.mult)
                link(dve.tensor_reduce(k1[:, :, 0], g4, AX, ALU.max))
                tt(g4, g4, k1.to_broadcast([P, TT, NG]), ALU.is_equal)
                ts(g4, g4, BIG, -BIG, ALU.mult, ALU.add)
                f4 = fine.rearrange("p t (g e) -> p t g e", g=NG)
                tt(f4, fi.rearrange("p t (g e) -> p t g e", g=NG), g4.unsqueeze(3).to_broadcast([P, TT, NG, EPG]), ALU.add)

                def first_max(v, m, out):
                    link(dve.tensor_reduce(m[:, :, 0], v, AX, ALU.max))
                    tt(out, v, m.to_broadcast([P, TT, NE]), ALU.is_equal)
                    tt(out, out, C("desc32").unsqueeze(1).to_broadcast([P, TT, NE]), ALU.mult)
                    link(dve.tensor_reduce(k1[:, :, 0], out, AX, ALU.max))
                    tt(out, out, k1.to_broadcast([P, TT, NE]), ALU.is_equal)

                first_max(fine, m1, oh)
                stt(t1, oh, -3.0 * BIG, fine, ALU.mult, ALU.add)
                first_max(t1, m2, oh2)
                tt(M, oh, oh2, ALU.add)
                tell(mask_ready)
                tt(w2, m2, m1, ALU.subtract)
                tell(route_d)
                dve.wait_ge(route_e, l + 1)
                link(dve.tensor_reduce(den[:, :, 0], e4, AX, ALU.add))
                ts(w1, w2, 1.0, None, ALU.add)
                tt(den, den, w1, ALU.mult)
                link(dve.reciprocal(w1, den))
                tt(w2, w1, w2, ALU.mult)
                tt(oh, oh, w1.to_broadcast([P, TT, NE]), ALU.mult)
                tt(oh2, oh2, w2.to_broadcast([P, TT, NE]), ALU.mult)
                tt(wt[:, :, 0:NE], oh, oh2, ALU.add)
                dve.wait_ge(rank_done, l + 1)
                R = B5[:, 0:2 * NE].rearrange("p (t e) -> p t e", t=2)
                stt(rankm[:, :, 0:NE], R, 1.0, M, ALU.add, ALU.mult)
                ts(rankm[:, :, 0:NE], rankm[:, :, 0:NE], -1.0, None, ALU.add)
                n_tok, n_more = small[:, 250:251], small[:, 251:252]
                link(dve.tensor_reduce(n_tok, B5[:, 2 * NE:3 * NE], AX, ALU.max))
                ts(n_more, n_tok, CH + 0.5, None, ALU.is_ge)
                for q in range(2, MORE + 1):
                    stt(n_more, n_tok, q * CH + 0.5, n_more, ALU.is_ge, ALU.add)
                dve.tensor_copy(cnti[:, l:l + 1], n_more).then_inc(cnt_ready, 1)

            def moe(l):
                dve.memset(hid[0:64, :, :], 0.0)
                route(l)
                dbase, sbase, ebase, mbase = l * NP5 * (2 * GE + 1), l * (2 * GE + 2), l * NE, l * TT * (2 * GE + 2)

                def matrices(sm, col, g, made):
                    io = C("iota").unsqueeze(1).to_broadcast([P, GE, CH])
                    for t in range(TT):
                        r = rankm[:, t, bass.ds(col, GE)].unsqueeze(2).to_broadcast([P, GE, CH])
                        dve.tensor_tensor(Sd[:, g, t, :].rearrange("p (e s) -> p e s", e=GE), io, r, ALU.is_equal).then_inc(sm.mat, 1)
                    dve.wait_ge(sm.mat, made + TT)
                    for t in range(TT):
                        w = wt[:, t, bass.ds(col, GE)].unsqueeze(2).to_broadcast([P, GE, CH])
                        ins = dve.tensor_tensor(Sw[:, g, t, :].rearrange("p (e s) -> p e s", e=GE),
                                                Sd[:, g, t, :].rearrange("p (e s) -> p e s", e=GE), w, ALU.mult)
                    ins.then_inc(sm.ready, 1)

                def copy_dispatched(sm, g, part, before, bank=B4):
                    dve.wait_ge(sm.disp, before + 1)
                    dst = xgT[:, g, 2 * part:2 * part + 2, :] if part < 4 else SwT[:, g, :, :]
                    dve.tensor_copy(dst, bank[:, :].rearrange("p (a b) -> p a b", a=2)).then_inc(sm.disp_ev, 1)

                def gated(sm, q, e1):
                    dve.wait_ge(sm.silu, e1 + 1)
                    dve.tensor_tensor(hid[64:128, q % 2, :], silu_a[64:128, q % 2, :], B5[64:128, :],
                                      ALU.mult).then_inc(sm.hid, 1)

                def copy_y(sm, q, e1):
                    dve.wait_ge(sm.y, e1 + 2)
                    dve.tensor_copy(y2[64 * (q % 2):64 * (q % 2) + 64, (q // 2) % 2, 0:512], B7[0:64, :]).then_inc(sm.y_lo, 1)

                matrices(main, 0, 0, mbase)
                for part in range(NP5):
                    copy_dispatched(main, 0, part, dbase + part, (B4, B5)[part % 2])
                matrices(main, GE, 1, mbase + TT)
                with dve.Fori(0, TURNS) as i:
                    for g in range(2):
                        gi = i * 2 + g
                        dve.wait_ge(main.disp, gi * NP5 + (dbase + NP5))
                        matrices(main, gi * GE + 2 * GE, g, gi * TT + (mbase + 2 * TT))
                        for j in range(GE):
                            q = GE * g + j
                            e1 = i * (2 * GE) + (ebase + q)
                            gated(main, q, e1)
                            copy_dispatched(main, 1 - g, j, gi * NP5 + (dbase + NP5 + j))
                            if j == 3:
                                copy_dispatched(main, 1 - g, 4, gi * NP5 + (dbase + NP5 + 4))
                            copy_y(main, q, e1)

                def more_experts(gb, i):
                    sm = more[l]
                    matrices(sm, i * GE, 0, gb * TT)
                    for part in range(NP5):
                        copy_dispatched(sm, 0, part, gb * NP5 + part)
                    for j in range(GE):
                        e1 = gb * GE + j
                        gated(sm, j, e1)
                        copy_y(sm, j, e1)

                def lower_ranks(c):
                    dve.tensor_scalar(rankm[:, :, :], rankm[:, :, :], float(CH), None, ALU.subtract).then_inc(ranks_down[l], 1)
                    dve.wait_ge(ranks_down[l], c + 1)
                    dve.sem_inc(more_over, 1)

                def all_combined(c):
                    dve.wait_ge(more[l].comb, (c + 1) * (NE // 2))
                    dve.sem_inc(more_over, 1)

                dve.wait_ge(main.disp, dbase + NP5 * (2 * GE + 1))
                dve.wait_ge(main.comb, (l + 1) * (NE // 2))
                more_chunks(dve, l, more_experts, before=lower_ranks, after=all_combined)
                residual(l, 1)

            dve.memset(brow[:, :], 0.0).then_inc(brow_zero, 1)
            for sm in (main, *more):
                for s in (sm.disp_ev, sm.hid, sm.y_lo):
                    tell(s)
            dve.wait_ge(in_cst, 16)
            dve.memset(rankm[:, :, NE:], -1.0)
            dve.memset(wt[:, :, NE:], 0.0)
            dve.wait_ge(c_exp, 1)
            ts(ctmp[:, 0, :], ctmp[:, 0, :], 1.0, None, ALU.add)
            link(dve.reciprocal(ctmp[:, 0, :], ctmp[:, 0, :]))
            tt(ctmp[:, 0, :], ctmp[:, 0, :], ccol[:, :], ALU.mult)
            link(dve.tensor_copy(crep[:, :, :], ctmp[:, 0, :].unsqueeze(2).to_broadcast([P, KD, 32])))
            tell(c_ready)
            dve.wait_ge(tr_ev, U["x3"] + 1)
            for b in range(4):
                square(b)
            norm_modulate(0)
            dve.wait_ge(in_par, 16 * N_PAR)
            lp = small[:, 64:192].rearrange("p (a b) -> p a b", a=2)
            tt(lp, lrow[:, 0:4:2, :], lrow[:, 1:4:2, :], ALU.mult)
            link(dve.tensor_reduce(lamt[:, 0:2], lp, AX, ALU.add))
            tell(lam_s)
            for t in range(TT):
                dve.wait_ge(z_ready, t + 1)
                iq = z0[:, t, 3072:3328].rearrange("p (h d) -> p h d", h=8)
                ik = z0[:, t, 3328:3360]
                tt(sqs[:, 0, 0:32], ik, ik, ALU.mult)
                ms = small[:, 0:1]
                link(dve.tensor_reduce(ms, sqs[:, 0, 0:32], AX, ALU.add))
                ts(ms, ms, 1.0 / 32, EPS, ALU.mult, ALU.add)
                rsqrt(ms)
                stt(ik, ik, ms, gidx[:, :], ALU.mult, ALU.mult)
                rope(iq, t, 8, 4, "ic", "is", tmp16)
                rope(ik.unsqueeze(1), t, 1, 4, "ic", "is", tmp16)
                link(dve.tensor_copy(ikrep[:, t, :].rearrange("p (r d) -> p r d", r=4), ik.unsqueeze(1).to_broadcast([P, 4, 32])))
                tell(qk_ready)
            dve.wait_ge(lam_e, 1)
            tt(lamt[:, 4:5], lamt[:, 2:3], lamt[:, 3:4], ALU.subtract)
            ts(lamt[:, 4:5], lamt[:, 4:5], 0.2, None, ALU.add)
            def q(n):
                return s5p[:, n, :]

            LRE, LIM, DT, TH, ARG, MAG, K, TURN, TC, SN, CS, ABR, ABI, DEN, CRE, CIM, T1, T2 = range(18)
            dve.wait_ge(in_s5, 16 * N_S5)
            dve.wait_ge(tr_ev, U["lam"] + 1)
            dve.wait_ge(p5_dt, 1)
            tt(q(TH), q(LIM), q(DT), ALU.mult)
            tt(q(ARG), q(LRE), q(DT), ALU.mult)
            ts(q(K), q(TH), 1.0 / TWO_PI, None, ALU.mult)
            ts(q(K), q(K), MAGIC, None, ALU.add)
            ts(q(K), q(K), -MAGIC, None, ALU.add)
            stt(q(TURN), q(K), -C1, q(TH), ALU.mult, ALU.add)
            stt(q(TURN), q(K), -C2, q(TURN), ALU.mult, ALU.add)
            ts(q(TURN), q(TURN), 1.0 / TWO_PI, None, ALU.mult)
            ts(q(TC), q(TURN), 0.25, None, ALU.add)
            for x in (TURN, TC):
                ts(q(T1), q(x), MAGIC, None, ALU.add)
                ts(q(T1), q(T1), -MAGIC, None, ALU.add)
                tt(q(x), q(x), q(T1), ALU.subtract)
            tell(p5_arg)
            dve.wait_ge(p5_sc, 1)
            tt(q(ABR), q(MAG), q(CS), ALU.mult)
            tt(q(ABI), q(MAG), q(SN), ALU.mult)
            ts(q(ABR), q(ABR), -1.0, None, ALU.add)
            tt(q(T1), q(LRE), q(LRE), ALU.mult)
            tt(q(T2), q(LIM), q(LIM), ALU.mult)
            tt(q(DEN), q(T1), q(T2), ALU.add)
            link(dve.reciprocal(q(DEN), q(DEN)))
            tt(q(T1), q(ABR), q(LRE), ALU.mult)
            tt(q(T2), q(ABI), q(LIM), ALU.mult)
            tt(q(CRE), q(T1), q(T2), ALU.add)
            tt(q(CRE), q(CRE), q(DEN), ALU.mult)
            tt(q(T1), q(ABI), q(LRE), ALU.mult)
            tt(q(T2), q(ABR), q(LIM), ALU.mult)
            tt(q(CIM), q(T1), q(T2), ALU.subtract)
            tt(q(CIM), q(CIM), q(DEN), ALU.mult)
            cre = q(CRE).unsqueeze(2).to_broadcast([P, 16, 16])
            cim = q(CIM).unsqueeze(2).to_broadcast([P, 16, 16])
            tt(Bbar[:, 0], s5b[:, 0], cre, ALU.mult)
            tt(Btmp, s5b[:, 1], cim, ALU.mult)
            tt(Bbar[:, 0], Bbar[:, 0], Btmp, ALU.subtract)
            tt(Bbar[:, 1], s5b[:, 1], cre, ALU.mult)
            tt(Btmp, s5b[:, 0], cim, ALU.mult)
            tt(Bbar[:, 1], Bbar[:, 1], Btmp, ALU.add)
            link(dve.memset(Bd, 0.0))
            for v in range(2):
                for gp in range(2):
                    link(dve.tensor_copy(Bd[64 * gp:64 * gp + 64, v, :, 16 * gp:16 * gp + 16], Bbar[64 * gp:64 * gp + 64, v]))
                for gp in range(2):
                    ts(Cd[:, v, :, 64 * gp:64 * gp + 64], s5c[:, v], C("par")[:, gp:gp + 1], (1.0, -1.0)[v], ALU.mult, ALU.mult)
            tell(p5_bt)
            def set_norm(s, zr, col):
                for t in range(TT):
                    dve.wait_ge(z_ready, zr - 1 + t)
                    norm_rope(z0[:, t, col:col + SETW].rearrange("p (h d) -> p h d", h=16), t, s, sqs, tmp16)

            set_norm(1, 6, 1536)
            for t in range(TT):
                w = P * (t + 1)
                acc = selb[:, t, 0:w]
                for u in range(2 * t, 2 * t + 2):
                    dve.wait_ge(idx_relu, u + 1)
                    for m in range(4):
                        h = 4 * (u % 2) + m
                        prev = C("cb2")[:, 2 * P - w:2 * P] if h == 0 else acc
                        stt(acc, relu_sb[u % 2][:, m, 0:w], z0[:, t, 3360 + h:3361 + h], prev, ALU.mult, ALU.add)
                    tell(idx_acc_s)
                m8 = small[:, 240:248]
                for _ in range(TOPK // 8):
                    link(dve.max(m8, acc))
                    link(dve.match_replace(acc, m8, acc, SENT))
                ts(acc, acc, SENT, -BIG, ALU.not_equal, ALU.mult)
                tt(acc, acc, C("cb2")[:, 2 * P - w:2 * P], ALU.add)
            set_norm(0, 10, 0)
            dve.wait_ge(tr_ev, U["ct1"] + 1)
            link(dve.tensor_scalar(CT[:, 1], CT[:, 0], -1.0, None, ALU.mult))
            units = L0_UNITS
            for j in range(N0 + 1):
                if j < N0:
                    softmax_unit(0, j, *units[j], sc_sb, prob)
                if j - 1 >= 8:
                    combine_unit(j - 1, *units[j - 1][1:])
                if j in (3 + LAG_PV, 7 + LAG_PV):
                    out_rows(0, (j - 3 - LAG_PV) // 4, 1, j - LAG_PV + 1, 512)
            out_rows_a(0, 12)
            out_rows_a(1, 16)
            residual(0, 0)
            norm_modulate(1)
            moe(0)
            norm_modulate(2)

            def s5_quad(q4):
                dve.wait_ge(bu_done, q4 + 1)
                cs, sn = tabs[:, 0, 4 * q4:4 * q4 + 4, :], tabs[:, 1, 4 * q4:4 * q4 + 4, :]
                bur, bui = A4[:, :, 0:TOK], A4[:, :, TOK:2 * TOK]
                if q4:
                    dve.wait_ge(y5_done, 2 * q4 - 1)
                dve.tensor_tensor(mm[:, 0], cs, bur, ALU.mult)
                tt(mm[:, 1], sn, bui, ALU.mult)
                if q4:
                    dve.wait_ge(y5_done, 2 * q4)
                tt(vv[:, 0], mm[:, 0], mm[:, 1], ALU.add)
                dve.tensor_tensor(mm[:, 0], cs, bui, ALU.mult)
                dve.tensor_tensor(mm[:, 1], sn, bur, ALU.mult).then_inc(bu_read, 1)
                dve.wait_ge(bu_read, q4 + 1)
                tt(vv[:, 1], mm[:, 0], mm[:, 1], ALU.subtract)
                for v in range(2):
                    for jj in range(4):
                        mg = s5p[:, MAG, 4 * q4 + jj:4 * q4 + jj + 1].to_broadcast([P, TOK])
                        ins = dve.tensor_tensor_scan(vv[:, v, jj, :], mg, vv[:, v, jj, :], 0.0, ALU.mult, ALU.add)
                link(ins)
                dve.tensor_tensor(mm[:, 0], cs, vv[:, 0], ALU.mult)
                dve.tensor_tensor(mm[:, 1], sn, vv[:, 1], ALU.mult).then_inc(prod_ready, 1)
                dve.wait_ge(prod_ready, 2 * q4 + 1)
                dve.tensor_tensor(vv[:, 0], sn, vv[:, 0], ALU.mult)
                dve.tensor_tensor(vv[:, 1], cs, vv[:, 1], ALU.mult).then_inc(prod_ready, 1)

            def s5_rows(q4):
                dve.wait_ge(y5_done, 2 * q4 + 2)
                ins = dve.scalar_tensor_tensor(y5[:, q4, :], uT[:, q4, :], s5d[:, q4:q4 + 1], B4[:, 0:TOK], ALU.mult, ALU.add)
                ins.then_inc(y5_read, 1)

            dve.wait_ge(tab_done, 2 * 16 // 2 + 1)
            for q4 in range(4):
                s5_quad(q4)
                if q4:
                    s5_rows(q4 - 1)

            def c_norm(t):
                dve.wait_ge(z_ready, 20 + 2 * t)
                norm_rope(z1[:, t, 0:SETW].rearrange("p (h d) -> p h d", h=16), t, 2, sqs1, tmp16_1)

            c_norm(0)
            s5_rows(3)
            dve.wait_ge(y5_read, 4)
            w0 = vv[:, 0]
            tt(w0, y5, y5, ALU.mult)
            ts(w0, w0, 0.044715, 1.0, ALU.mult, ALU.add)
            dve.tensor_tensor(w0, w0, y5, ALU.mult).then_inc(tanh_in, 1)
            c_norm(1)
            dve.wait_ge(tanh_out, 1)
            ts(w0, w0, 0.5, 0.5, ALU.mult, ALU.add)
            dve.tensor_tensor(gy, w0, y5, ALU.mult).then_inc(gy_ready, 1)
            for j, (s, b, t) in enumerate(L1_UNITS):
                softmax_unit(16, j, s, b, t, sc_sb1, prob1)
            dve.wait_ge(gy_ready, 1)
            dve.wait_ge(sig_ready, 1)
            dve.tensor_tensor(hT[:, 4:8, :], gy, vv[:, 1], ALU.mult).then_inc(yo_ready, 1)
            out_rows(16, 0, 2, 20, 0)
            out_rows(16, 1, 2, 24, 0)
            residual(1, 0)
            norm_modulate(3)
            moe(1)
            for h in range(2):
                for t in range(TT):
                    dve.wait_ge(x_tr, 2 * h + t + 1)
                    dve.tensor_copy(htok[:, t, 512 * h:512 * h + 512], (B4, B5, B6, B7)[2 * h + t][:, :]).then_inc(x_ev, 1)

        @block.scalar
        def _(act):
            count = [0]

            def link(ins):
                count[0] += 1
                ins.then_inc(s_act, 1)
                act.wait_ge(s_act, count[0])

            act.nop().then_inc(tab_done, 1)
            for sm in (main, *more):
                act.nop().then_inc(sm.y_hi, 1)
            act.dma_start(htok[:, :, :], a["x"][0].rearrange("(t p) d -> p t d", p=P)).then_inc(in_x, 16)
            act.dma_start(cst[:, :], cst_d).then_inc(in_cst, 16)
            act.dma_start(ccol[:, :], a["c"][0].rearrange("(k p) -> p k", p=P), allow_slow_non_contiguous=True).then_inc(in_c, 16)
            act.wait_ge(brow_zero, 1)
            act.dma_start(brow[0:12 * LAYERS, :], a["ada_b"].rearrange("l (q n) -> (l q) n", q=12)).then_inc(in_brow, 16)
            for dst, src, slow in S5_PARAMS:
                act.dma_start(dst, src, allow_slow_non_contiguous=slow).then_inc(in_s5, 16)
            for dst, src, slow in PARAMS:
                act.dma_start(dst, src, allow_slow_non_contiguous=slow).then_inc(in_par, 16)
            act.wait_ge(in_c, 16)
            act.activation(ctmp[:, 0, :], ccol[:, :], ACT.Exp, scale=-1.0).then_inc(c_exp, 1)
            passes = [0]

            def passed(name):
                u = passes[0]
                assert ORDER[u] == name, (ORDER[u], name)
                passes[0] += 1
                act.wait_ge(tr_done, u + 1)
                return TRB[u % 2]

            def tr_evac(name, dst, nb):
                src = passed(name)[:, 0:P * nb].rearrange("p (a b) -> p a b", a=nb)
                act.copy(dst, src).then_inc(tr_ev, 1)

            def ada_evac(l, what):
                if what[0] == "r":
                    act.copy(modrow[:, :], passed(f"ada{l}{what}")[:, :]).then_inc(tr_ev, 1)
                else:
                    r = int(what[1])
                    act.copy(modc[:, l, 16 * r:16 * r + 16].rearrange("p (g b) -> p g b", g=4),
                             passed(f"ada{l}{what}")[:, :].rearrange("p (b g x) -> p g b x", b=4, g=4)[:, :, :, 0]).then_inc(tr_ev, 1)

            def root(n, x):
                act.wait_ge(ms_ready, n)
                act.activation(x, x, ACT.Sqrt).then_inc(sq_root, 1)

            def norm_root(q):
                act.wait_ge(var_ready, q + 1)
                act.activation(rstd[:, :], rstd[:, :], ACT.Sqrt).then_inc(sd_ready, 1)

            def att_exp(base, j, s, b, t, buf, pr):
                u = base + j
                w = P * (t + 1)
                act.wait_ge(negmax, u + 1)
                if j >= 2:
                    act.wait_ge(tr_done, U[f"p{u - 2}"] + 1)
                for m in range(2):
                    ins = act.activation(pr[:, u % 2, m, 0:w], buf[:, u % 2, m, 0:w], ACT.Exp,
                                         bias=small[:, 16 + 2 * (u % 4) + m:17 + 2 * (u % 4) + m],
                                         accum_out=small[:, 32 + 2 * u + m:33 + 2 * u + m])
                ins.then_inc(expd, 1)

            def att_pt(base, j, s, b, t, pt):
                if j >= 2:
                    act.wait_ge(pv_done, base + j - 1)
                nb = n_maps(s) * (t + 1)
                tr_evac(f"p{base + j}", pt[:, (base + j) % 2, 0:nb, :], nb)

            def attention(base, units, buf, pr, pt, hook):
                n = len(units)
                for j in range(n + LAG_PT):
                    if 0 <= j - 1 < n:
                        att_exp(base, j - 1, *units[j - 1], buf, pr)
                    if 0 <= j - LAG_PT:
                        att_pt(base, j - LAG_PT, *units[j - LAG_PT], pt)
                    hook(j)

            def moe(l):
                for h in range(2):
                    for t in range(TT):
                        tr_evac(f"h{l}_{2 * h + t}", htok[:, t, 512 * h:512 * h + 512].rearrange("p (a b) -> p a b", a=4), 4)
                act.wait_ge(route_d, l + 1)
                link(act.activation(rt[:, 12, :, 12:16], rt[:, 12, :, 12:16], ACT.Exp))
                act.activation(rt[:, 12, :, 6:7], rt[:, 12, :, 6:7], ACT.Exp).then_inc(route_e, 1)
                ebase = l * NE

                def silu(sm, q, e1):
                    act.wait_ge(sm.ab, e1 + 1)
                    act.activation(silu_a[64:128, q % 2, :], B5[0:64, :], ACT.Silu).then_inc(sm.silu, 1)

                def copy_hidT(sm, q, e1):
                    act.wait_ge(sm.hidT_ps, e1 + 1)
                    act.copy(hidTb[:, q % 2, :, :], B6[:, :].rearrange("p (a b) -> p a b", a=KF)[:, :, P - CH:]).then_inc(sm.hidT, 1)

                def copy_y(sm, q, e1):
                    act.wait_ge(sm.y, e1 + 2)
                    act.copy(y2[64 * (q % 2):64 * (q % 2) + 64, (q // 2) % 2, 512:1024], B7[64:128, :]).then_inc(sm.y_hi, 1)

                if l == 0:
                    act.wait_ge(slot_used, used_after(n_of(0, "out", 0)))
                with act.Fori(0, TURNS) as i:
                    for q in range(2 * GE):
                        e1 = i * (2 * GE) + (ebase + q)
                        silu(main, q, e1)
                        copy_hidT(main, q, e1)
                        copy_y(main, q, e1)
                        if l == 0 and q % 2 == 1:
                            u, v = q // 4, q // 2 % 2
                            act.wait_ge(ph_ready, i * 4 + (2 * u + v + 1))
                            act.activation(tabs[:, v, bass.ds(i * 4 + 2 * u, 2), :], ph[:, v], ACT.Sin,
                                           scale=SIN_SCALE).then_inc(tab_done, 1)

                def more_experts(gb, i):
                    for j in range(GE):
                        e1 = gb * GE + j
                        silu(more[l], j, e1)
                        copy_hidT(more[l], j, e1)
                        copy_y(more[l], j, e1)

                act.wait_ge(main.comb, (l + 1) * (NE // 2))
                more_chunks(act, l, more_experts)

            for t in range(TT):
                for h in range(2):
                    tr_evac(f"x{2 * t + h}", xT[:, 4 * h:4 * h + 4, P * t:P * t + P], 4)
            norm_root(0)
            ada_evac(0, "r0")
            ada_evac(0, "c0")
            def z_evac(q, t):
                ch = IN0_ORDER[q]
                w = min(512, EV_IN - 512 * ch)
                act.wait_ge(proj_done, TT * q + t + 1)
                act.copy(z0[:, t, 512 * ch:512 * ch + w], OB[t][:, 0:w]).then_inc(z_ready, 1)

            def index_relu(u):
                t, half, w = u // 2, u % 2, P * (u // 2 + 1)
                act.wait_ge(idx_s, t + 1)
                if u >= 2:
                    act.wait_ge(idx_acc_s, u - 1)
                act.activation(relu_sb[u % 2][:, :, 0:w], A4[:, :, TOK * half:TOK * half + w], ACT.Relu).then_inc(idx_relu, 1)

            for q in range(7):
                for t in range(TT):
                    z_evac(q, t)
                if q == 0:
                    act.copy(s5p[:, 0:2, :], passed("lam")[:, 0:32].rearrange("p (a b) -> p a b", a=2)).then_inc(tr_ev, 1)
                    act.activation(s5p[:, 2, :], logdt[:, :], ACT.Exp).then_inc(p5_dt, 1)
                    act.wait_ge(lam_s, 1)
                    act.activation(lamt[:, 2:4], lamt[:, 0:2], ACT.Exp).then_inc(lam_e, 1)
                    root(1, small[:, 0:1])
                    root(2, small[:, 0:1])
                    act.wait_ge(p5_arg, 1)
                    act.activation(s5p[:, 5, :], s5p[:, 4, :], ACT.Exp)
                    act.activation(s5p[:, 9, :], s5p[:, 7, :], ACT.Sin, scale=SIN_SCALE)
                    act.activation(s5p[:, 10, :], s5p[:, 8, :], ACT.Sin, scale=SIN_SCALE).then_inc(p5_sc, 1)
                if q == 1:
                    ada_evac(0, "r1")
                if q == 2:
                    ada_evac(0, "c1")
                    for t in range(TT):
                        tr_evac(f"idx{t}", idxT[:, 0:3, P * t:P * t + P], 3)
                    for v in range(2):
                        tr_evac(f"bt{v}", BT[:, v], 4)
                    for v in range(2):
                        tr_evac(f"ct{v}", CT[:, 2 * v], 4)
                    root(3, small[:, 0:16])
                    root(4, small[:, 0:16])
                if q == 3:
                    index_relu(0)
                    index_relu(1)
                    ada_evac(0, "r2")
                if q == 4:
                    ada_evac(0, "c2")
                    for t in range(TT):
                        for h in range(2):
                            tr_evac(f"B{2 * t + h}", qkT0[:, 8 + 4 * h:12 + 4 * h, P * t:P * t + P], 4)
                    index_relu(2)
                    index_relu(3)
                if q >= 5:
                    root(q, small[:, 0:16])
            ada_evac(1, "r0")
            for t in range(TT):
                for h in range(2):
                    tr_evac(f"A{2 * t + h}", qkT0[:, 4 * h:4 * h + 4, P * t:P * t + P], 4)

            def ada1(j):
                for r in (1, 2):
                    if j == ADA1_ROWS[r][3]:
                        act.wait_ge(ada_done, 4 + r)
                        act.copy(modrow[:, :], OB[1][:, :]).then_inc(ada1_read, 1)
                if j in ADA1_COLS:
                    ada_evac(1, f"c{ADA1_COLS[j]}")

            attention(0, L0_UNITS, sc_sb, prob, PT, ada1)
            for t in range(TT):
                tr_evac(f"oB{t}", hT[:, 4:8, P * t:P * t + P], 4)
            root(7, small[:, 0:4])
            root(8, small[:, 0:4])
            for t in range(TT):
                tr_evac(f"oA{t}", hT[:, 0:4, P * t:P * t + P], 4)
            norm_root(1)
            moe(0)
            norm_root(2)
            for f in range(4):
                act.wait_ge(proj_done, 15 + f)
                act.copy(uT[:, f, :], B5[:, 0:TOK]).then_inc(z_ready, 1)
            for m, (ch, t) in enumerate(PROJ1):
                if m == 5:
                    root(9, small[:, 0:16])
                act.wait_ge(proj_done, 19 + m)
                act.copy(z1[:, t, 512 * ch:512 * ch + 512], B5[:, :]).then_inc(z_ready, 1)
            for t in range(TT):
                if t:
                    act.wait_ge(tanh_in, 1)
                    act.activation(vv[:, 0], vv[:, 0], ACT.Tanh, scale=GELU_C).then_inc(tanh_out, 1)
                    root(10, small[:, 0:16])
                for h in range(2):
                    tr_evac(f"C{2 * t + h}", qkT1[:, 4 * h:4 * h + 4, P * t:P * t + P], 4)
            def gate(j):
                if j == GATE_AT + 1:
                    act.wait_ge(glu_done, 1)
                    for f in range(4):
                        ins = act.activation(vv[:, 1, f, :], OB[f // 2][:, TOK * (f % 2):TOK * (f % 2) + TOK], ACT.Sigmoid, bias=glub[:, f:f + 1])
                    ins.then_inc(sig_ready, 1)

            attention(N0, L1_UNITS, sc_sb1, prob1, PT1, gate)
            for t in range(TT):
                tr_evac(f"oC{t}", hT[:, 0:4, P * t:P * t + P], 4)
            norm_root(3)
            moe(1)
            for h in range(2):
                for t in range(TT):
                    act.wait_ge(x_ev, 2 * h + t + 1)
                    act.dma_start(out_d[0, P * t:P * t + P, 512 * h:512 * h + 512], htok[:, t, 512 * h:512 * h + 512]).then_inc(out_s, 16)
            act.wait_ge(out_s, 64)

        @block.gpsimd
        def _(pool):
            count = [0]

            def link(ins):
                count[0] += 1
                ins.then_inc(s_pool, 1)
                pool.wait_ge(s_pool, count[0])

            TURN = 7
            pool.wait_ge(x_upd, 4)
            time = C("time").unsqueeze(1).to_broadcast([P, 2, TOK])
            K = 7
            with pool.Fori(0, TURNS) as i:
                for u in range(2):
                    pool.wait_ge(tab_done, i * 4 + (2 * u + 1))
                    turn = s5p[:, TURN, bass.ds(i * 4 + 2 * u, 2)].unsqueeze(2).to_broadcast([P, 2, TOK])
                    step = [0]

                    def chained(ins):
                        step[0] += 1
                        ins.then_inc(s_pool, 1)
                        pool.wait_ge(s_pool, i * (2 * K) + (K * u + step[0]))
                        pool.sem_inc(more_over, 1)

                    chained(pool.tensor_tensor(ph[:, 1], time, turn, ALU.mult))
                    chained(pool.tensor_scalar(ph[:, 0], ph[:, 1], 0.25, None, ALU.add))
                    for v in range(2):
                        chained(pool.tensor_scalar(phr, ph[:, v], MAGIC, None, ALU.add))
                        chained(pool.tensor_scalar(phr, phr, -MAGIC, None, ALU.add))
                        if v == 0:
                            chained(pool.tensor_tensor(ph[:, v], ph[:, v], phr, ALU.subtract))
                            pool.nop().then_inc(ph_ready, 1)
                        else:
                            pool.tensor_tensor(ph[:, v], ph[:, v], phr, ALU.subtract).then_inc(ph_ready, 1)
                    assert step[0] <= K


_INS = ["x", "c", "ada_w", "ada_b", "moe_wg", "moe_bg", "moe_we", "moe_be", "moe_w1", "moe_w3", "moe_w2",
        "ev_w_in", "ev_w_out", "a_qn", "a_kn", "a_lq1", "a_lk1", "a_lq2", "a_lk2", "a_subln", "b_qn", "b_kn",
        "b_idx_kn", "od_w_in", "od_w_out", "c_qn", "c_kn", "s5_lam_re", "s5_lam_im", "s5_b_re", "s5_b_im",
        "s5_c_re", "s5_c_im", "s5_d", "s5_log_dt", "s5_glu_w", "s5_glu_b"]


def constants():
    import numpy as np

    t = np.zeros((P, CONST_W), np.float32)

    def put(name, v):
        lo, hi = CONST_AT[name]
        t[:, lo:hi] = v

    i = np.arange(P)
    put("ident", np.eye(P))
    put("ones", 1.0)
    put("tri", (i[:, None] < i[None, :]) * 1.0)
    put("cb2", np.concatenate([np.zeros((P, P)), np.where(i[None, :] <= i[:, None], 0.0, -BIG)], axis=1))
    put("iota", np.arange(CH)[None, :])
    put("time", np.arange(TOK)[None, :])
    put("desc4", np.arange(NG, 0, -1)[None, :])
    put("desc32", np.arange(NE, 0, -1)[None, :])
    put("par", np.stack([(i // 16) % 2 == 0, (i // 16) % 2 == 1], axis=1) * 1.0)
    for cn, sn, rot in (("rc", "rs", 16), ("ic", "is", 8)):
        inv = np.float32(500000.0) ** (-(np.arange(0, rot, 2, dtype=np.float32) / np.float32(rot)))
        ang = np.arange(TOK, dtype=np.float32)[:, None] * inv[None, :].astype(np.float32)
        for name, f in ((cn, np.cos), (sn, np.sin)):
            v = f(ang.astype(np.float32)).astype(np.float32)
            v = np.concatenate([v, v], axis=1)
            put(name, v.reshape(TT, P, rot).transpose(1, 0, 2).reshape(P, TT * rot))
    return t


def kernel(**inputs):
    import numpy as np
    import concourse.bacc as bacc
    from concourse.bass_utils import run_bass_kernel_spmd

    nc = bacc.Bacc("TRN2", target_bir_lowering=False, num_devices=1)
    arrays, aps = {}, {}
    for name in _INS:
        arrays[f"in_{name}"] = np.ascontiguousarray(inputs[name])
        aps[name] = nc.dram_tensor(f"in_{name}", arrays[f"in_{name}"].shape, F32, kind="ExternalInput").ap()
    arrays["in_const"] = constants()
    cst_d = nc.dram_tensor("in_const", (P, CONST_W), F32, kind="ExternalInput").ap()
    out_d = nc.dram_tensor("out_x", (1, TOK, D), F32, kind="ExternalOutput").ap()
    build(nc, aps, cst_d, out_d)
    r = run_bass_kernel_spmd(nc, [arrays], core_ids=[0])
    return r.results[0]["out_x"]
```
